# Optimizing a Trainium2 kernel written in Bass

```python
import math
import jax, jax.numpy as jnp
from jax import lax
import numpy as np

D_MODEL = 1024
BATCH = 1
SEQ = 256
DEPTH = 1
DEC_BATCH = 8
DEC_SEQ = 4
PAST_LEN = 2048
PAGE_SIZE = 128

HG_HEADS = 8
HG_DK = 128
HG_DV = 128
HG_DIM = HG_HEADS * HG_DK
HG_CHUNK = 32
SSD_EXPAND = 2
SSD_INNER = SSD_EXPAND * D_MODEL
SSD_HEADDIM = 64
SSD_HEADS = SSD_INNER // SSD_HEADDIM
SSD_GROUPS = 4
SSD_HPG = SSD_HEADS // SSD_GROUPS
SSD_STATE = 128
CONV_K = 4
CONV_DIM = SSD_INNER + 2 * SSD_GROUPS * SSD_STATE
SSD_CHUNK = 64
N_EXPERTS = 32
TOP_K = 4
D_FF = D_MODEL
SWIGLU_LIMIT = 7.0
SWIGLU_ALPHA = 1.702
MOE_BLOCK = 128
ALPHA = (2.0 * DEPTH) ** 0.25
BETA = (8.0 * DEPTH) ** -0.25
LN_EPS = 1e-5
RMS_EPS = 1e-6
IN_SPLITS = (HG_DIM, HG_DIM, HG_DIM, HG_DIM, SSD_INNER, CONV_DIM, SSD_HEADS, D_MODEL, D_MODEL)
N_IN = sum(IN_SPLITS)

kernel_name = 'hgrn2_mamba2_moe_deepnorm_step'

def _split_cols(a, sizes):
    idx = np.cumsum(sizes)[:-1].tolist()
    return jnp.split(a, idx, axis=-1)

def layer_norm(x, g, b):
    xf = x.astype(jnp.float32)
    mu = jnp.mean(xf, axis=-1, keepdims=True)
    var = jnp.mean(jnp.square(xf - mu), axis=-1, keepdims=True)
    return ((xf - mu) * lax.rsqrt(var + LN_EPS) * g + b).astype(x.dtype)

def rms_norm(x, w):
    xf = x.astype(jnp.float32)
    return xf * lax.rsqrt(jnp.mean(xf * xf, axis=-1, keepdims=True) + RMS_EPS) * w

def _to_chunks(a, c):
    b, l = a.shape[:2]
    return jnp.swapaxes(a.reshape((b, l // c, c) + a.shape[2:]), 0, 1)

def _from_chunks(a):
    n, b, c = a.shape[:3]
    return jnp.swapaxes(a, 0, 1).reshape((b, n * c) + a.shape[3:])

def hgrn2_recurrence(q, k, v, log_f, s0):
    c = math.gcd(q.shape[1], HG_CHUNK)
    causal = jnp.tril(jnp.ones((c, c), bool))[None, :, :, None, None]

    def step(s, inp):
        qc, kc, vc, lf = inp
        bcum = jnp.cumsum(lf, axis=1)
        o_inter = jnp.einsum('bthk,bhkv->bthv', qc * jnp.exp(bcum), s)
        decay = jnp.exp(jnp.where(causal, bcum[:, :, None] - bcum[:, None], -jnp.inf))
        scores = jnp.einsum('bthk,btshk->bths', qc, decay * kc[:, None])
        o_intra = jnp.einsum('bths,bshv->bthv', scores, vc)
        blast = bcum[:, -1]
        s_new = jnp.exp(blast)[..., None] * s + jnp.einsum('bshk,bshv->bhkv', kc * jnp.exp(blast[:, None] - bcum), vc)
        return s_new, o_inter + o_intra

    xs = (_to_chunks(q, c), _to_chunks(k, c), _to_chunks(v, c), _to_chunks(log_f, c))
    s_fin, o = lax.scan(step, s0, xs)
    return _from_chunks(o), s_fin

def ssd_recurrence(x, dt, a, bm, cm, h0):
    c = math.gcd(x.shape[1], SSD_CHUNK)
    causal = jnp.tril(jnp.ones((c, c), bool))[None, :, :, None, None]

    def step(h, inp):
        xc, dtc, bc, cc = inp
        acum = jnp.cumsum(dtc * a, axis=1)
        seg = jnp.exp(jnp.where(causal, acum[:, :, None] - acum[:, None], -jnp.inf))
        cb = jnp.einsum('btgn,bsgn->btsg', cc, bc)
        w = cb[..., None] * seg * dtc[:, None]
        y_intra = jnp.einsum('btsgr,bsgrp->btgrp', w, xc)
        y_inter = jnp.einsum('btgn,bgrpn->btgrp', cc, h) * jnp.exp(acum)[..., None]
        alast = acum[:, -1]
        wdec = jnp.exp(alast[:, None] - acum) * dtc
        h_new = jnp.exp(alast)[..., None, None] * h + jnp.einsum('bsgr,bsgn,bsgrp->bgrpn', wdec, bc, xc)
        return h_new, y_intra + y_inter

    xs = (_to_chunks(x, c), _to_chunks(dt, c), _to_chunks(bm, c), _to_chunks(cm, c))
    h_fin, y = lax.scan(step, h0, xs)
    return _from_chunks(y), h_fin

def causal_dwconv(u, prev, w, b):
    L = u.shape[1]
    full = jnp.concatenate([prev.astype(u.dtype), u], axis=1)
    out = b + w[0] * full[:, 0:L]
    for j in range(1, CONV_K):
        out = out + w[j] * full[:, j:j + L]
    return out, full[:, -(CONV_K - 1):]

def mixer_block(x, s_hg, h_ssm, conv_prev, lb, w_in, hg_norm_w, hg_proj, conv_w, conv_b,
                dt_bias, a_log, d_skip, ssd_norm_w, ssd_proj, w_out):
    B, L, _ = x.shape
    f32 = jnp.float32
    q, fr, iv, g, z, xbc, dt, gate_a, gate_b = _split_cols(x @ w_in, IN_SPLITS)

    q = jax.nn.silu(q.astype(f32)).reshape(B, L, HG_HEADS, HG_DK)
    lbh = lb.astype(f32).reshape(HG_HEADS, HG_DK)
    log_f = jnp.logaddexp(jnp.log(lbh), jnp.log1p(-lbh) + jax.nn.log_sigmoid(fr.astype(f32).reshape(B, L, HG_HEADS, HG_DK)))
    k = -jnp.expm1(log_f)
    v = iv.astype(f32).reshape(B, L, HG_HEADS, HG_DV)
    o, s_hg_new = hgrn2_recurrence(q, k, v, log_f, s_hg.astype(f32))
    o = rms_norm(o, hg_norm_w.reshape(HG_HEADS, HG_DV)).reshape(B, L, HG_DIM) * jax.nn.sigmoid(g.astype(f32))
    out_a = o.astype(x.dtype) @ hg_proj

    xbc, conv_new = causal_dwconv(xbc, conv_prev, conv_w, conv_b)
    xbc = jax.nn.silu(xbc.astype(f32))
    xs, bm, cm = _split_cols(xbc, (SSD_INNER, SSD_GROUPS * SSD_STATE, SSD_GROUPS * SSD_STATE))
    xs = xs.reshape(B, L, SSD_GROUPS, SSD_HPG, SSD_HEADDIM)
    bm = bm.reshape(B, L, SSD_GROUPS, SSD_STATE)
    cm = cm.reshape(B, L, SSD_GROUPS, SSD_STATE)
    dt = jax.nn.softplus(dt.astype(f32) + dt_bias).reshape(B, L, SSD_GROUPS, SSD_HPG)
    a = -jnp.exp(a_log.astype(f32)).reshape(SSD_GROUPS, SSD_HPG)
    h0 = h_ssm.astype(f32).reshape(B, SSD_GROUPS, SSD_HPG, SSD_HEADDIM, SSD_STATE)
    y, h_new = ssd_recurrence(xs, dt, a, bm, cm, h0)
    y = y + d_skip.reshape(SSD_GROUPS, SSD_HPG)[..., None] * xs
    y = y.reshape(B, L, SSD_GROUPS, SSD_INNER // SSD_GROUPS) * jax.nn.silu(z.astype(f32)).reshape(B, L, SSD_GROUPS, SSD_INNER // SSD_GROUPS)
    y = rms_norm(y, ssd_norm_w.reshape(SSD_GROUPS, SSD_INNER // SSD_GROUPS)).reshape(B, L, SSD_INNER)
    out_b = y.astype(x.dtype) @ ssd_proj

    merged = jax.nn.sigmoid(gate_a) * out_a + jax.nn.sigmoid(gate_b) * out_b
    h_new = h_new.reshape(B, SSD_HEADS, SSD_HEADDIM, SSD_STATE)
    return merged @ w_out, s_hg_new.astype(s_hg.dtype), h_new.astype(h_ssm.dtype), conv_new

def moe_ffn(x, router_w, router_b, w_gu, b_gu, w_down, b_down):
    B, L, D = x.shape
    T = B * L
    S = T * TOP_K
    f32 = jnp.float32
    xt = x.reshape(T, D)
    logits = (xt @ router_w + router_b).astype(f32)
    top_v, top_e = lax.top_k(logits, TOP_K)
    gates = jax.nn.softmax(top_v, axis=-1)
    e_slot = top_e.reshape(S).astype(jnp.int32)
    tok_slot = jnp.arange(S, dtype=jnp.int32) // TOP_K
    order = jnp.argsort(e_slot)
    e_sorted = e_slot[order]
    counts = jnp.bincount(e_slot, length=N_EXPERTS).astype(jnp.int32)
    start = jnp.cumsum(counts) - counts
    padded = (counts + MOE_BLOCK - 1) // MOE_BLOCK * MOE_BLOCK
    pend = jnp.cumsum(padded)
    pstart = pend - padded
    dest_sorted = (pstart[e_sorted] + jnp.arange(S, dtype=jnp.int32) - start[e_sorted]).astype(jnp.int32)
    dest = jnp.zeros((S,), jnp.int32).at[order].set(dest_sorted)
    n_blocks = (S + N_EXPERTS * (MOE_BLOCK - 1) + MOE_BLOCK - 1) // MOE_BLOCK
    buf = jnp.zeros((n_blocks * MOE_BLOCK, D), x.dtype).at[dest].set(xt[tok_slot])
    block_e = jnp.minimum(jnp.searchsorted(pend, jnp.arange(n_blocks, dtype=jnp.int32) * MOE_BLOCK, side='right'), N_EXPERTS - 1)

    def expert(args):
        xb, e = args
        gu = (xb @ w_gu[e] + b_gu[e]).astype(f32)
        gate, up = jnp.split(gu, 2, axis=-1)
        gate = jnp.minimum(gate, SWIGLU_LIMIT)
        up = jnp.clip(up, -SWIGLU_LIMIT, SWIGLU_LIMIT)
        act = (up + 1.0) * gate * jax.nn.sigmoid(SWIGLU_ALPHA * gate)
        return act.astype(x.dtype) @ w_down[e] + b_down[e]

    out = lax.map(expert, (buf.reshape(n_blocks, MOE_BLOCK, D), block_e))
    y_slot = out.reshape(n_blocks * MOE_BLOCK, D)[dest].reshape(T, TOP_K, D)
    y = jnp.einsum('tk,tkd->td', gates.astype(x.dtype), y_slot)
    return y.reshape(B, L, D)

def trunk(x, s_hg, s_ssm, s_conv, params):
    (hg_lower_bounds, w_in, hg_norm_w, hg_proj, conv_w, conv_b, dt_bias, a_log, d_skip,
     ssd_norm_w, ssd_proj, w_out, ln1_g, ln1_b, router_w, router_b, w_gu, b_gu, w_down, b_down,
     ln2_g, ln2_b) = params
    lb_all = jnp.cumsum(jax.nn.softmax(hg_lower_bounds.astype(jnp.float32), axis=0), axis=0)
    lb_all = lb_all - lb_all[0]
    new_hg, new_ssm, new_conv = [], [], []
    for l in range(DEPTH):
        mix, sh, ss, sc = mixer_block(x, s_hg[l], s_ssm[l], s_conv[l], lb_all[l], w_in[l], hg_norm_w[l], hg_proj[l],
                                      conv_w[l], conv_b[l], dt_bias[l], a_log[l], d_skip[l], ssd_norm_w[l],
                                      ssd_proj[l], w_out[l])
        h = layer_norm(ALPHA * x + mix, ln1_g[l], ln1_b[l])
        x = layer_norm(ALPHA * h + moe_ffn(h, router_w[l], router_b[l], w_gu[l], b_gu[l], w_down[l], b_down[l]),
                       ln2_g[l], ln2_b[l])
        new_hg.append(sh)
        new_ssm.append(ss)
        new_conv.append(sc)
    return x, jnp.stack(new_hg), jnp.stack(new_ssm), jnp.stack(new_conv)

def setup_inputs(seed: int = 0) -> dict:
    key = jax.random.key(seed)
    ks = jax.random.split(key, 32)
    f32 = jnp.float32

    def nrm(i, shape, scale):
        return scale * jax.random.normal(ks[i], shape, f32)

    dt0 = jnp.exp(jax.random.uniform(ks[9], (DEPTH, SSD_HEADS), f32, math.log(1e-3), math.log(1e-1)))
    return {
        'x_prompt': nrm(0, (BATCH, SEQ, D_MODEL), 1.0),
        'x_sample': nrm(1, (DEC_BATCH, DEC_SEQ, D_MODEL), 1.0),
        'state_hgrn': nrm(2, (DEPTH, DEC_BATCH, HG_HEADS, HG_DK, HG_DV), 0.5),
        'state_ssm': nrm(3, (DEPTH, DEC_BATCH, SSD_HEADS, SSD_HEADDIM, SSD_STATE), 0.1),
        'state_conv': nrm(4, (DEPTH, DEC_BATCH, CONV_K - 1, CONV_DIM), 1.0),
        'hg_lower_bounds': nrm(5, (DEPTH, HG_DIM), 0.5),
        'w_in': nrm(6, (DEPTH, D_MODEL, N_IN), D_MODEL ** -0.5),
        'hg_norm_w': 1.0 + nrm(7, (DEPTH, HG_DIM), 0.02),
        'hg_proj': nrm(8, (DEPTH, HG_DIM, D_MODEL), BETA * HG_DIM ** -0.5),
        'conv_w': nrm(10, (DEPTH, CONV_K, CONV_DIM), CONV_K ** -0.5),
        'conv_b': nrm(11, (DEPTH, CONV_DIM), 0.01),
        'dt_bias': dt0 + jnp.log(-jnp.expm1(-dt0)),
        'a_log': jnp.log(jax.random.uniform(ks[12], (DEPTH, SSD_HEADS), f32, 1.0, 16.0)),
        'd_skip': 1.0 + nrm(13, (DEPTH, SSD_HEADS), 0.1),
        'ssd_norm_w': 1.0 + nrm(14, (DEPTH, SSD_INNER), 0.02),
        'ssd_proj': nrm(15, (DEPTH, SSD_INNER, D_MODEL), BETA * SSD_INNER ** -0.5),
        'w_out': nrm(16, (DEPTH, D_MODEL, D_MODEL), BETA * D_MODEL ** -0.5),
        'ln1_g': 1.0 + nrm(17, (DEPTH, D_MODEL), 0.02),
        'ln1_b': nrm(18, (DEPTH, D_MODEL), 0.02),
        'router_w': nrm(19, (DEPTH, D_MODEL, N_EXPERTS), D_MODEL ** -0.5),
        'router_b': nrm(20, (DEPTH, N_EXPERTS), 0.01),
        'w_gu': nrm(21, (DEPTH, N_EXPERTS, D_MODEL, 2 * D_FF), D_MODEL ** -0.5),
        'b_gu': nrm(22, (DEPTH, N_EXPERTS, 2 * D_FF), 0.02),
        'w_down': nrm(23, (DEPTH, N_EXPERTS, D_FF, D_MODEL), BETA * D_FF ** -0.5),
        'b_down': nrm(24, (DEPTH, N_EXPERTS, D_MODEL), 0.02),
        'ln2_g': 1.0 + nrm(25, (DEPTH, D_MODEL), 0.02),
        'ln2_b': nrm(26, (DEPTH, D_MODEL), 0.02),
    }

def reference(x_prompt, x_sample, state_hgrn, state_ssm, state_conv, hg_lower_bounds, w_in, hg_norm_w, hg_proj,
              conv_w, conv_b, dt_bias, a_log, d_skip, ssd_norm_w, ssd_proj, w_out, ln1_g, ln1_b, router_w,
              router_b, w_gu, b_gu, w_down, b_down, ln2_g, ln2_b):
    params = (hg_lower_bounds, w_in, hg_norm_w, hg_proj, conv_w, conv_b, dt_bias, a_log, d_skip,
              ssd_norm_w, ssd_proj, w_out, ln1_g, ln1_b, router_w, router_b, w_gu, b_gu, w_down, b_down,
              ln2_g, ln2_b)
    bp = x_prompt.shape[0]
    zero_hg = jnp.zeros((DEPTH, bp) + state_hgrn.shape[2:], state_hgrn.dtype)
    zero_ssm = jnp.zeros((DEPTH, bp) + state_ssm.shape[2:], state_ssm.dtype)
    zero_conv = jnp.zeros((DEPTH, bp) + state_conv.shape[2:], x_prompt.dtype)
    y_prompt, hg_p, ssm_p, conv_p = trunk(x_prompt, zero_hg, zero_ssm, zero_conv, params)
    y_sample, hg_s, ssm_s, conv_s = trunk(x_sample, state_hgrn, state_ssm, state_conv, params)
    return (y_prompt, y_sample, hg_p, ssm_p, conv_p, hg_s, ssm_s, conv_s)


_drawn_inputs = setup_inputs


def setup_inputs(seed=0):
    import zlib

    import numpy as np

    out = dict(_drawn_inputs(seed))
    spreads = {}
    factors = {'hg_norm_w': 8.0,
     'conv_b': 3.536,
     'ssd_norm_w': 7.013,
     'router_b': 3.629,
     'b_gu': 8.0,
     'b_down': 6.329,
     'ln2_g': 2.781,
     'ln2_b': 2.803}
    for name, (base, spread) in spreads.items():
        noise = np.random.default_rng([zlib.crc32(name.encode()), seed]).standard_normal(out[name].shape)
        drawn = base * np.exp(spread * noise) if base else spread * noise
        out[name] = __import__('jax').numpy.asarray(drawn.astype(out[name].dtype))
    for name, factor in factors.items():
        out[name] = (out[name] * factor).astype(out[name].dtype)
    return out
```

```python
from contextlib import ExitStack, contextmanager

import concourse.bass as bass
from concourse import mybir

F32 = mybir.dt.float32
I32 = mybir.dt.int32
U32 = mybir.dt.uint32
ALU = mybir.AluOpType
ACT = mybir.ActivationFunctionType
AX_X = mybir.AxisListType.X

P = 128
D = 1024
SEQ = 256
NB, NS = 8, 4
T = SEQ + NB * NS
TILES = ((0, 128), (128, 128), (256, 32))
KD = D // P
HH = 8
CH = 32
SH, SP_, SG, SN = 32, 64, 4, 128
INNER = SH * SP_
HPG = SH // SG
GW = INNER // SG
XBC = INNER + 2 * SG * SN
CT = XBC // P
XT_ = INNER // P
CK = 4
E_, TOPK = 32, 4
BLK = 64
NBLK = (T * TOPK + E_ * (BLK - 1)) // BLK
LIMIT, SALPHA = 7.0, 1.702
ALPHA = 2.0 ** 0.25
LN_EPS, RMS_EPS = 1e-5, 1e-6
C_Q, C_F, C_V, C_G, C_Z = 0, D, 2 * D, 3 * D, 4 * D
C_X = C_Z + INNER
C_DT = C_X + XBC
C_GA = C_DT + SH
C_GB = C_GA + D
CW = 512
FROW = 3 + SEQ
CROW = FROW + NB * (CK - 1 + NS)
CO = CROW - (CK - 1)
SC = 416
EXPMAX = 80.0
FMIN = 2.0 ** -62


class Steps:

    def __init__(self, sem):
        self.sem, self.n = sem, 0

    def on(self, eng):
        self.eng = eng
        return self

    def __call__(self, ins):
        ins.then_inc(self.sem, 1)
        self.n = self.n + 1
        self.eng.wait_ge(self.sem, self.n)


@contextmanager
def turns(eng, first, end, *counts):
    base = [s.n - first * per for s, per in counts]
    with eng.Fori(first, end) as i:
        for (s, per), b in zip(counts, base):
            s.n = i * per + b
        yield i
    for (s, per), b in zip(counts, base):
        s.n = b + end * per


def build(nc, x_prompt, x_sample, state_hgrn, state_ssm, state_conv, hg_lower_bounds, w_in, hg_norm_w, hg_proj,
          conv_w, conv_b, dt_bias, a_log, d_skip, ssd_norm_w, ssd_proj, w_out, ln1_g, ln1_b, router_w,
          router_b, w_gu, b_gu, w_down, b_down, ln2_g, ln2_b,
          y_prompt, y_sample, o_hg_p, o_ssm_p, o_conv_p, o_hg_s, o_ssm_s, o_conv_s, stop=99):
    ctx = ExitStack()
    base = (nc.sbuf_base + 31) // 32 * 32

    def at(name, kb, shape, dt=F32):
        return nc.alloc_sbuf_tensor_at(name, shape, dt, offset=base + int(kb * 1024))

    def S(name):
        return ctx.enter_context(nc.semaphore(name))

    def row(v):
        return v.partition_broadcast(P)

    with ctx:
        ps = ctx.enter_context(nc.psum_tensor("ps", [P, 8, 512], F32))

        ident = at("ident", 96, [P, P])
        tri = at("tri", 96.5, [P, P])
        ones = at("ones", 97, [P, P])
        smask = at("smask", 97.5, [32, 32])
        sbatch = at("sbatch", 97.625, [32, 32])
        bsel = at("bsel", 97.75, [32, NB])
        cmask = at("cmask", 97.875, [P, CH])
        keep = at("keep", 98, [P, T])
        vecs = at("vecs", 99.25, [P, 160])
        jcol = at("jcol", 100, [P, BLK])
        ecol = at("ecol", 100.25, [P, E_])
        prow = at("prow", 100.5, [P, 1])
        rb = at("rb", 101, [P, E_])
        xtok = at("xtok", 104, [P, 3, D])
        xT = at("xT", 116, [P, KD, T])
        ynT = at("ynT", 125.5, [P, XT_, T])
        onT = at("onT", 144, [P, HH, T])
        ring = [at(f"ring{i}", 16 * i, [P, KD, CW]) for i in range(2)]
        z = at("z", 154, [P, 3, INNER])
        convBC = at("convBC", 178, [P, CT - XT_, T])
        convX = at("convX", 188, [P, XT_, T])
        wconv = vecs[:, 0:CK * CT].rearrange("p (j c) -> p j c", c=CT)
        bconv = vecs[:, CK * CT:CK * CT + CT]
        hgw = vecs[:, 120:128]
        ssdw = vecs[:, 128:144]
        lbv = vecs[:, 144:152]
        w_k = w_in[0].rearrange("(k p) n -> p k n", p=P)

        def chunk_src(c):
            return w_k[:, :, bass.ds(c, CW)]

        xrow = at("xrow", 32, [P, CT, CROW])
        prev = at("prev", 62, [NB * 3, XBC])
        ncol = at("ncol", 74, [P, CT, 27])
        nrows = at("nrows", 80, [27, XBC])
        acc = [at(f"acc{i}", 92 + 1.25 * i, [P, CROW]) for i in range(2)]
        vrows = [at("vrows0", 94.5, [P, P]), at("vrows1", 95, [24, P])]
        wdt = at("wdt", 103, [P, KD, SH])
        dtb = at("dtb", 102, [P, SH])
        dt = at("dt", 101.25, [P, 3, SH])

        s_in = S("x_loaded")
        s_vec = S("vectors_loaded")
        s_prev = S("conv_state_loaded")
        s_wdt = S("dt_weights_loaded")
        s_w = [S(f"chunk_loaded{i}") for i in range(2)]
        s_const = S("constants_ready")
        s_zero = S("xrow_cleared")
        s_xtp = S("xT_transposed")
        s_xte = S("xT_copied")
        s_vt = S("vectors_transposed")
        s_ve = S("vectors_copied")
        s_pt = S("conv_state_transposed")
        s_pe_ = S("conv_state_copied")
        s_mt = S("projection_ready")
        s_me = S("projection_copied")
        s_conv = S("conv_ready")
        s_silu = S("conv_activated")
        s_dtp = S("dt_ready")
        s_dte = S("dt_copied")
        s_nc = S("conv_tail_gathered")
        s_nct = S("conv_tail_transposed")
        s_nce = S("conv_tail_copied")
        s_out = S("outputs_stored")
        dstep, astep, pstep = Steps(S("dve_step")), Steps(S("act_step")), Steps(S("pool_step"))
        stored = 0

        with nc.Block() as block:
            @block.sync
            def _(sp):
                for t in range(2):
                    sp.dma_start(xtok[:, t, :], x_prompt[0, P * t:P * t + P, :]).then_inc(s_in, 16)
                sp.dma_start(xtok[0:32, 2, :], x_sample.rearrange("b s d -> (b s) d")).then_inc(s_in, 16)
                sp.dma_start(ring[0][:], chunk_src(C_X)).then_inc(s_w[0], 16)
                sp.dma_start(ring[1][:], chunk_src(C_X + CW)).then_inc(s_w[1], 16)
                with sp.Fori(1, 3) as i:
                    for n in range(2):
                        sp.wait_ge(s_mt, i * 8 + (4 * n - 4))
                        sp.dma_start(ring[n][:], chunk_src(i * (2 * CW) + (C_X + n * CW))).then_inc(s_w[n], 16)
                for c in range(INNER // CW):
                    sp.wait_ge(s_mt, CT - 4 + 4 * c if c < 2 else CT + 3 * (c - 1))
                    sp.dma_start(ring[c % 2][:], chunk_src(C_Z + c * CW)).then_inc(s_w[c % 2], 16)
                sp.wait_ge(s_nce, 2)
                sp.dma_start(o_conv_p[0, 0], nrows[0:3, :]).then_inc(s_out, 16)
                sp.dma_start(o_conv_s[0].rearrange("b r c -> (b r) c"), nrows[3:27, :]).then_inc(s_out, 16)
                sp.wait_ge(s_out, 32)

            @block.gpsimd
            def _(pool):
                g = nc.gpsimd
                pstep.on(pool)
                g.memset(xrow[:, :, 0:3], 0.0).then_inc(s_zero, 1)
                g.memset(dt[:], 0.0).then_inc(s_zero, 1)
                pstep(g.memset(ones[:], 1.0))
                pstep(g.memset(ident[:], 0.0))
                pstep(g.memset(keep[:], 1.0))
                pstep(g.memset(sbatch[:], 1.0))
                pstep(g.iota(jcol[:], [[1, BLK]], base=0, channel_multiplier=0, allow_small_or_imprecise_dtypes=True))
                pstep(g.iota(ecol[:], [[1, E_]], base=0, channel_multiplier=0, allow_small_or_imprecise_dtypes=True))
                pstep(g.iota(prow[:], [[1, 1]], base=0, channel_multiplier=1, allow_small_or_imprecise_dtypes=True))
                pstep(g.affine_select(out=ident[:], in_=ident[:], compare_op=ALU.not_equal, fill=1.0, base=0,
                                pattern=[[-1, P]], channel_multiplier=1))
                pstep(g.affine_select(out=tri[:], in_=ones[:], compare_op=ALU.is_ge, fill=0.0, base=0,
                                pattern=[[1, P]], channel_multiplier=-1))
                for r in range(4):
                    pstep(g.affine_select(out=cmask[32 * r:32 * r + 32, :], in_=ones[32 * r:32 * r + 32, 0:CH],
                                    compare_op=ALU.is_ge, fill=0.0, base=0, pattern=[[1, CH]],
                                    channel_multiplier=-1))
                pstep(g.memset(keep[:, 0:SEQ].rearrange("p (c s) -> p c s", s=CH)[:, :, 0:1], 0.0))
                pstep(g.memset(keep[:, SEQ:T].rearrange("p (c s) -> p c s", s=NS)[:, :, 0:1], 0.0))
                sb3 = sbatch[:].rearrange("p (b s) -> p b s", s=NS)
                pstep(g.affine_select(out=sb3, in_=sb3, compare_op=ALU.is_ge, fill=0.0, base=0,
                                      pattern=[[-NS, NB], [0, NS]], channel_multiplier=1))
                pstep(g.affine_select(out=sb3, in_=sb3, compare_op=ALU.is_ge, fill=0.0, base=NS - 1,
                                      pattern=[[NS, NB], [0, NS]], channel_multiplier=-1))
                pstep(g.tensor_copy(bsel[:], sb3[:, :, 0]))
                g.tensor_tensor(smask[:], sbatch[:], tri[0:32, 0:32], ALU.mult).then_inc(s_const, 1)

            @block.scalar
            def _(act):
                a = nc.scalar
                vr = vrows[0]
                act.dma_start(vr[0:96, :], conv_w[0].rearrange("j (c p) -> (j c) p", p=P)).then_inc(s_vec, 16)
                act.dma_start(vr[96:120, :], conv_b[0].rearrange("(c p) -> c p", p=P)).then_inc(s_vec, 16)
                act.dma_start(vr[120:128, :], hg_norm_w[0].rearrange("(c p) -> c p", p=P)).then_inc(s_vec, 16)
                act.dma_start(vrows[1][0:16, :], ssd_norm_w[0].rearrange("(c p) -> c p", p=P)).then_inc(s_vec, 16)
                act.dma_start(vrows[1][16:24, :], hg_lower_bounds[0].rearrange("(c p) -> c p", p=P)).then_inc(s_vec, 16)
                act.dma_start(prev[:], state_conv[0].rearrange("b r c -> (b r) c")).then_inc(s_prev, 16)
                act.dma_start(wdt[:], w_k[:, :, C_DT:C_DT + SH]).then_inc(s_wdt, 16)
                act.dma_start(dtb[:], row(dt_bias[0])).then_inc(s_wdt, 16)
                for k in range(KD):
                    act.wait_ge(s_xtp, k + 1)
                    a.copy(xT[:, k, :], ps[:, k % 2, 0:T]).then_inc(s_xte, 1)
                with act.Fori(0, CT // 4) as i:
                    for m in range(4):
                        act.wait_ge(s_mt, i * 4 + (m + 1))
                        a.copy(xrow[:, bass.ds(i * 4 + m, 1), 3:3 + SEQ], ps[:, 4 + m:5 + m, 0:SEQ])
                        a.copy(xrow[:, bass.ds(i * 4 + m, 1), FROW:CROW].rearrange("p c (b s) -> p (c b) s", s=7)[:, :, 3:7],
                               ps[:, 4 + m, SEQ:T].rearrange("p (b s) -> p b s", s=NS)).then_inc(s_me, 1)
                zc = INNER // CW
                for j in range(3 * zc):
                    n, (t, (_, rows)) = j // 3, (j % 3, TILES[j % 3])
                    act.wait_ge(s_mt, CT + j + 1)
                    a.activation(z[0:rows, t, n * CW:(n + 1) * CW], ps[0:rows, 4 + j % 4, :], ACT.Silu).then_inc(s_me, 1)
                    for c in (2 * j, 2 * j + 1):
                        act.wait_ge(s_conv, c + 1)
                        out = convX[:, c, :] if c < XT_ else convBC[:, c - XT_, :]
                        a.activation(out[:, 0:SEQ], acc[c % 2][:, 0:SEQ], ACT.Silu)
                        a.activation(out[:, SEQ:T].rearrange("p (b s) -> p b s", s=NS),
                                     acc[c % 2][:, FROW:CROW].rearrange("p (b s) -> p b s", s=7)[:, :, 0:NS],
                                     ACT.Silu).then_inc(s_silu, 1)

            @block.vector
            def _(dve):
                v = nc.vector
                dstep.on(dve)
                dve.wait_ge(s_vt, 1)
                v.tensor_copy(vecs[:, 0:152], ps[:, 2, 0:152]).then_inc(s_ve, 1)
                dve.wait_ge(s_zero, 1)
                for h in range(2):
                    dve.wait_ge(s_pt, h + 1)
                    v.tensor_copy(xrow[:, 12 * h:12 * h + 12, FROW:CROW].rearrange("p c (b s) -> p c b s", s=7)[:, :, :, 0:3],
                                  ps[:, h, 0:288].rearrange("p (c b s) -> p c b s", b=NB, s=3)).then_inc(s_pe_, 1)
                dve.wait_ge(s_ve, 1)
                dve.wait_ge(s_pe_, 2)
                def convolve(i, n):
                    dve.wait_ge(s_me, i * 2 + (n + 1))
                    if not isinstance(i, int) or i > 0:
                        dve.wait_ge(s_silu, i * 2 + (n - 1))
                    c = bass.ds(i * 2 + n, 1)
                    o = acc[n][:, 0:CO]
                    tap = [xrow[:, c, j:j + CO].rearrange("p c l -> p (c l)") for j in range(CK)]
                    w = [wconv[:, j, c] for j in range(CK)]
                    dstep(v.tensor_scalar(o, tap[0], w[0], bconv[:, c], ALU.mult, ALU.add))
                    dstep(v.scalar_tensor_tensor(o, tap[1], w[1], o, ALU.mult, ALU.add))
                    dstep(v.scalar_tensor_tensor(o, tap[2], w[2], o, ALU.mult, ALU.add))
                    v.scalar_tensor_tensor(o, tap[3], w[3], o, ALU.mult, ALU.add).then_inc(s_conv, 1)

                convolve(0, 0)
                convolve(0, 1)
                with turns(dve, 1, CT // 2, (dstep, 6)) as i:
                    convolve(i, 0)
                    convolve(i, 1)
                v.tensor_copy(ncol[:, :, 0:3], xrow[:, :, SEQ:FROW]).then_inc(s_nc, 1)
                v.tensor_copy(ncol[:, :, 3:27].rearrange("p c (b s) -> p c b s", s=3),
                              xrow[:, :, FROW:CROW].rearrange("p c (b s) -> p c b s", s=7)[:, :, :, 4:7]).then_inc(s_nc, 1)
                dve.wait_ge(s_dtp, 1)
                dve.wait_ge(s_wdt, 32)
                dve.wait_ge(s_zero, 2)
                for t, (_, rows) in enumerate(TILES):
                    v.tensor_tensor(dt[0:rows, t, :], ps[0:rows, 3, 32 * t:32 * t + 32], dtb[0:rows, :], ALU.add).then_inc(s_dte, 1)
                for h in range(2):
                    dve.wait_ge(s_nct, h + 1)
                    v.tensor_copy(nrows[:, 1536 * h:1536 * h + 1536].rearrange("p (c n) -> p c n", n=512),
                                  ps[0:27, 0:3, :]).then_inc(s_nce, 1)

            @block.tensor
            def _(pe):
                m = nc.tensor
                pe.wait_ge(s_const, 1)
                pe.wait_ge(s_in, 48)
                for k in range(KD):
                    if k >= 2:
                        pe.wait_ge(s_xte, k - 1)
                    for t, (t0, rows) in enumerate(TILES):
                        last = m.transpose(ps[:, k % 2, t0:t0 + rows], xtok[0:rows, t, k * P:(k + 1) * P], ident[0:rows, 0:rows])
                    last.then_inc(s_xtp, 1)
                pe.wait_ge(s_vec, 80)
                m.transpose(ps[:, 2, 0:P], vrows[0][:], ident[:])
                m.transpose(ps[:, 2, P:P + 24], vrows[1][:], ident[0:24, 0:24]).then_inc(s_vt, 1)
                pe.wait_ge(s_prev, 16)
                pe.wait_ge(s_xte, KD)
                for h in range(2):
                    for c in range(12):
                        last = m.transpose(ps[:, h, 24 * c:24 * c + 24], prev[:, (12 * h + c) * P:(12 * h + c + 1) * P], ident[0:24, 0:24])
                    last.then_inc(s_pt, 1)
                pe.wait_ge(s_wdt, 32)
                for t, (t0, rows) in enumerate(TILES):
                    for k in range(KD):
                        last = m.matmul(ps[0:rows, 3, 32 * t:32 * t + 32], xT[:, k, t0:t0 + rows], wdt[:, k, :],
                                        start=(k == 0), stop=(k == KD - 1))
                last.then_inc(s_dtp, 1)

                def columns(i, n):
                    pe.wait_ge(s_w[n], i * 16 + 16)
                    for mt in range(4):
                        if not (isinstance(i, int) and i == 0) or n > 0:
                            pe.wait_ge(s_me, i * 8 + (4 * n + mt - 3))
                        for k in range(KD):
                            last = m.matmul(ps[:, 4 + mt, 0:T], ring[n][:, k, mt * P:(mt + 1) * P], xT[:, k, :],
                                            start=(k == 0), stop=(k == KD - 1))
                        last.then_inc(s_mt, 1)

                columns(0, 0)
                columns(0, 1)
                with pe.Fori(1, CT // 8) as i:
                    columns(i, 0)
                    columns(i, 1)
                for c in range(INNER // CW):
                    n = c % 2
                    pe.wait_ge(s_w[n], 16 * (3 + c // 2 + 1))
                    for t, (t0, rows) in enumerate(TILES):
                        j = 3 * c + t
                        pe.wait_ge(s_me, CT + j - 3)
                        for k in range(KD):
                            last = m.matmul(ps[0:rows, 4 + j % 4, :], xT[:, k, t0:t0 + rows], ring[n][:, k, :],
                                            start=(k == 0), stop=(k == KD - 1))
                        last.then_inc(s_mt, 1)
                pe.wait_ge(s_nc, 2)
                for h in range(2):
                    if h == 1:
                        pe.wait_ge(s_nce, 1)
                    for c in range(12):
                        last = m.transpose(ps[0:27, c // 4, (c % 4) * P:(c % 4 + 1) * P], ncol[:, 12 * h + c, :], ident[:])
                    last.then_inc(s_nct, 1)

        if stop <= 1:
            return
        xtk = at("xtk", 0, [P, 3, INNER])
        xdt = at("xdt", 24, [P, 3, INNER])
        cbm = at("cbm", 48, [P, SG, SC])
        dbuf = [at(f"dbuf{i}", 55 + 1.75 * i, [P, SC]) for i in range(2)]
        wbuf = [at(f"wbuf{i}", 58.5 + 1.75 * i, [P, SC]) for i in range(2)]
        btok = at("btok", 62, [P, 3, SG * SN])
        xw2 = at("xw2", 68, [32, INNER])
        hst = [at(f"hst{i}", 76 + 8 * i, [P, XT_, SN]) for i in range(2)]
        dsk = at("dsk", 92, [P, SH])
        alog = at("alog", 92.125, [P, SH])
        av = at("av", 92.25, [P, 3, SH])
        wd = at("wd", 92.625, [P, 3, SH])
        dtv = at("dtv", 93, [P, 3, SH])
        dta = at("dta", 93.375, [P, 3, SH])
        dtmp = at("dtmp", 93.75, [P, 3, SH])
        dabs = at("dabs", 94.125, [P, 3, SH])
        eA = at("eA", 94.5, [32, SH])
        dec = at("dec", 94.625, [P, XT_ * NB])
        ss = at("ss", 95.125, [P, 3 * SG])
        ats = at("ats", 101.75, [32, T])
        ath = [at(f"ath{i}", 138 + 1.25 * i, [32, T]) for i in range(2)]
        hT = at("hT", 144, [P, XT_, P])
        yis = at("yis", 152, [P, 512])
        bm = [at(f"bm{i}", 125.5 + 2 * i, [32, SG * SN]) for i in range(2)]
        hp = at("hp", 130, [P, XT_, SN])
        sq = at("sq", 141, [P, GW])
        xw = at("xw", 188, [P, 2, INNER])

        q_h = [S(f"state_loaded{i}") for i in range(2)]
        q_par = S("ssd_parameters_loaded")
        q_xp = S("x_transposed")
        q_xa = S("x_copied_act")
        q_xv = S("x_copied_dve")
        q_dt = S("softplus_parts")
        q_dta = S("dta_ready")
        q_dx = S("dta_widened")
        q_A = S("A_ready")
        q_ac = S("A_copied")
        q_dif = S("decay_exponents_ready")
        q_exp = S("decays_ready")
        q_wd = S("state_weights_ready")
        q_xdt = S("xdt_ready")

        with nc.Block() as block:
            @block.sync
            def _(sp):
                sp.dma_start(dsk[:], row(d_skip[0])).then_inc(q_par, 16)
                sp.dma_start(alog[:], row(a_log[0])).then_inc(q_par, 16)
                for n in range(2):
                    sp.dma_start(hst[n][:], state_ssm[0, n].rearrange("h p n -> (h p) n").rearrange("(i q) n -> q i n", q=P)).then_inc(q_h[n], 16)

            @block.gpsimd
            def _(pool):
                g = nc.gpsimd
                pstep.on(pool)
                pstep(g.memset(xdt[:, 2, :], 0.0))
                pool.wait_ge(q_dta, 1)
                g.tensor_copy(xw2[:].rearrange("p (h d) -> p h d", d=SP_),
                              dta[0:32, 2, :].unsqueeze(2).broadcast_to([32, SH, SP_])).then_inc(q_dx, 1)
                for t, (_, rows) in enumerate(TILES):
                    pool.wait_ge(q_xa, 2 * t + 2)
                    pool.wait_ge(q_xv, 2 * t + 2)
                    g.tensor_tensor(xdt[0:rows, t, :].rearrange("p (h d) -> p h d", d=SP_),
                                    xtk[0:rows, t, :].rearrange("p (h d) -> p h d", d=SP_),
                                    dtv[0:rows, t, :].unsqueeze(2).broadcast_to([rows, SH, SP_]), ALU.mult).then_inc(q_xdt, 1)

            def copy_x(eng_copy, j):
                t = j // 4 if j < 12 else j - 12
                rows = TILES[t][1]
                dst = xtk[0:rows, t, (j % 4) * 512:(j % 4 + 1) * 512] if j < 12 else btok[0:rows, t, :]
                return eng_copy(dst, ps[0:rows, j % 4, :])

            @block.scalar
            def _(act):
                a = nc.scalar
                astep.on(act)
                act.wait_ge(q_par, 32)
                a.activation(alog[:], alog[:], ACT.Exp).then_inc(q_dt, 1)
                astep(a.activation(dabs[:], dt[:], ACT.Abs))
                astep(a.activation(dabs[:], dabs[:], ACT.Exp, scale=-1.0))
                a.activation(dabs[:], dabs[:], ACT.Ln, bias=1.0).then_inc(q_dt, 1)
                for j in range(0, 15, 2):
                    act.wait_ge(q_xp, j + 1)
                    copy_x(a.copy, j).then_inc(q_xa, 1)
                act.wait_ge(q_A, 1)
                act.wait_ge(q_ac, 3)
                a.activation(eA[:], av[0:32, 2, :], ACT.Exp)
                a.activation(dec[:], ps[:, 6, 0:XT_ * NB], ACT.Exp)
                a.copy(ats[:], ps[0:32, 5, 0:T])
                act.wait_ge(q_dif, 1)
                a.activation(dtmp[:], dtmp[:], ACT.Exp).then_inc(q_exp, 1)

            @block.vector
            def _(dve):
                v = nc.vector
                dstep.on(dve)
                dstep(v.tensor_scalar(dtv[:], dt[:], 0.0, None, ALU.max))
                dve.wait_ge(q_dt, 2)
                dstep(v.tensor_tensor(dtv[:], dtv[:], dabs[:], ALU.add))
                v.scalar_tensor_tensor(dta[:], dtv[:], -1.0, alog[:].unsqueeze(1).broadcast_to([P, 3, SH]),
                                       ALU.mult, ALU.mult).then_inc(q_dta, 1)
                v.memset(dtmp[:], 0.0)
                v.memset(av[:], 0.0)
                dstep(v.memset(cbm[:, :, 384:SC], 0.0))
                for j in range(1, 15, 2):
                    dve.wait_ge(q_xp, j + 1)
                    copy_x(v.tensor_copy, j).then_inc(q_xv, 1)
                dve.wait_ge(q_A, 1)
                for t, (_, rows) in enumerate(TILES):
                    v.tensor_copy(av[0:rows, t, :], ps[0:rows, 4, 32 * t:32 * t + 32]).then_inc(q_ac, 1)
                dve.wait_ge(q_ac, 3)
                for t, (_, rows) in enumerate(TILES):
                    last = v.tensor_tensor(dtmp[0:rows, t, :], ps[0:rows, 4, 96 + 32 * t:128 + 32 * t], av[0:rows, t, :], ALU.subtract)
                last.then_inc(q_dif, 1)
                dve.wait_ge(q_exp, 1)
                v.tensor_tensor(wd[:], dtmp[:], dtv[:], ALU.mult).then_inc(q_wd, 1)

            @block.tensor
            def _(pe):
                m = nc.tensor
                for j in range(15):
                    t = j // 4 if j < 12 else j - 12
                    t0, rows = TILES[t]
                    if j >= 4:
                        pe.wait_ge(q_xa if j % 2 == 0 else q_xv, (j - 4) // 2 + 1)
                    for c in range(4):
                        src = convX[:, 4 * (j % 4) + c, t0:t0 + rows] if j < 12 else convBC[:, c, t0:t0 + rows]
                        last = m.transpose(ps[0:rows, j % 4, c * P:(c + 1) * P], src, ident[:])
                    last.then_inc(q_xp, 1)
                pe.wait_ge(q_dta, 1)
                d0, d1, d2 = dta[:, 0, :], dta[:, 1, :], dta[0:32, 2, :]
                for o, l, r in ((0, tri, smask), (96, ones, sbatch)):
                    if o == 0:
                        m.matmul(ps[:, 4, 0:32], l[:], d0, start=True, stop=True)
                    else:
                        m.matmul(ps[:, 4, 96:128], ones[:], d0, start=True, stop=False)
                        m.matmul(ps[:, 4, 96:128], ones[:], d1, start=False, stop=True)
                    m.matmul(ps[:, 4, o + 32:o + 64], ones[:], d0, start=True, stop=False)
                    m.matmul(ps[:, 4, o + 32:o + 64], l[:], d1, start=False, stop=True)
                    m.matmul(ps[0:32, 4, o + 64:o + 96], r[:], d2, start=True, stop=True)
                m.matmul(ps[0:32, 5, 0:P], d0, tri[:], start=True, stop=True)
                m.matmul(ps[0:32, 5, P:2 * P], d0, ones[:], start=True, stop=False)
                m.matmul(ps[0:32, 5, P:2 * P], d1, tri[:], start=False, stop=True)
                m.matmul(ps[0:32, 5, 2 * P:T], d2, smask[:], start=True, stop=True)
                pe.wait_ge(q_dx, 1)
                for i in range(XT_):
                    last = m.matmul(ps[:, 6, NB * i:NB * i + NB], xw2[:, P * i:P * i + P], bsel[:], start=True, stop=True)
                last.then_inc(q_A, 1)

        if stop <= 2:
            return
        r_bm = S("masked_B_ready")
        r_tr = S("state_transposed")
        r_tc = S("state_copied")
        r_in = S("state_read_out")
        r_up = S("state_update_ready")
        r_ud = S("state_updated")
        r_dc = S("state_decayed")
        r_st = [S(f"state_stored{i}") for i in range(2)]
        r_yi = S("inter_ready")
        r_yc = S("inter_copied")
        r_yt = S("inter_transposed")
        r_ya = S("inter_added")
        r_w = S("weighted_x_ready")
        r_sk = S("skip_ready")
        r_cb = S("scores_ready")
        r_cm = S("scores_masked")
        r_hp = S("final_state_ready")
        r_hc = S("final_state_copied")
        r_sel = S("head_A_ready")
        r_ab = S("head_A_spread")
        r_d = S("head_exponents_ready")
        r_e = S("head_decays_ready")
        r_W = S("head_weights_ready")
        r_y = S("group_y_ready")
        r_z = S("group_y_gated")
        r_yh = S("head_y_done")

        with nc.Block() as block:
            @block.sync
            def _(sp):
                def rows_of(state, b):
                    return state[0, b].rearrange("h p n -> (h p) n").rearrange("(i q) n -> q i n", q=P)

                for b in range(NB):
                    sp.wait_ge(r_ud, 4 * b + 4)
                    sp.dma_start(rows_of(o_ssm_s, b), hst[b % 2][:]).then_inc(r_st[b % 2], 16)
                    if b + 2 < NB:
                        sp.wait_ge(r_st[b % 2], 16 * (b // 2 + 1))
                        sp.dma_start(hst[b % 2][:], rows_of(state_ssm, b + 2)).then_inc(q_h[b % 2], 16)
                sp.wait_ge(r_hc, 4)
                sp.dma_start(o_ssm_p[0, 0].rearrange("h p n -> (h p) n").rearrange("(i q) n -> q i n", q=P), hp[:]).then_inc(s_out, 16)
                sp.wait_ge(s_out, 32 + 16)
                for n in range(2):
                    sp.wait_ge(r_st[n], 16 * (NB // 2))

            @block.gpsimd
            def _(pool):
                g = nc.gpsimd
                g.tensor_tensor(xw2[:].rearrange("p (h d) -> p h d", d=SP_), xtk[0:32, 2, :].rearrange("p (h d) -> p h d", d=SP_),
                                wd[0:32, 2, :].unsqueeze(2).broadcast_to([32, SH, SP_]), ALU.mult).then_inc(r_w, 1)
                with pool.Fori(0, NB // 2) as i:
                    for n in range(2):
                        pool.wait_ge(r_tr, i * 8 + (4 * n + 4))
                        g.tensor_tensor(hst[n][:], hst[n][:], dec[:].rearrange("p (i b) -> p i b", b=NB)[:, :, bass.ds(i * 2 + n, 1)]
                                        .broadcast_to([P, XT_, SN]), ALU.mult).then_inc(r_dc, 1)
                for t in range(2):
                    g.tensor_tensor(xw[:, t, :].rearrange("p (h d) -> p h d", d=SP_), xtk[:, t, :].rearrange("p (h d) -> p h d", d=SP_),
                                    wd[:, t, :].unsqueeze(2).broadcast_to([P, SH, SP_]), ALU.mult).then_inc(r_w, 1)
                pool.wait_ge(r_w, 3)
                for t, (_, rows) in enumerate(TILES):
                    xv = xtk[0:rows, t, :].rearrange("p (h d) -> p h d", d=SP_)
                    g.tensor_tensor(xv, xv, dsk[0:rows, :].unsqueeze(2).broadcast_to([rows, SH, SP_]), ALU.mult).then_inc(r_sk, 1)

            @block.scalar
            def _(act):
                a = nc.scalar
                astep.on(act)
                with act.Fori(0, NB) as i:
                    for q in range(4):
                        act.wait_ge(r_tr, i * 4 + (q + 1))
                        if q == 0:
                            act.wait_ge(r_in, i)
                        a.copy(hT[:, 4 * q:4 * q + 4, :], ps[:, q % 2, :]).then_inc(r_tc, 1)
                act.wait_ge(r_in, NB)
                a.copy(yis[:], ps[:, 4, :]).then_inc(r_yc, 1)
                for q in range(4):
                    act.wait_ge(r_hp, q + 1)
                    a.copy(hp[:, 4 * q:4 * q + 4, :], ps[:, 5 + q % 2, :]).then_inc(r_hc, 1)

                with turns(act, 0, SG) as i:
                    for n in range(HPG + 1):
                        if n < HPG:
                            act.wait_ge(r_ab, i * HPG + max(n - 1, 0))
                            a.activation(ath[n % 2][:], ats[:], ACT.Identity, scale=ident[0:32, bass.ds(i * HPG + n, 1)]).then_inc(r_sel, 1)
                        if n > 0:
                            act.wait_ge(r_d, i * HPG + n)
                            act.wait_ge(r_yh, i * HPG + max(n - 2, 0))
                            a.activation(wbuf[(n - 1) % 2][:], dbuf[(n - 1) % 2][:], ACT.Exp).then_inc(r_e, 1)
                for g in range(SG):
                    for t, (_, rows) in enumerate(TILES):
                        act.wait_ge(r_z, 3 * g + t + 1)
                        astep(a.activation(sq[0:rows, :], z[0:rows, t, GW * g:GW * g + GW], ACT.Square,
                                           accum_out=ss[0:rows, SG * t + g:SG * t + g + 1]))

            @block.vector
            def _(dve):
                v = nc.vector
                dstep.on(dve)
                v.memset(ss[:], 1.0)
                dstep(v.memset(dbuf[0][:], 0.0))
                dstep(v.memset(dbuf[1][:], 0.0))
                with turns(dve, 0, NB // 2) as i:
                    for n in range(2):
                        dve.wait_ge(r_up, i * 8 + (4 * n if n == 0 else 0))
                        v.tensor_scalar(bm[n][:], btok[0:32, 2, :], bsel[:, bass.ds(i * 2 + n, 1)], None, ALU.mult).then_inc(r_bm, 1)
                    for n in range(2):
                        dve.wait_ge(r_dc, i * 2 + (n + 1))
                        for q in range(4):
                            dve.wait_ge(r_up, i * 8 + (4 * n + q + 1))
                            hq = hst[n][:, 4 * q:4 * q + 4, :].rearrange("p i n -> p (i n)")
                            v.tensor_tensor(hq, hq, ps[:, 2 + q % 2, :], ALU.add).then_inc(r_ud, 1)
                for g in range(SG):
                    dve.wait_ge(r_cb, g + 1)
                    b = ps[:, 6 + g % 2, :]
                    v.tensor_tensor(cbm[:, g, 0:P], b[:, 0:P], tri[:], ALU.mult)
                    v.tensor_copy(cbm[:, g, P:2 * P], b[:, P:2 * P])
                    v.tensor_tensor(cbm[:, g, 2 * P:3 * P], b[:, 2 * P:3 * P], tri[:], ALU.mult)
                    v.tensor_tensor(cbm[0:32, g, 3 * P:SC], b[0:32, 3 * P:SC], smask[:], ALU.mult).then_inc(r_cm, 1)
                dve.wait_ge(r_cm, SG)
                dve.wait_ge(r_sk, 3)
                for q in range(4):
                    dve.wait_ge(r_yt, q + 1)
                    if q > 0:
                        dve.wait_ge(r_ya, q)
                    dstep(v.tensor_tensor(sq[0:32, :].rearrange("p (h d) -> p h d", d=SP_), ps[0:32, q, :].rearrange("p (h d) -> p h d", d=SP_),
                                          eA[:, HPG * q:HPG * q + HPG].unsqueeze(2).broadcast_to([32, HPG, SP_]), ALU.mult))
                    xq = xtk[0:32, 2, 512 * q:512 * q + 512]
                    v.tensor_tensor(xq, xq, sq[0:32, :], ALU.add).then_inc(r_ya, 1)
                dve.wait_ge(r_ya, 4)
                with turns(dve, 0, SG, (dstep, 3)) as i:
                    for n in range(HPG + 1):
                        if n < HPG:
                            d, b = dbuf[n % 2], ps[:, n % 2, :]
                            h = bass.ds(i * HPG + n, 1)
                            dve.wait_ge(r_ab, i * HPG + (n + 1))
                            dve.wait_ge(r_W, i * HPG + max(n - 1, 0))
                            v.tensor_scalar(d[:, 0:2 * P], b[:, 0:2 * P], av[:, 0, h], 0.0, ALU.subtract, ALU.min)
                            v.tensor_scalar(d[:, 2 * P:3 * P], b[:, P:2 * P], av[:, 1, h], 0.0, ALU.subtract, ALU.min)
                            v.tensor_scalar(d[0:32, 3 * P:SC], b[0:32, 2 * P:T], av[0:32, 2, h], 0.0, ALU.subtract, ALU.min).then_inc(r_d, 1)
                        if n > 0:
                            dve.wait_ge(r_e, i * HPG + n)
                            v.tensor_tensor(wbuf[(n - 1) % 2][:], wbuf[(n - 1) % 2][:], cbm[:, bass.ds(i, 1), :].rearrange("p g s -> p (g s)"),
                                            ALU.mult).then_inc(r_W, 1)
                    dve.wait_ge(r_yh, i * HPG + HPG)
                    for t, (_, rows) in enumerate(TILES):
                        cols = bass.ds(i * GW, GW)
                        dstep(v.tensor_tensor(xtk[0:rows, t, cols], xtk[0:rows, t, cols], ps[0:rows, 2 + t, :], ALU.add))
                        v.tensor_tensor(z[0:rows, t, cols], z[0:rows, t, cols], xtk[0:rows, t, cols], ALU.mult).then_inc(r_z, 1)

            @block.tensor
            def _(pe):
                m = nc.tensor
                pe.wait_ge(r_w, 1)
                with pe.Fori(0, NB // 2) as i:
                    for n in range(2):
                        b = i * 2 + n
                        pe.wait_ge(q_h[n], i * 16 + 16)
                        for q in range(4):
                            pe.wait_ge(r_tc, i * 8 + max(4 * n + q - 1, 0))
                            for c in range(4):
                                last = m.transpose(ps[:, q % 2, c * P:(c + 1) * P], hst[n][:, 4 * q + c, :], ident[:])
                            last.then_inc(r_tr, 1)
                        pe.wait_ge(r_tc, i * 8 + (4 * n + 4))
                        for c in range(XT_):
                            last = m.matmul(ps[:, 4, bass.ds(i * 8 + (32 * c + 4 * n), NS)], hT[:, c, :],
                                            convBC[:, SG + c // 4, bass.ds(i * 8 + (SEQ + 4 * n), NS)], start=True, stop=True)
                        last.then_inc(r_in, 1)
                        pe.wait_ge(r_bm, i * 2 + (n + 1))
                        for q in range(4):
                            pe.wait_ge(r_ud, i * 8 + max(4 * n + q - 1, 0))
                            for c in range(4):
                                last = m.matmul(ps[:, 2 + q % 2, c * P:(c + 1) * P], xw2[:, (4 * q + c) * P:(4 * q + c + 1) * P],
                                                bm[n][:, q * SN:(q + 1) * SN], start=True, stop=True)
                            last.then_inc(r_up, 1)
                for g in range(SG):
                    bT, cT, b = convBC[:, g, :], convBC[:, SG + g, :], 6 + g % 2
                    if g >= 2:
                        pe.wait_ge(r_cm, g - 1)
                    m.matmul(ps[:, b, 0:2 * P], bT[:, 0:P], cT[:, 0:2 * P], start=True, stop=True)
                    m.matmul(ps[:, b, 2 * P:3 * P], bT[:, P:2 * P], cT[:, P:2 * P], start=True, stop=True)
                    m.matmul(ps[0:32, b, 3 * P:SC], bT[:, 2 * P:T], cT[:, 2 * P:T], start=True, stop=True).then_inc(r_cb, 1)
                pe.wait_ge(r_yc, 1)
                for q in range(4):
                    for c in range(4):
                        k = 4 * q + c
                        last = m.transpose(ps[0:32, q, c * P:(c + 1) * P], yis[:, 32 * k:32 * k + 32], ident[:])
                    last.then_inc(r_yt, 1)
                pe.wait_ge(r_w, 3)
                pe.wait_ge(r_cm, SG)
                for q in range(4):
                    if q >= 2:
                        pe.wait_ge(r_hc, q - 1)
                    for c in range(4):
                        k = 4 * q + c
                        for t in range(2):
                            last = m.matmul(ps[:, 5 + q % 2, c * P:(c + 1) * P], xw[:, t, k * P:(k + 1) * P],
                                            btok[:, t, q * SN:(q + 1) * SN], start=(t == 0), stop=(t == 1))
                    last.then_inc(r_hp, 1)
                pe.wait_ge(r_ya, 4)

                with pe.Fori(0, SG) as i:
                    for n in range(HPG + 2):
                        if n < HPG:
                            pe.wait_ge(r_sel, i * HPG + (n + 1))
                            pe.wait_ge(r_d, i * HPG + max(n - 1, 0))
                            m.matmul(ps[:, n % 2, 0:T], ones[0:32, :], ath[n % 2][:], start=True, stop=True).then_inc(r_ab, 1)
                        if n >= 2:
                            h = n - 2
                            if h == 0:
                                pe.wait_ge(r_z, i * 3)
                            pe.wait_ge(r_W, i * HPG + (h + 1))
                            w, cols = wbuf[h % 2], slice(SP_ * h, SP_ * h + SP_)
                            x = [xdt[:, t, bass.ds(i * GW + SP_ * h, SP_)] for t in range(3)]
                            m.matmul(ps[:, 2, cols], w[:, 0:P], x[0], start=True, stop=True)
                            m.matmul(ps[:, 3, cols], w[:, P:2 * P], x[0], start=True, stop=False)
                            m.matmul(ps[:, 3, cols], w[:, 2 * P:3 * P], x[1], start=False, stop=True)
                            m.matmul(ps[0:32, 4, cols], w[:, 3 * P:SC], x[2], start=True, stop=True).then_inc(r_yh, 1)

        n_rs = S("group_rms_ready")
        n_sq = S("group_rms_rooted")
        n_y = S("y_normalised")
        n_t = S("y_transposed")
        n_c = S("y_copied")
        with nc.Block() as block:
            @block.scalar
            def _(act):
                act.wait_ge(n_rs, 1)
                nc.scalar.activation(ss[:], ss[:], ACT.Sqrt).then_inc(n_sq, 1)
                for c in range(XT_):
                    act.wait_ge(n_t, c + 1)
                    nc.scalar.activation(ynT[:, c, :], ps[:, c % 4, 0:T], ACT.Copy, scale=ssdw[:, c:c + 1]).then_inc(n_c, 1)

            @block.vector
            def _(dve):
                v = nc.vector
                dstep.on(dve)
                v.tensor_scalar(ss[:], ss[:], 1.0 / GW, RMS_EPS, ALU.mult, ALU.add).then_inc(n_rs, 1)
                dve.wait_ge(n_sq, 1)
                dstep(v.reciprocal(ss[:], ss[:]))
                for g in range(SG):
                    for t, (_, rows) in enumerate(TILES):
                        y = z[0:rows, t, GW * g:GW * g + GW]
                        v.tensor_scalar(y, y, ss[0:rows, SG * t + g:SG * t + g + 1], None, ALU.mult).then_inc(n_y, 1)

            @block.tensor
            def _(pe):
                for c in range(XT_):
                    pe.wait_ge(n_y, 3 * (c // 4 + 1))
                    if c >= 4:
                        pe.wait_ge(n_c, c - 3)
                    for t, (t0, rows) in enumerate(TILES):
                        last = nc.tensor.transpose(ps[:, c % 4, t0:t0 + rows], z[0:rows, t, c * P:(c + 1) * P], ident[0:rows, 0:rows])
                    last.then_inc(n_t, 1)

        if stop <= 3:
            return
        qT = at("qT", 32, [P, HH, T])
        kT = at("kT", 41.5, [P, HH, T])
        bT = at("bT", 51, [P, HH, T])
        eT = at("eT", 60.5, [P, HH, T])
        vtok = at("vtok", 70, [P, 3, D])
        gtok = at("gtok", 82, [P, 3, D])
        otok = at("otok", 0, [P, 3, D])
        U = [at(f"U{i}", 12 + 4 * i, [P, HH, P]) for i in range(2)]
        vm = [at(f"vm{i}", 20 + 4 * i, [32, NB, P]) for i in range(2)]
        scm = at("scm", 28, [P, 3, HH * CH])
        oiT = at("oiT", 31, [P, HH * 32])
        Sb = at("Sb", 154, [P, NB, HH, P])
        kpt = at("kpt", 186, [P, 3, D])
        mid = at("mid", 198, [P, HH, 16])
        lst = at("lst", 198.5, [P, HH, 16])
        dl = at("dl", 199, [P, HH, 16])
        gate = at("gate", 199.5, [P, HH, 8])
        qs = at("qs", 200, [P, HH, 32])
        lb4 = at("lb4", 201, [P, 4, HH])
        hss = at("hss", 201.25, [P, 3 * HH])
        sq3 = at("sq3", 202, [P, D])

        w_z = 16 * ((XBC + INNER) // CW // 2)
        h_S = S("hg_state_loaded")
        h_p = S("hg_projection_ready")
        h_c = S("hg_projection_copied")
        h_lb = S("lower_bound_step")
        h_f = S("forget_gate_ready")
        h_ln = S("log_gate_ready")
        h_ek = S("k_exponents_ready")
        h_eq = S("q_exponents_ready")
        h_x = S("hg_exponentials_ready")
        h_xe = S("hg_factor_exponents_ready")
        h_k = S("kq_weighted")
        h_kt = S("k_transposed")
        h_kc = S("k_copied")
        h_sc = S("hg_scores_ready")
        h_sm = S("hg_scores_masked")
        h_P = S("chunk_sum_ready")
        h_U = S("state_carried")
        h_o = S("o_ready")
        h_oc = S("o_copied")
        h_oi = S("sample_inter_ready")
        h_oic = S("sample_inter_copied")
        h_vm = S("masked_v_ready")
        h_sd = S("sample_state_decayed")
        h_su = S("sample_sum_ready")
        h_sa = S("sample_state_updated")
        h_n = S("o_normalised")
        h_nt = S("o_transposed")
        h_nc = S("o_transposed_copied")
        NPROJ = 2 * HH + 12

        def chunks32(x):
            return x[:, :, 0:SEQ].rearrange("p h (c s) -> p h c s", s=CH)

        def chunks4(x):
            return x[:, :, SEQ:T].rearrange("p h (c s) -> p h c s", s=NS)

        with nc.Block() as block:
            @block.sync
            def _(sp):
                for n in range(2):
                    sp.dma_start(ring[n][:], chunk_src(C_Q + n * CW)).then_inc(s_w[n], 16)
                for b in range(NB):
                    sp.dma_start(Sb[:, b], state_hgrn[0, b].rearrange("h k v -> k h v")).then_inc(h_S, 16)
                for c in range(2, 8):
                    sp.wait_ge(h_p, 4 * (c - 1) if c <= 5 else 16 + 3 * (c - 5))
                    sp.dma_start(ring[c % 2][:], chunk_src(C_Q + c * CW)).then_inc(s_w[c % 2], 16)
                sp.wait_ge(h_U, 8)
                sp.dma_start(o_hg_p[0, 0].rearrange("h k v -> k h v"), U[0][:]).then_inc(s_out, 16)
                sp.wait_ge(h_sa, 2 * HH)
                for b in range(NB):
                    sp.dma_start(o_hg_s[0, b].rearrange("h k v -> k h v"), Sb[:, b]).then_inc(s_out, 16)
                sp.wait_ge(s_out, 48 + 16 * (NB + 1))

            @block.gpsimd
            def _(pool):
                g = nc.gpsimd
                pool.wait_ge(h_c, NPROJ)
                for h in range(HH):
                    if h >= 2:
                        pool.wait_ge(h_su, 2 * (h - 1))
                    g.tensor_tensor(vm[h % 2][:], vtok[0:32, 2, h * P:(h + 1) * P].unsqueeze(1).broadcast_to([32, NB, P]),
                                    bsel[:].unsqueeze(2).broadcast_to([32, NB, P]), ALU.mult).then_inc(h_vm, 1)
                    if h == 0:
                        pool.wait_ge(h_oi, 1)
                        pool.wait_ge(h_x, 5)
                    s = Sb[:, :, h, :]
                    g.tensor_tensor(s, s, lst[:, h, 8:16].unsqueeze(2).broadcast_to([P, NB, P]), ALU.mult).then_inc(h_sd, 1)

            @block.scalar
            def _(act):
                a = nc.scalar
                astep.on(act)
                act.wait_ge(h_lb, 1)
                a.activation(lb4[:, 1, :], lb4[:, 0, :], ACT.Exp).then_inc(h_lb, 1)
                with act.Fori(0, 2) as i:
                    for n in range(4):
                        act.wait_ge(h_p, i * 4 + (n + 1))
                        a.activation(qT[:, bass.ds(i * 4 + n, 1), :], ps[:, 4 + n:5 + n, 0:T], ACT.Silu).then_inc(h_c, 1)
                with act.Fori(0, 2) as i:
                    for n in range(4):
                        act.wait_ge(h_p, i * 4 + (HH + n + 1))
                        a.activation(eT[:, bass.ds(i * 4 + n, 1), :], ps[:, 4 + n:5 + n, 0:T], ACT.Sigmoid).then_inc(h_c, 1)
                act.wait_ge(h_f, 1)
                a.activation(bT[:], eT[:], ACT.Ln).then_inc(h_ln, 1)
                for j in range(6):
                    t, rows = j % 3, TILES[j % 3][1]
                    act.wait_ge(h_p, 2 * HH + j + 1)
                    a.copy(vtok[0:rows, t, CW * (j // 3):CW * (j // 3) + CW], ps[0:rows, 4 + j % 4, :]).then_inc(h_c, 1)
                act.wait_ge(h_ek, 1)
                a.activation(eT[:], eT[:], ACT.Exp).then_inc(h_x, 1)
                act.wait_ge(h_eq, 1)
                a.activation(bT[:], bT[:], ACT.Exp).then_inc(h_x, 1)
                act.wait_ge(h_xe, 2)
                a.activation(mid[:], mid[:], ACT.Exp).then_inc(h_x, 1)
                a.activation(gate[:], gate[:], ACT.Exp).then_inc(h_x, 1)
                a.activation(lst[:], lst[:], ACT.Exp).then_inc(h_x, 1)
                a.activation(dl[:], dl[:], ACT.Exp).then_inc(h_x, 1)
                for j in range(6, 12):
                    t, rows = j % 3, TILES[j % 3][1]
                    act.wait_ge(h_p, 2 * HH + j + 1)
                    a.activation(gtok[0:rows, t, CW * (j // 3 - 2):CW * (j // 3 - 1)], ps[0:rows, 4 + j % 4, :], ACT.Sigmoid).then_inc(h_c, 1)
                for j in range(6):
                    rows = TILES[j // 2][1]
                    act.wait_ge(h_kt, j + 1)
                    a.copy(kpt[0:rows, j // 2, 512 * (j % 2):512 * (j % 2) + 512], ps[0:rows, j % 4, :]).then_inc(h_kc, 1)
                act.wait_ge(h_oi, 1)
                a.copy(oiT[:], ps[:, 4, 0:256]).then_inc(h_oic, 1)
                for t in range(3):
                    rows = TILES[t][1]
                    act.wait_ge(h_o, (4, 8, 9)[t])
                    a.copy(otok[0:rows, t, :].rearrange("p (b n) -> p b n", b=2), ps[0:rows, 6:8, :]).then_inc(h_oc, 1)
                act.wait_ge(n_rs, 2)
                a.activation(hss[:], hss[:], ACT.Sqrt).then_inc(n_sq, 1)
                for h in range(HH):
                    act.wait_ge(h_nt, h + 1)
                    a.activation(onT[:, h, :], ps[:, h % 2, 0:T], ACT.Copy, scale=hgw[:, h:h + 1]).then_inc(h_nc, 1)

            @block.vector
            def _(dve):
                v = nc.vector
                dstep.on(dve)
                v.tensor_tensor(lb4[:, 0, :], lbv, lbv, ALU.subtract).then_inc(h_lb, 1)
                dve.wait_ge(h_lb, 2)
                dstep(v.reciprocal(lb4[:, 2, :], lb4[:, 1, :]))
                dstep(v.tensor_tensor(lb4[:, 3, :], lb4[:, 1, :], lb4[:, 2, :], ALU.mult))
                dstep(v.tensor_tensor(lb4[:, 0, :], lb4[:, 3, :], lb4[:, 3, :], ALU.subtract))
                dstep(v.tensor_scalar(lb4[:, 1, :], lb4[:, 0, :], -1.0, 1.0, ALU.mult, ALU.add))
                for h in range(HH):
                    dve.wait_ge(h_c, HH + h + 1)
                    dstep(v.tensor_scalar(eT[:, h, :], eT[:, h, :], lb4[:, 1, h:h + 1], lb4[:, 0, h:h + 1], ALU.mult, ALU.add))
                dstep(v.tensor_scalar(kT[:], eT[:], -1.0, 1.0, ALU.mult, ALU.add))
                v.tensor_scalar(eT[:], eT[:], FMIN, None, ALU.max).then_inc(h_f, 1)
                dve.wait_ge(h_ln, 1)
                for h in range(HH):
                    last = v.tensor_tensor_scan(eT[:, h, :], keep[:], bT[:, h, :], 0.0, ALU.mult, ALU.add)
                dstep(last)
                for x, at32, at4 in ((mid, CH // 2 - 1, 1), (lst, CH - 1, NS - 1)):
                    dstep(v.tensor_copy(x[:, :, 0:8].unsqueeze(3), chunks32(eT)[:, :, :, at32:at32 + 1]))
                    dstep(v.tensor_copy(x[:, :, 8:16].unsqueeze(3), chunks4(eT)[:, :, :, at4:at4 + 1]))
                dstep(v.tensor_tensor(chunks32(bT), chunks32(eT), mid[:, :, 0:8].unsqueeze(3).broadcast_to([P, HH, 8, CH]), ALU.subtract))
                dstep(v.tensor_tensor(chunks4(bT), chunks4(eT), mid[:, :, 8:16].unsqueeze(3).broadcast_to([P, HH, 8, NS]), ALU.subtract))
                v.tensor_scalar(eT[:], bT[:], -1.0, EXPMAX, ALU.mult, ALU.min).then_inc(h_ek, 1)
                dve.wait_ge(h_ek, 1)
                v.tensor_scalar(bT[:], bT[:], EXPMAX, None, ALU.min).then_inc(h_eq, 1)
                dstep(v.tensor_tensor(dl[:], lst[:], mid[:], ALU.subtract))
                v.tensor_tensor(gate[:, :, 0:7], dl[:, :, 0:7], mid[:, :, 1:8], ALU.add).then_inc(h_xe, 1)
                v.tensor_copy(gate[:, :, 7:8], dl[:, :, 7:8]).then_inc(h_xe, 1)
                dstep(v.memset(hss[:], 1.0))
                dve.wait_ge(h_x, 1)
                v.tensor_tensor(kT[:], kT[:], eT[:], ALU.mult).then_inc(h_k, 1)
                dve.wait_ge(h_x, 2)
                v.tensor_tensor(qT[:], qT[:], bT[:], ALU.mult).then_inc(h_k, 1)
                dve.wait_ge(h_x, 6)
                dve.wait_ge(h_k, 2)
                v.tensor_tensor(qs[:].rearrange("p h (c s) -> p h c s", s=NS), chunks4(qT), mid[:, :, 8:16].unsqueeze(3)
                                .broadcast_to([P, HH, 8, NS]), ALU.mult).then_inc(h_k, 1)
                v.tensor_tensor(chunks4(eT), chunks4(kT), dl[:, :, 8:16].unsqueeze(3).broadcast_to([P, HH, 8, NS]), ALU.mult).then_inc(h_k, 1)
                dve.wait_ge(h_c, NPROJ)
                dstep(v.memset(U[0][:], 0.0))
                for t in range(2):
                    dve.wait_ge(h_sc, t + 1)
                    v.tensor_tensor(scm[:, t, :].rearrange("p (h s) -> p h s", s=CH), ps[:, 4 + t, 0:256].rearrange("p (h s) -> p h s", s=CH),
                                    cmask[:].unsqueeze(1).broadcast_to([P, HH, CH]), ALU.mult).then_inc(h_sm, 1)
                dve.wait_ge(h_sc, 3)
                v.tensor_tensor(scm[0:32, 2, :].rearrange("p (h s) -> p h s", s=CH), ps[0:32, 5, 256:512].rearrange("p (h s) -> p h s", s=CH),
                                smask[:].unsqueeze(1).broadcast_to([32, HH, CH]), ALU.mult).then_inc(h_sm, 1)
                for c in range(8):
                    dve.wait_ge(h_P, c + 1)
                    if c >= 1:
                        dve.wait_ge(h_o, c)
                    b0, o, n = 2 * (c % 2), U[c % 2], U[(c + 1) % 2]
                    dstep(v.tensor_tensor(n[:].rearrange("p (b h) v -> p b (h v)", b=2), o[:].rearrange("p (b h) v -> p b (h v)", b=2),
                                          ps[:, b0:b0 + 2, :], ALU.add))
                    v.tensor_tensor(n[:], n[:], gate[:, :, c:c + 1].broadcast_to([P, HH, P]), ALU.mult).then_inc(h_U, 1)
                    dve.wait_ge(h_U, c + 1)
                for j in range(2 * HH):
                    h, half = j // 2, j % 2
                    dve.wait_ge(h_su, j + 1)
                    dve.wait_ge(h_sd, h + 1)
                    s = Sb[:, 4 * half:4 * half + 4, h, :]
                    v.tensor_tensor(s, s, ps[:, j % 4, :].rearrange("p (b v) -> p b v", b=4), ALU.add).then_inc(h_sa, 1)
                for t, (_, rows) in enumerate(TILES):
                    dve.wait_ge(h_oc, t + 1)
                    o = otok[0:rows, t, :]
                    dstep(v.tensor_tensor(sq3[0:rows, :], o, o, ALU.mult))
                    dstep(v.tensor_reduce(hss[0:rows, HH * t:HH * t + HH], sq3[0:rows, :].rearrange("p (h v) -> p h v", v=P), AX_X, ALU.add))
                v.tensor_scalar(hss[:], hss[:], 1.0 / P, RMS_EPS, ALU.mult, ALU.add).then_inc(n_rs, 1)
                dve.wait_ge(n_sq, 2)
                dstep(v.reciprocal(hss[:], hss[:]))
                for t, (_, rows) in enumerate(TILES):
                    o = otok[0:rows, t, :].rearrange("p (h v) -> p h v", v=P)
                    dstep(v.tensor_tensor(o, o, hss[0:rows, HH * t:HH * t + HH].unsqueeze(2).broadcast_to([rows, HH, P]), ALU.mult))
                    v.tensor_tensor(otok[0:rows, t, :], otok[0:rows, t, :], gtok[0:rows, t, :], ALU.mult).then_inc(h_n, 1)

            @block.tensor
            def _(pe):
                m = nc.tensor

                def columns(i, n):
                    pe.wait_ge(s_w[n], i * 16 + (w_z + 16))
                    for mt in range(4):
                        if not (isinstance(i, int) and i == 0) or n > 0:
                            pe.wait_ge(h_c, i * 8 + (4 * n + mt - 3))
                        for k in range(KD):
                            last = m.matmul(ps[:, 4 + mt, 0:T], ring[n][:, k, mt * P:(mt + 1) * P], xT[:, k, :],
                                            start=(k == 0), stop=(k == KD - 1))
                        last.then_inc(h_p, 1)

                columns(0, 0)
                columns(0, 1)
                columns(1, 0)
                columns(1, 1)
                for c in range(4):
                    n = c % 2
                    pe.wait_ge(s_w[n], w_z + 16 * (c // 2 + 3))
                    for t, (t0, rows) in enumerate(TILES):
                        j = 3 * c + t
                        pe.wait_ge(h_c, 2 * HH + j - 3)
                        for k in range(KD):
                            last = m.matmul(ps[0:rows, 4 + j % 4, :], xT[:, k, t0:t0 + rows], ring[n][:, k, :],
                                            start=(k == 0), stop=(k == KD - 1))
                        last.then_inc(h_p, 1)
                pe.wait_ge(h_k, 4)
                for j in range(6):
                    t0, rows = TILES[j // 2]
                    if j >= 4:
                        pe.wait_ge(h_kc, j - 3)
                    for c in range(4):
                        src = (kT if j < 4 else eT)[:, 4 * (j % 2) + c, t0:t0 + rows]
                        last = m.transpose(ps[0:rows, j % 4, c * P:(c + 1) * P], src, ident[:])
                    last.then_inc(h_kt, 1)
                pe.wait_ge(h_c, NPROJ)
                for t in range(2):
                    for h in range(HH):
                        for r in range(4):
                            s = slice(P * t + CH * r, P * t + CH * r + CH)
                            last = m.matmul(ps[CH * r:CH * r + CH, 4 + t, CH * h:CH * h + CH], kT[:, h, s], qT[:, h, s], start=True, stop=True)
                    last.then_inc(h_sc, 1)
                pe.wait_ge(h_sm, 2)
                for h in range(HH):
                    last = m.matmul(ps[0:32, 5, 256 + 32 * h:288 + 32 * h], kT[:, h, SEQ:T], qT[:, h, SEQ:T], start=True, stop=True)
                last.then_inc(h_sc, 1)
                pe.wait_ge(h_S, 16 * NB)
                for h in range(HH):
                    for b in range(NB):
                        last = m.matmul(ps[:, 4, 32 * h + NS * b:32 * h + NS * b + NS], Sb[:, b, h, :], qs[:, h, NS * b:NS * b + NS], start=True, stop=True)
                last.then_inc(h_oi, 1)

                def chunk_sum(c):
                    r = slice(CH * (c % 4), CH * (c % 4) + CH)
                    if c >= 2:
                        pe.wait_ge(h_U, c - 1)
                    for h in range(HH):
                        last = m.matmul(ps[:, 2 * (c % 2) + h // 4, (h % 4) * P:(h % 4 + 1) * P], kpt[r, c // 4, h * P:(h + 1) * P],
                                        vtok[r, c // 4, h * P:(h + 1) * P], start=True, stop=True)
                    last.then_inc(h_P, 1)

                pe.wait_ge(h_kc, 6)
                chunk_sum(0)
                pe.wait_ge(h_sm, 3)
                for c in range(8):
                    if c + 1 < 8:
                        chunk_sum(c + 1)
                    t, r = c // 4, slice(CH * (c % 4), CH * (c % 4) + CH)
                    if c == 4:
                        pe.wait_ge(h_oc, 1)
                    if c > 0:
                        pe.wait_ge(h_U, c)
                    for h in range(HH):
                        o = ps[r, 6 + h // 4, (h % 4) * P:(h % 4 + 1) * P]
                        last = m.matmul(o, scm[r, t, CH * h:CH * h + CH], vtok[r, t, h * P:(h + 1) * P], start=True, stop=(c == 0),
                                        tile_position=(CH * (c % 4), CH * (c % 4)))
                        if c > 0:
                            last = m.matmul(o, qT[:, h, CH * c:CH * c + CH], U[c % 2][:, h, :], start=False, stop=True)
                    last.then_inc(h_o, 1)
                pe.wait_ge(h_oc, 2)
                pe.wait_ge(h_oic, 1)
                for h in range(HH):
                    o = ps[0:32, 6 + h // 4, (h % 4) * P:(h % 4 + 1) * P]
                    m.matmul(o, scm[0:32, 2, 32 * h:32 * h + 32], vtok[0:32, 2, h * P:(h + 1) * P], start=True, stop=False)
                    last = m.matmul(o, oiT[:, 32 * h:32 * h + 32], ident[:], start=False, stop=True)
                last.then_inc(h_o, 1)
                pe.wait_ge(h_U, 8)
                for j in range(2 * HH):
                    h, half = j // 2, j % 2
                    if j >= 4:
                        pe.wait_ge(h_sa, j - 3)
                    pe.wait_ge(h_vm, h + 1)
                    m.matmul(ps[:, j % 4, :], kpt[0:32, 2, h * P:(h + 1) * P], vm[h % 2][:, 4 * half:4 * half + 4, :].rearrange("p b v -> p (b v)"),
                             start=True, stop=True).then_inc(h_su, 1)
                pe.wait_ge(h_sa, 2 * HH)
                for h in range(HH):
                    if h >= 2:
                        pe.wait_ge(h_nc, h - 1)
                    for t, (t0, rows) in enumerate(TILES):
                        pe.wait_ge(h_n, t + 1)
                        last = m.transpose(ps[:, h % 2, t0:t0 + rows], otok[0:rows, t, h * P:(h + 1) * P], ident[0:rows, 0:rows])
                    last.then_inc(h_nt, 1)

        if stop <= 4:
            return
        wSSD = at("wSSD", 32, [P, XT_, D])
        wHG = at("wHG", 154, [P, KD, D])
        wOUT = at("wOUT", 0, [P, KD, D])
        gA = at("gA", 186, [P, KD, T])
        gB = at("gB", 195.25, [P, KD, T])
        mT = at("mT", 116, [P, KD, T])
        tmpA = [at(f"tmpA{i}", 204.5 + 1.25 * i, [P, T]) for i in range(2)]
        lnw = at("lnw", 125.5, [P, D])
        lnb = at("lnb", 129.5, [P, D])
        lnq = at("lnq", 133.5, [P, D])
        lst4 = at("lst4", 137.5, [P, 6])
        lmu = at("lmu", 137.625, [P, 3])
        lvar = at("lvar", 137.75, [P, 3])

        w_g = w_z + 16 * (4 * D // CW // 2)
        g_ws, g_wh, g_wo, g_ln = S("ssd_proj_loaded"), S("hg_proj_loaded"), S("w_out_loaded"), S("ln_loaded")
        g_p, g_c = S("output_gate_ready"), S("output_gate_copied")
        g_ab, g_m = S("branches_ready"), S("merged_ready")
        g_mx, g_x = S("mix_ready"), S("residual_added")
        ln_c, ln_v, ln_r, ln_s = S("ln_centred"), S("ln_squares_ready"), S("ln_variance_ready"), S("ln_rooted")
        ln_done = S("ln_done")

        def ln_vector(dve, dstep, n):
            v = nc.vector
            dstep(v.tensor_tensor(lmu[:], lst4[:, 0:6:2], lst4[:, 1:6:2], ALU.add))
            dstep(v.tensor_scalar(lmu[:], lmu[:], 1.0 / D, None, ALU.mult))
            for t, (_, rows) in enumerate(TILES):
                x = xtok[0:rows, t, :]
                v.tensor_scalar(x, x, lmu[0:rows, t:t + 1], None, ALU.subtract).then_inc(ln_c, 1)
            dve.wait_ge(ln_v, 3 * n)
            v.tensor_scalar(lvar[:], lvar[:], 1.0 / D, LN_EPS, ALU.mult, ALU.add).then_inc(ln_r, 1)
            dve.wait_ge(ln_s, n)
            dstep(v.reciprocal(lvar[:], lvar[:]))
            dve.wait_ge(ln_c, 3 * n)
            for t, (_, rows) in enumerate(TILES):
                x = xtok[0:rows, t, :]
                dstep(v.scalar_tensor_tensor(x, x, lvar[0:rows, t:t + 1], lnw[0:rows, :], ALU.mult, ALU.mult))
                v.tensor_tensor(x, x, lnb[0:rows, :], ALU.add).then_inc(ln_done, 1)

        def ln_scalar(act, n):
            for t, (_, rows) in enumerate(TILES):
                act.wait_ge(ln_c, 3 * (n - 1) + t + 1)
                if t > 0 or n > 1:
                    act.wait_ge(ln_v, 3 * (n - 1) + t)
                nc.scalar.activation(lnq[0:rows, :], xtok[0:rows, t, :], ACT.Square, accum_out=lvar[0:rows, t:t + 1]).then_inc(ln_v, 1)
            act.wait_ge(ln_r, n)
            nc.scalar.activation(lvar[:], lvar[:], ACT.Sqrt).then_inc(ln_s, 1)

        with nc.Block() as block:
            @block.sync
            def _(sp):
                for n in range(2):
                    sp.dma_start(ring[n][:], chunk_src(C_GA + n * CW)).then_inc(s_w[n], 16)
                sp.dma_start(wHG[:], hg_proj[0].rearrange("(k p) n -> p k n", p=P)).then_inc(g_wh, 16)
                for n in range(2):
                    sp.wait_ge(g_p, 4 * n + 4)
                    sp.dma_start(ring[n][:], chunk_src(C_GB + n * CW)).then_inc(s_w[n], 16)
                sp.dma_start(wSSD[:], ssd_proj[0].rearrange("(k p) n -> p k n", p=P)).then_inc(g_ws, 16)
                sp.wait_ge(g_p, 16)
                sp.dma_start(wOUT[:], w_out[0].rearrange("(k p) n -> p k n", p=P)).then_inc(g_wo, 16)
                sp.wait_ge(g_ab, KD)
                sp.dma_start(lnw[:], row(ln1_g[0])).then_inc(g_ln, 16)
                sp.dma_start(lnb[:], row(ln1_b[0])).then_inc(g_ln, 16)

            @block.scalar
            def _(act):
                for dst, first in ((gA, 0), (gB, KD)):
                    with act.Fori(0, 2) as i:
                        for n in range(4):
                            act.wait_ge(g_p, i * 4 + (first + n + 1))
                            nc.scalar.activation(dst[:, bass.ds(i * 4 + n, 1), :], ps[:, 4 + n:5 + n, 0:T], ACT.Sigmoid).then_inc(g_c, 1)
                ln_scalar(act, 1)

            @block.vector
            def _(dve):
                v = nc.vector
                dstep.on(dve)
                for c in range(KD):
                    dve.wait_ge(g_ab, c + 1)
                    if c == 0:
                        dve.wait_ge(g_c, 2 * KD)
                    if c >= 2:
                        dve.wait_ge(g_m, c - 1)
                    b = 2 * (c % 2)
                    dstep(v.tensor_tensor(tmpA[c % 2][:], ps[:, b, 0:T], gA[:, c, :], ALU.mult))
                    dstep(v.tensor_tensor(mT[:, c, :], ps[:, b + 1, 0:T], gB[:, c, :], ALU.mult))
                    v.tensor_tensor(mT[:, c, :], mT[:, c, :], tmpA[c % 2][:], ALU.add).then_inc(g_m, 1)
                v.memset(lvar[:], 1.0)
                dstep(v.memset(lst4[:], 0.0))
                for j in range(6):
                    t, n, rows = j // 2, j % 2, TILES[j // 2][1]
                    dve.wait_ge(g_mx, j + 1)
                    x = xtok[0:rows, t, 512 * n:512 * n + 512]
                    v.scalar_tensor_tensor(x, x, ALPHA, ps[0:rows, 4 + j % 4, :], ALU.mult, ALU.add,
                                           accum_out=lst4[0:rows, j:j + 1]).then_inc(g_x, 1)
                dve.wait_ge(g_x, 6)
                dve.wait_ge(g_ln, 32)
                ln_vector(dve, dstep, 1)

            @block.tensor
            def _(pe):
                m = nc.tensor
                for c in range(4):
                    pe.wait_ge(s_w[c % 2], w_g + 16 * (c // 2 + 1))
                    for mt in range(4):
                        if c > 0:
                            pe.wait_ge(g_c, 4 * c + mt - 3)
                        for k in range(KD):
                            last = m.matmul(ps[:, 4 + mt, 0:T], ring[c % 2][:, k, mt * P:(mt + 1) * P], xT[:, k, :],
                                            start=(k == 0), stop=(k == KD - 1))
                        last.then_inc(g_p, 1)
                pe.wait_ge(g_wh, 16)
                pe.wait_ge(g_ws, 16)
                for c in range(KD):
                    if c >= 2:
                        pe.wait_ge(g_m, c - 1)
                    b, cols = 2 * (c % 2), slice(c * P, (c + 1) * P)
                    for k in range(HH):
                        m.matmul(ps[:, b, 0:T], wHG[:, k, cols], onT[:, k, :], start=(k == 0), stop=(k == HH - 1))
                    for k in range(XT_):
                        last = m.matmul(ps[:, b + 1, 0:T], wSSD[:, k, cols], ynT[:, k, :], start=(k == 0), stop=(k == XT_ - 1))
                    last.then_inc(g_ab, 1)
                pe.wait_ge(g_wo, 16)
                pe.wait_ge(g_m, KD)
                pe.wait_ge(g_c, 2 * KD)
                for j in range(6):
                    (t0, rows), n = TILES[j // 2], j % 2
                    if j >= 4:
                        pe.wait_ge(g_x, j - 3)
                    for k in range(KD):
                        last = m.matmul(ps[0:rows, 4 + j % 4, :], mT[:, k, t0:t0 + rows], wOUT[:, k, 512 * n:512 * n + 512],
                                        start=(k == 0), stop=(k == KD - 1))
                    last.then_inc(g_mx, 1)

        if stop <= 5:
            return
        yacc = at("yacc", 154, [P, 3, D])
        psel = at("psel", 166, [P, 3, BLK])
        gsel = at("gsel", 167, [P, 3, BLK])
        xe = at("xe", 168, [P, KD, BLK])
        gu = [at(f"gu{i}", 170 + 2 * i, [P, 2, 4, BLK]) for i in range(2)]
        aT = at("aT", 174, [P, KD, BLK])
        sg = [at(f"sg{i}", 176 + i, [P, 4, BLK]) for i in range(2)]
        gT = at("gT", 178, [BLK, 3 * P])
        ysb = at("ysb", 180, [BLK, D])
        biasT = at("biasT", 184, [P, 16, E_])
        bse = at("bse", 186, [P, 16])
        dsel = at("dsel", 186.125, [P, 3])
        boff = at("boff", 186.25, [P, 1])
        dest = at("dest", 187, [P, 3, E_])
        gm = at("gm", 187.5, [P, 3, E_])
        tab = at("tab", 188, [1, 96], I32)
        TAB_N = 64
        hT_ = at("h_T", 116, [P, KD, T])
        wr = at("wr", 189, [P, KD, E_])
        rbr = at("rbr", 190, [P, E_])
        lg = at("lg", 190.25, [P, 3, E_])
        mx8 = at("mx8", 190.75, [P, 3, 8])
        ix8 = at("ix8", 191, [P, 3, 8], U32)
        gt4 = at("gt4", 191.25, [P, 3, TOPK])
        id4 = at("id4", 191.375, [P, 3, TOPK])
        gsum = at("gsum", 191.5, [P, 3])
        msk = at("msk", 188.5, [P, 3, E_])
        eq = at("eq", 192, [P, 3, TOPK, E_])
        eg = at("eg", 193.5, [P, 3, TOPK, E_])
        cum = at("cum", 195, [P, 3, E_])
        cnt = at("cnt", 195.5, [P, E_])
        nbl = at("nbl", 195.75, [P, E_])
        binc = at("binc", 196, [P, E_])
        st64 = at("st64", 196.25, [P, E_])
        ebc = at("ebc", 196.5, [P, 1])
        gmT = at("gmT", 197, [E_, T])
        bgr = at("bgr", 198.25, [E_, 2 * D])
        bdr = at("bdr", 144, [E_, D])

        t_wr, t_b, t_ht, t_hc = S("router_loaded"), S("expert_biases_loaded"), S("h_transposed"), S("h_copied")
        t_lg, t_e, t_ex, t_mk = S("logits_ready"), S("top_values_ready"), S("top_exp_ready"), S("choices_ready")
        t_cm, t_cc, t_eb, t_tb = S("token_counts_ready"), S("counts_copied"), S("block_experts_ready"), S("block_table_row")
        t_bt, t_bc, t_gt, t_gc = S("biases_transposed"), S("biases_copied"), S("gates_transposed"), S("gates_copied")
        t_y, t_yc = S("bias_sum_ready"), S("bias_sum_copied")

        with nc.Block() as block:
            @block.sync
            def _(sp):
                sp.dma_start(wr[:], router_w[0].rearrange("(k p) n -> p k n", p=P)).then_inc(t_wr, 16)
                sp.dma_start(rbr[:], row(router_b[0])).then_inc(t_wr, 16)
                sp.dma_start(bgr[:], b_gu[0]).then_inc(t_b, 16)
                sp.dma_start(bdr[:], b_down[0]).then_inc(t_b, 16)

            @block.scalar
            def _(act):
                a = nc.scalar
                for k in range(KD):
                    act.wait_ge(t_ht, k + 1)
                    a.copy(hT_[:, k, :], ps[:, k % 2, 0:T]).then_inc(t_hc, 1)
                act.wait_ge(t_bt, 1)
                a.copy(biasT[:].rearrange("p f e -> p (f e)"), ps[:, 3, :]).then_inc(t_bc, 1)
                act.wait_ge(t_e, 1)
                a.activation(gt4[:], gt4[:], ACT.Exp).then_inc(t_ex, 1)
                act.wait_ge(t_gt, 1)
                a.copy(gmT[:], ps[0:E_, 0, 0:T]).then_inc(t_gc, 1)
                for j in range(6):
                    rows = TILES[j // 2][1]
                    act.wait_ge(t_y, j + 1)
                    a.copy(yacc[0:rows, j // 2, 512 * (j % 2):512 * (j % 2) + 512], ps[0:rows, 4 + j % 4, :]).then_inc(t_yc, 1)

            @block.vector
            def _(dve):
                v = nc.vector
                dstep.on(dve)
                v.memset(mx8[:], 0.0)
                v.memset(cum[:], 0.0)
                dstep(v.memset(ix8[:], 0))
                dve.wait_ge(t_wr, 32)
                dve.wait_ge(t_lg, 1)
                for t, (_, rows) in enumerate(TILES):
                    dstep(v.tensor_tensor(lg[0:rows, t, :], ps[0:rows, 2, 32 * t:32 * t + 32], rbr[0:rows, :], ALU.add))
                    dstep(v.max(mx8[0:rows, t, :], lg[0:rows, t, :]))
                    dstep(v.max_index(ix8[0:rows, t, :], mx8[0:rows, t, :], lg[0:rows, t, :]))
                v.tensor_tensor(gt4[:], mx8[:, :, 0:TOPK], mx8[:, :, 0:1].broadcast_to([P, 3, TOPK]), ALU.subtract).then_inc(t_e, 1)
                dstep(v.tensor_copy(id4[:], ix8[:, :, 0:TOPK]))
                dve.wait_ge(t_ex, 1)
                dstep(v.tensor_reduce(gsum[:], gt4[:], AX_X, ALU.add))
                dstep(v.reciprocal(gsum[:], gsum[:]))
                dstep(v.tensor_tensor(gt4[:], gt4[:], gsum[:].unsqueeze(2).broadcast_to([P, 3, TOPK]), ALU.mult))
                dstep(v.tensor_tensor(eq[:], ecol[:].unsqueeze(1).unsqueeze(1).broadcast_to([P, 3, TOPK, E_]),
                                      id4[:].unsqueeze(3).broadcast_to([P, 3, TOPK, E_]), ALU.is_equal))
                dstep(v.tensor_tensor(eg[:], eq[:], gt4[:].unsqueeze(3).broadcast_to([P, 3, TOPK, E_]), ALU.mult))
                v.tensor_reduce(msk[:], eq[:].rearrange("p t k e -> p t e k"), AX_X, ALU.add).then_inc(t_mk, 1)
                v.tensor_reduce(gm[:], eg[:].rearrange("p t k e -> p t e k"), AX_X, ALU.add).then_inc(t_mk, 1)
                dve.wait_ge(t_cm, 1)
                for t, (_, rows) in enumerate(TILES):
                    v.tensor_copy(cum[0:rows, t, :], ps[0:rows, 2, 128 + 32 * t:160 + 32 * t])
                dstep(v.tensor_copy(cnt[:], ps[:, 2, 224:256]))
                dstep(v.tensor_scalar(nbl[:], cnt[:], 0.0, None, ALU.is_gt))
                for j in range(1, (T + BLK - 1) // BLK):
                    dstep(v.scalar_tensor_tensor(nbl[:], cnt[:], float(BLK * j), nbl[:], ALU.is_gt, ALU.add))
                dstep(v.tensor_tensor_scan(binc[:], ones[:, 0:E_], nbl[:], 0.0, ALU.mult, ALU.add))
                dstep(v.tensor_tensor(st64[:], binc[:], nbl[:], ALU.subtract))
                dstep(v.tensor_scalar(st64[:], st64[:], float(BLK), None, ALU.mult))
                dstep(v.tensor_tensor(dest[:], cum[:], st64[:].unsqueeze(1).broadcast_to([P, 3, E_]), ALU.add))
                dve.wait_ge(t_mk, 2)
                dstep(v.tensor_tensor(dest[:], dest[:], msk[:], ALU.mult))
                dstep(v.tensor_scalar(dest[:], dest[:], -1.0, None, ALU.add))
                dstep(v.tensor_scalar(lg[:, 0, :], binc[:], prow[:, 0:1], None, ALU.is_le))
                dstep(v.tensor_reduce(ebc[:], lg[:, 0, :], AX_X, ALU.add))
                v.tensor_scalar(ebc[:], ebc[:], float(E_ - 1), None, ALU.min).then_inc(t_eb, 1)
                dve.wait_ge(t_tb, 1)
                v.tensor_copy(tab[0:1, 0:64], ps[0:1, 2, 256:320])
                v.tensor_copy(tab[0:1, TAB_N:TAB_N + 1], binc[0:1, E_ - 1:E_])

            @block.tensor
            def _(pe):
                m = nc.tensor
                for k in range(KD):
                    if k >= 2:
                        pe.wait_ge(t_hc, k - 1)
                    for t, (t0, rows) in enumerate(TILES):
                        last = m.transpose(ps[:, k % 2, t0:t0 + rows], xtok[0:rows, t, k * P:(k + 1) * P], ident[0:rows, 0:rows])
                    last.then_inc(t_ht, 1)
                pe.wait_ge(t_b, 32)
                for f in range(16):
                    last = m.transpose(ps[:, 3, 32 * f:32 * f + 32], bgr[:, f * P:(f + 1) * P], ident[0:32, 0:32])
                last.then_inc(t_bt, 1)
                pe.wait_ge(t_hc, KD)
                pe.wait_ge(t_wr, 32)
                for t, (t0, rows) in enumerate(TILES):
                    for k in range(KD):
                        last = m.matmul(ps[0:rows, 2, 32 * t:32 * t + 32], hT_[:, k, t0:t0 + rows], wr[:, k, :], start=(k == 0), stop=(k == KD - 1))
                last.then_inc(t_lg, 1)
                pe.wait_ge(t_mk, 2)
                for o, lhs in ((128, (tri,)), (160, (ones, tri)), (192, (ones, ones, tri)), (224, (ones, ones, ones))):
                    rows = 32 if o == 192 else P
                    for t, l in enumerate(lhs):
                        kk = TILES[t][1]
                        last = m.matmul(ps[0:rows, 2, o:o + 32], l[0:kk, 0:rows], msk[0:kk, t, :], start=(t == 0), stop=(t == len(lhs) - 1))
                last.then_inc(t_cm, 1)
                for t, (t0, rows) in enumerate(TILES):
                    last = m.transpose(ps[0:E_, 0, t0:t0 + rows], gm[0:rows, t, :], ident[0:rows, 0:rows])
                last.then_inc(t_gt, 1)
                pe.wait_ge(t_eb, 1)
                m.matmul(ps[0:1, 2, 256:320], ebc[0:64, 0:1], ident[0:64, 0:64], start=True, stop=True).then_inc(t_tb, 1)
                pe.wait_ge(t_gc, 1)
                for j in range(6):
                    (t0, rows), n = TILES[j // 2], j % 2
                    if j >= 4:
                        pe.wait_ge(t_yc, j - 3)
                    m.matmul(ps[0:rows, 4 + j % 4, :], gmT[:, t0:t0 + rows], bdr[:, 512 * n:512 * n + 512], start=True, stop=True).then_inc(t_y, 1)

        if stop <= 6:
            return
        wA = [at(f"wGU{i}", 32 * i, [P, KD, 2, CW]) for i in range(2)]
        wD = at("wD", 64, [P, KD, D])
        m_w = [S(f"expert_gu_loaded{i}") for i in range(2)]
        m_wd = S("expert_down_loaded")
        m_p, m_g, m_b = S("block_tokens_selected"), S("block_gates_selected"), S("block_bias_selected")
        m_x, m_xc = S("block_gathered"), S("block_copied")
        m_u = S("gate_up_ready")
        m_gl, m_sg, m_a = S("gate_limited"), S("gate_sigmoid_ready"), S("activation_ready")
        m_gt, m_gc = S("block_gates_transposed"), S("block_gates_copied")
        m_y, m_yc = S("block_output_ready"), S("block_output_copied")
        m_s, m_sa = S("scattered"), S("scattered_added")
        m_z = S("block_buffers_cleared")
        PER = 8

        with nc.Block() as block:
            def blocks(eng):
                return eng.value_load(tab[0:1, TAB_N:TAB_N + 1], min_val=1, max_val=NBLK)

            @block.sync
            def _(sp):
                nb = blocks(sp)
                with sp.Fori(0, NBLK) as b:
                    with sp.If(b < nb):
                        e = sp.value_load(tab[0:1, bass.ds(b, 1)], min_val=0, max_val=E_ - 1)
                        for half in range(2):
                            sp.wait_ge(m_u, b * 2)
                            for u in range(2):
                                sp.dma_start(wA[half][:, :, u, :], w_gu[0, bass.ds(e, 1), :, u * D + half * CW:u * D + half * CW + CW]
                                             .rearrange("a (k p) n -> p (a k) n", p=P)).then_inc(m_w[half], 16)
                        sp.wait_ge(m_y, b)
                        sp.dma_start(wD[:], w_down[0, bass.ds(e, 1)].rearrange("a (k p) n -> p (a k) n", p=P)).then_inc(m_wd, 16)

            @block.scalar
            def _(act):
                a = nc.scalar
                nb = blocks(act)
                act.wait_ge(m_x, 1)
                a.copy(xe[:].rearrange("p k j -> p (k j)"), ps[:, 0, :]).then_inc(m_xc, 1)
                with act.Fori(0, NBLK) as b:
                    with act.If(b < nb):
                        for half in range(2):
                            act.wait_ge(m_gl, b * 2 + (half + 1))
                            a.activation(sg[half][:], gu[half][:, 0], ACT.Sigmoid, scale=SALPHA).then_inc(m_sg, 1)
                        act.wait_ge(m_gt, b + 1)
                        a.copy(gT[:, 0:T], ps[0:BLK, 0, 0:T]).then_inc(m_gc, 1)
                        act.wait_ge(m_x, b + 2)
                        a.copy(xe[:].rearrange("p k j -> p (k j)"), ps[:, 0, :]).then_inc(m_xc, 1)
                        act.wait_ge(m_y, b + 1)
                        a.copy(ysb[:].rearrange("p (b n) -> p b n", b=2), ps[0:BLK, 3:5, :]).then_inc(m_yc, 1)

            @block.vector
            def _(dve):
                v = nc.vector
                dstep.on(dve)
                nb = blocks(dve)
                v.memset(ysb[:], 0.0).then_inc(m_z, 1)
                v.memset(gT[:], 0.0).then_inc(m_z, 1)
                dstep(v.memset(boff[:], 0.0))

                def tokens(e):
                    dstep(v.tensor_scalar(dsel[:].unsqueeze(2), dest[:, :, bass.ds(e, 1)], boff[:, 0:1], None, ALU.subtract))
                    v.tensor_tensor(psel[:], jcol[:].unsqueeze(1).broadcast_to([P, 3, BLK]), dsel[:].unsqueeze(2).broadcast_to([P, 3, BLK]),
                                    ALU.is_equal).then_inc(m_p, 1)

                def gates(e):
                    v.tensor_tensor(gsel[:], psel[:], gm[:, :, bass.ds(e, 1)].broadcast_to([P, 3, BLK]), ALU.mult).then_inc(m_g, 1)

                def bias(e):
                    v.tensor_copy(bse[:].unsqueeze(2), biasT[:, :, bass.ds(e, 1)]).then_inc(m_b, 1)

                def add(j, n):
                    rows = TILES[j // 2][1]
                    y = yacc[0:rows, j // 2, 512 * (j % 2):512 * (j % 2) + 512]
                    dve.wait_ge(m_s, n + (j + 1))
                    v.tensor_tensor(y, y, ps[0:rows, 5 + j % 3, :], ALU.add).then_inc(m_sa, 1)

                e = dve.value_load(tab[0:1, 0:1], min_val=0, max_val=E_ - 1)
                tokens(e)
                dve.wait_ge(m_p, 1)
                gates(e)
                bias(e)
                with turns(dve, 0, NBLK, (dstep, PER)) as b:
                    with dve.If(b < nb):
                        e = dve.value_load(tab[0:1, bass.ds(b + 1, 1)], min_val=0, max_val=E_ - 1)
                        dstep(v.tensor_scalar(boff[:], boff[:], float(BLK), None, ALU.add))
                        for half in range(2):
                            g, u = gu[half][:, 0], gu[half][:, 1]
                            dve.wait_ge(m_u, b * 2 + (half + 1))
                            dve.wait_ge(m_b, b + 1)
                            dstep(v.tensor_tensor(gu[half][:], ps[:, 1 + half, :].rearrange("p (u f j) -> p u f j", u=2, f=4),
                                                  bse[:].rearrange("p (u f) -> p u f", u=2)[:, :, 4 * half:4 * half + 4].unsqueeze(3)
                                                  .broadcast_to([P, 2, 4, BLK]), ALU.add))
                            v.tensor_scalar(g, g, LIMIT, None, ALU.min).then_inc(m_gl, 1)
                            dstep(v.tensor_scalar(u, u, LIMIT, -LIMIT, ALU.min, ALU.max))
                            dve.wait_ge(m_gl, b * 2 + (half + 1))
                            dstep(v.scalar_tensor_tensor(u, u, 1.0, g, ALU.add, ALU.mult))
                            if half == 0:
                                dve.wait_ge(m_x, b + 1)
                                dve.wait_ge(m_g, b + 1)
                                tokens(e)
                            dve.wait_ge(m_sg, b * 2 + (half + 1))
                            v.tensor_tensor(aT[:, 4 * half:4 * half + 4, :], u, sg[half][:], ALU.mult).then_inc(m_a, 1)
                        dve.wait_ge(m_p, b + 2)
                        for j in range(6):
                            if j == 0:
                                dve.wait_ge(m_sa, b * 6)
                            add(j, b * 6)
                        dve.wait_ge(m_gt, b + 1)
                        gates(e)
                        bias(e)
                dve.wait_ge(m_sa, nb * 6)
                for j in range(6):
                    add(j, nb * 6)

            @block.tensor
            def _(pe):
                m = nc.tensor
                nb = blocks(pe)

                def gather():
                    for k in range(KD):
                        for t, (_, rows) in enumerate(TILES):
                            last = m.matmul(ps[:, 0, BLK * k:BLK * k + BLK], xtok[0:rows, t, k * P:(k + 1) * P], psel[0:rows, t, :],
                                            start=(t == 0), stop=(t == 2))
                    last.then_inc(m_x, 1)

                def scatter(n):
                    for j in range(6):
                        t0 = TILES[j // 2][0]
                        pe.wait_ge(m_sa, n + max(j - 2, 0))
                        m.matmul(ps[:, 5 + j % 3, :], gT[:, t0:t0 + P], ysb[:, 512 * (j % 2):512 * (j % 2) + 512],
                                 start=True, stop=True).then_inc(m_s, 1)

                pe.wait_ge(m_z, 2)
                pe.wait_ge(m_p, 1)
                gather()
                with pe.Fori(0, NBLK) as b:
                    with pe.If(b < nb):
                        pe.wait_ge(m_xc, b + 1)
                        for half in range(2):
                            pe.wait_ge(m_w[half], b * 32 + 32)
                            pe.wait_ge(m_a, b * 2)
                            for u in range(2):
                                for f in range(4):
                                    for k in range(KD):
                                        last = m.matmul(ps[:, 1 + half, (4 * u + f) * BLK:(4 * u + f + 1) * BLK],
                                                        wA[half][:, k, u, f * P:(f + 1) * P], xe[:, k, :], start=(k == 0), stop=(k == KD - 1))
                            last.then_inc(m_u, 1)
                        pe.wait_ge(m_yc, b)
                        scatter(b * 6)
                        pe.wait_ge(m_g, b + 1)
                        for t, (t0, rows) in enumerate(TILES):
                            last = m.matmul(ps[0:BLK, 0, t0:t0 + rows], gsel[0:rows, t, :], ident[0:rows, 0:rows], start=True, stop=True)
                        last.then_inc(m_gt, 1)
                        pe.wait_ge(m_p, b + 2)
                        pe.wait_ge(m_gc, b + 1)
                        gather()
                        pe.wait_ge(m_wd, b * 16 + 16)
                        pe.wait_ge(m_a, b * 2 + 2)
                        for n in range(2):
                            for k in range(KD):
                                last = m.matmul(ps[0:BLK, 3 + n, :], aT[:, k, :], wD[:, k, 512 * n:512 * n + 512], start=(k == 0), stop=(k == KD - 1))
                        last.then_inc(m_y, 1)
                pe.wait_ge(m_yc, nb)
                scatter(nb * 6)

        if stop <= 7:
            return
        dstep = Steps(S("last_dve_step"))
        with nc.Block() as block:
            @block.sync
            def _(sp):
                sp.dma_start(lnw[:], row(ln2_g[0])).then_inc(g_ln, 16)
                sp.dma_start(lnb[:], row(ln2_b[0])).then_inc(g_ln, 16)
                sp.wait_ge(ln_done, 6)
                for t in range(2):
                    sp.dma_start(y_prompt[0, P * t:P * t + P, :], xtok[:, t, :]).then_inc(s_out, 16)
                sp.dma_start(y_sample.rearrange("b s d -> (b s) d"), xtok[0:32, 2, :]).then_inc(s_out, 16)
                sp.wait_ge(s_out, 48 + 16 * (NB + 1) + 48)

            @block.scalar
            def _(act):
                ln_scalar(act, 2)

            @block.vector
            def _(dve):
                v = nc.vector
                dstep.on(dve)
                dstep(v.memset(lst4[:], 0.0))
                for t, (_, rows) in enumerate(TILES):
                    x = xtok[0:rows, t, :]
                    dstep(v.scalar_tensor_tensor(x, x, ALPHA, yacc[0:rows, t, :], ALU.mult, ALU.add,
                                                 accum_out=lst4[0:rows, 2 * t:2 * t + 1]))
                dve.wait_ge(g_ln, 64)
                ln_vector(dve, dstep, 2)


_INS = ["x_prompt", "x_sample", "state_hgrn", "state_ssm", "state_conv", "hg_lower_bounds", "w_in", "hg_norm_w",
        "hg_proj", "conv_w", "conv_b", "dt_bias", "a_log", "d_skip", "ssd_norm_w", "ssd_proj", "w_out", "ln1_g",
        "ln1_b", "router_w", "router_b", "w_gu", "b_gu", "w_down", "b_down", "ln2_g", "ln2_b"]
_OUTS = [(1, SEQ, D), (NB, NS, D), (1, 1, HH, P, P), (1, 1, SH, SP_, SN), (1, 1, CK - 1, XBC),
         (1, NB, HH, P, P), (1, NB, SH, SP_, SN), (1, NB, CK - 1, XBC)]


def kernel(**inputs):
    import numpy as _np
    import concourse.bacc as _bacc
    from concourse.bass_utils import run_bass_kernel_spmd as _run

    nc = _bacc.Bacc("TRN2", target_bir_lowering=False, num_devices=1)
    arrays, args = {}, []
    for name in _INS:
        a = _np.ascontiguousarray(inputs[name])
        arrays[f"in_{name}"] = a
        args.append(nc.dram_tensor(f"in_{name}", a.shape, mybir.dt.from_np(a.dtype), kind="ExternalInput").ap())
    for i, shape in enumerate(_OUTS):
        args.append(nc.dram_tensor(f"out_{i}", shape, F32, kind="ExternalOutput").ap())
    build(nc, *args)
    r = _run(nc, [arrays], core_ids=[0])
    return tuple(r.results[0][f"out_{i}"] for i in range(len(_OUTS)))
```

```python
from contextlib import ExitStack, contextmanager

import concourse.bass as bass
from concourse import mybir

F32 = mybir.dt.float32
I32 = mybir.dt.int32
U32 = mybir.dt.uint32
ALU = mybir.AluOpType
ACT = mybir.ActivationFunctionType
AX_X = mybir.AxisListType.X

P = 128
D = 1024
SEQ = 256
NB, NS = 8, 4
T = SEQ + NB * NS
TILES = ((0, 128), (128, 128), (256, 32))
KD = D // P
HH = 8
CH = 32
SH, SP_, SG, SN = 32, 64, 4, 128
INNER = SH * SP_
HPG = SH // SG
GW = INNER // SG
XBC = INNER + 2 * SG * SN
CT = XBC // P
XT_ = INNER // P
CK = 4
E_, TOPK = 32, 4
BLK = 64
NBLK = (T * TOPK + E_ * (BLK - 1)) // BLK
LIMIT, SALPHA = 7.0, 1.702
ALPHA = 2.0 ** 0.25
LN_EPS, RMS_EPS = 1e-5, 1e-6
C_Q, C_F, C_V, C_G, C_Z = 0, D, 2 * D, 3 * D, 4 * D
C_X = C_Z + INNER
C_DT = C_X + XBC
C_GA = C_DT + SH
C_GB = C_GA + D
CW = 512
FROW = 3 + SEQ
CROW = FROW + NB * (CK - 1 + NS)
CO = CROW - (CK - 1)
SC = 416
EXPMAX = 80.0
FMIN = 2.0 ** -62


class Steps:

    def __init__(self, sem):
        self.sem, self.n = sem, 0

    def on(self, eng):
        self.eng = eng
        return self

    def __call__(self, ins):
        ins.then_inc(self.sem, 1)
        self.n = self.n + 1
        self.eng.wait_ge(self.sem, self.n)


@contextmanager
def turns(eng, first, end, *counts):
    base = [s.n - first * per for s, per in counts]
    with eng.Fori(first, end) as i:
        for (s, per), b in zip(counts, base):
            s.n = i * per + b
        yield i
    for (s, per), b in zip(counts, base):
        s.n = b + end * per


def build(nc, x_prompt, x_sample, state_hgrn, state_ssm, state_conv, hg_lower_bounds, w_in, hg_norm_w, hg_proj,
          conv_w, conv_b, dt_bias, a_log, d_skip, ssd_norm_w, ssd_proj, w_out, ln1_g, ln1_b, router_w,
          router_b, w_gu, b_gu, w_down, b_down, ln2_g, ln2_b,
          y_prompt, y_sample, o_hg_p, o_ssm_p, o_conv_p, o_hg_s, o_ssm_s, o_conv_s, stop=99):
    ctx = ExitStack()
    base = (nc.sbuf_base + 31) // 32 * 32

    def at(name, kb, shape, dt=F32):
        return nc.alloc_sbuf_tensor_at(name, shape, dt, offset=base + int(kb * 1024))

    def S(name):
        return ctx.enter_context(nc.semaphore(name))

    def row(v):
        return v.partition_broadcast(P)

    def product(out, lhs, rhs, rows):
        for k in range(KD):
            if rows == P:
                last = nc.tensor.matmul(out[:], lhs(k), rhs(k), start=(k == 0), stop=(k == KD - 1))
            else:
                for r in range(4):
                    last = nc.tensor.matmul(out[32 * r:32 * r + 32, 0:P], lhs(k), rhs(k)[:, P * r:P * r + P],
                                            start=(k == 0), stop=(k == KD - 1))
        return last

    def pieces(rows):
        if rows == P:
            return ((slice(0, P), slice(0, CW), slice(0, CW)),)
        return tuple((slice(32 * r, 32 * r + 32), slice(0, P), slice(P * r, P * r + P)) for r in range(4))

    with ctx:
        ps = ctx.enter_context(nc.psum_tensor("ps", [P, 8, 512], F32))

        ident = at("ident", 96, [P, P])
        tri = at("tri", 96.5, [P, P])
        ones = at("ones", 97, [P, P])
        smask = at("smask", 97.5, [32, 32])
        sbatch = at("sbatch", 97.625, [32, 32])
        bsel = at("bsel", 97.75, [32, NB])
        cmask = at("cmask", 97.875, [P, CH])
        keep = at("keep", 98, [P, T])
        vecs = at("vecs", 99.25, [P, 160])
        jcol = at("jcol", 100, [P, BLK])
        ecol = at("ecol", 100.25, [P, E_])
        prow = at("prow", 100.5, [P, 1])
        rb = at("rb", 101, [P, E_])
        xtok = at("xtok", 104, [P, 3, D])
        xT = at("xT", 116, [P, KD, T])
        ynT = at("ynT", 125.5, [P, XT_, T])
        onT = at("onT", 144, [P, HH, T])
        ring = [at(f"ring{i}", 16 * i, [P, KD, CW]) for i in range(2)]
        z = at("z", 154, [P, 3, INNER])
        convBC = at("convBC", 178, [P, CT - XT_, T])
        convX = at("convX", 188, [P, XT_, T])
        wconv = vecs[:, 0:CK * CT].rearrange("p (j c) -> p j c", c=CT)
        bconv = vecs[:, CK * CT:CK * CT + CT]
        hgw = vecs[:, 120:128]
        ssdw = vecs[:, 128:144]
        lbv = vecs[:, 144:152]
        w_k = w_in[0].rearrange("(k p) n -> p k n", p=P)

        def chunk_src(c):
            return w_k[:, :, bass.ds(c, CW)]

        xrow = at("xrow", 32, [P, CT, CROW])
        prev = at("prev", 62, [NB * 3, XBC])
        ncol = at("ncol", 74, [P, CT, 27])
        nrows = at("nrows", 80, [27, XBC])
        acc = [at(f"acc{i}", 92 + 1.25 * i, [P, CROW]) for i in range(2)]
        vrows = [at("vrows0", 94.5, [P, P]), at("vrows1", 95, [24, P])]
        wdt = at("wdt", 103, [P, KD, SH])
        dtb = at("dtb", 102, [P, SH])
        dt = at("dt", 101.25, [P, 3, SH])

        s_in = S("x_loaded")
        s_vec = S("vectors_loaded")
        s_prev = S("conv_state_loaded")
        s_wdt = S("dt_weights_loaded")
        s_w = [S(f"chunk_loaded{i}") for i in range(2)]
        s_const = S("constants_ready")
        s_zero = S("xrow_cleared")
        s_xtp = S("xT_transposed")
        s_xte = S("xT_copied")
        s_vt = S("vectors_transposed")
        s_ve = S("vectors_copied")
        s_pt = S("conv_state_transposed")
        s_pe_ = S("conv_state_copied")
        s_mt = S("projection_ready")
        s_me = S("projection_copied")
        s_conv = S("conv_ready")
        s_silu = S("conv_activated")
        s_dtp = S("dt_ready")
        s_dte = S("dt_copied")
        s_nc = S("conv_tail_gathered")
        s_nct = S("conv_tail_transposed")
        s_nce = S("conv_tail_copied")
        s_out = S("outputs_stored")
        dstep, astep, pstep = Steps(S("dve_step")), Steps(S("act_step")), Steps(S("pool_step"))
        stored = 0

        with nc.Block() as block:
            @block.sync
            def _(sp):
                for t in range(2):
                    sp.dma_start(xtok[:, t, :], x_prompt[0, P * t:P * t + P, :]).then_inc(s_in, 16)
                sp.dma_start(xtok[0:32, 2, :], x_sample.rearrange("b s d -> (b s) d")).then_inc(s_in, 16)
                sp.dma_start(ring[0][:], chunk_src(C_X)).then_inc(s_w[0], 16)
                sp.dma_start(ring[1][:], chunk_src(C_X + CW)).then_inc(s_w[1], 16)
                with sp.Fori(1, 3) as i:
                    for n in range(2):
                        sp.wait_ge(s_mt, i * 8 + (4 * n - 4))
                        sp.dma_start(ring[n][:], chunk_src(i * (2 * CW) + (C_X + n * CW))).then_inc(s_w[n], 16)
                for c in range(INNER // CW):
                    sp.wait_ge(s_mt, CT - 4 + 4 * c if c < 2 else CT + 3 * (c - 1))
                    sp.dma_start(ring[c % 2][:], chunk_src(C_Z + c * CW)).then_inc(s_w[c % 2], 16)
                sp.wait_ge(s_nce, 2)
                sp.dma_start(o_conv_p[0, 0], nrows[0:3, :]).then_inc(s_out, 16)
                sp.dma_start(o_conv_s[0].rearrange("b r c -> (b r) c"), nrows[3:27, :]).then_inc(s_out, 16)
                sp.wait_ge(s_out, 32)

            @block.gpsimd
            def _(pool):
                g = nc.gpsimd
                pstep.on(pool)
                g.memset(xrow[:, :, 0:3], 0.0).then_inc(s_zero, 1)
                g.memset(dt[:], 0.0).then_inc(s_zero, 1)
                pstep(g.memset(ones[:], 1.0))
                pstep(g.memset(ident[:], 0.0))
                pstep(g.memset(keep[:], 1.0))
                pstep(g.memset(sbatch[:], 1.0))
                pstep(g.iota(jcol[:], [[1, BLK]], base=0, channel_multiplier=0, allow_small_or_imprecise_dtypes=True))
                pstep(g.iota(ecol[:], [[1, E_]], base=0, channel_multiplier=0, allow_small_or_imprecise_dtypes=True))
                pstep(g.iota(prow[:], [[1, 1]], base=0, channel_multiplier=1, allow_small_or_imprecise_dtypes=True))
                pstep(g.affine_select(out=ident[:], in_=ident[:], compare_op=ALU.not_equal, fill=1.0, base=0,
                                pattern=[[-1, P]], channel_multiplier=1))
                pstep(g.affine_select(out=tri[:], in_=ones[:], compare_op=ALU.is_ge, fill=0.0, base=0,
                                pattern=[[1, P]], channel_multiplier=-1))
                for r in range(4):
                    pstep(g.affine_select(out=cmask[32 * r:32 * r + 32, :], in_=ones[32 * r:32 * r + 32, 0:CH],
                                    compare_op=ALU.is_ge, fill=0.0, base=0, pattern=[[1, CH]],
                                    channel_multiplier=-1))
                pstep(g.memset(keep[:, 0:SEQ].rearrange("p (c s) -> p c s", s=CH)[:, :, 0:1], 0.0))
                pstep(g.memset(keep[:, SEQ:T].rearrange("p (c s) -> p c s", s=NS)[:, :, 0:1], 0.0))
                sb3 = sbatch[:].rearrange("p (b s) -> p b s", s=NS)
                pstep(g.affine_select(out=sb3, in_=sb3, compare_op=ALU.is_ge, fill=0.0, base=0,
                                      pattern=[[-NS, NB], [0, NS]], channel_multiplier=1))
                pstep(g.affine_select(out=sb3, in_=sb3, compare_op=ALU.is_ge, fill=0.0, base=NS - 1,
                                      pattern=[[NS, NB], [0, NS]], channel_multiplier=-1))
                pstep(g.tensor_copy(bsel[:], sb3[:, :, 0]))
                g.tensor_tensor(smask[:], sbatch[:], tri[0:32, 0:32], ALU.mult).then_inc(s_const, 1)

            @block.scalar
            def _(act):
                a = nc.scalar
                vr = vrows[0]
                act.dma_start(vr[0:96, :], conv_w[0].rearrange("j (c p) -> (j c) p", p=P)).then_inc(s_vec, 16)
                act.dma_start(vr[96:120, :], conv_b[0].rearrange("(c p) -> c p", p=P)).then_inc(s_vec, 16)
                act.dma_start(vr[120:128, :], hg_norm_w[0].rearrange("(c p) -> c p", p=P)).then_inc(s_vec, 16)
                act.dma_start(vrows[1][0:16, :], ssd_norm_w[0].rearrange("(c p) -> c p", p=P)).then_inc(s_vec, 16)
                act.dma_start(vrows[1][16:24, :], hg_lower_bounds[0].rearrange("(c p) -> c p", p=P)).then_inc(s_vec, 16)
                act.dma_start(prev[:], state_conv[0].rearrange("b r c -> (b r) c")).then_inc(s_prev, 16)
                act.dma_start(wdt[:], w_k[:, :, C_DT:C_DT + SH]).then_inc(s_wdt, 16)
                act.dma_start(dtb[:], row(dt_bias[0])).then_inc(s_wdt, 16)
                for k in range(KD):
                    act.wait_ge(s_xtp, k + 1)
                    a.copy(xT[:, k, :], ps[:, k % 2, 0:T]).then_inc(s_xte, 1)
                with act.Fori(0, CT // 4) as i:
                    for m in range(4):
                        act.wait_ge(s_mt, i * 4 + (m + 1))
                        a.copy(xrow[:, bass.ds(i * 4 + m, 1), 3:3 + SEQ], ps[:, 4 + m:5 + m, 0:SEQ])
                        a.copy(xrow[:, bass.ds(i * 4 + m, 1), FROW:CROW].rearrange("p c (b s) -> p (c b) s", s=7)[:, :, 3:7],
                               ps[:, 4 + m, SEQ:T].rearrange("p (b s) -> p b s", s=NS)).then_inc(s_me, 1)
                zc = INNER // CW
                for j in range(3 * zc):
                    n, (t, (_, rows)) = j // 3, (j % 3, TILES[j % 3])
                    act.wait_ge(s_mt, CT + j + 1)
                    for pr, pc, cols in pieces(rows):
                        last = a.activation(z[0:rows, t, n * CW:(n + 1) * CW][:, cols], ps[pr, 4 + j % 4, pc], ACT.Silu)
                    last.then_inc(s_me, 1)
                    for c in (2 * j, 2 * j + 1):
                        act.wait_ge(s_conv, c + 1)
                        out = convX[:, c, :] if c < XT_ else convBC[:, c - XT_, :]
                        a.activation(out[:, 0:SEQ], acc[c % 2][:, 0:SEQ], ACT.Silu)
                        a.activation(out[:, SEQ:T].rearrange("p (b s) -> p b s", s=NS),
                                     acc[c % 2][:, FROW:CROW].rearrange("p (b s) -> p b s", s=7)[:, :, 0:NS],
                                     ACT.Silu).then_inc(s_silu, 1)

            @block.vector
            def _(dve):
                v = nc.vector
                dstep.on(dve)
                dve.wait_ge(s_vt, 1)
                v.tensor_copy(vecs[:, 0:152], ps[:, 2, 0:152]).then_inc(s_ve, 1)
                dve.wait_ge(s_zero, 1)
                for h in range(2):
                    dve.wait_ge(s_pt, h + 1)
                    v.tensor_copy(xrow[:, 12 * h:12 * h + 12, FROW:CROW].rearrange("p c (b s) -> p c b s", s=7)[:, :, :, 0:3],
                                  ps[:, h, 0:288].rearrange("p (c b s) -> p c b s", b=NB, s=3)).then_inc(s_pe_, 1)
                dve.wait_ge(s_ve, 1)
                dve.wait_ge(s_pe_, 2)
                def convolve(i, n):
                    dve.wait_ge(s_me, i * 2 + (n + 1))
                    if not isinstance(i, int) or i > 0:
                        dve.wait_ge(s_silu, i * 2 + (n - 1))
                    c = bass.ds(i * 2 + n, 1)
                    o = acc[n][:, 0:CO]
                    tap = [xrow[:, c, j:j + CO].rearrange("p c l -> p (c l)") for j in range(CK)]
                    w = [wconv[:, j, c] for j in range(CK)]
                    dstep(v.tensor_scalar(o, tap[0], w[0], bconv[:, c], ALU.mult, ALU.add))
                    dstep(v.scalar_tensor_tensor(o, tap[1], w[1], o, ALU.mult, ALU.add))
                    dstep(v.scalar_tensor_tensor(o, tap[2], w[2], o, ALU.mult, ALU.add))
                    v.scalar_tensor_tensor(o, tap[3], w[3], o, ALU.mult, ALU.add).then_inc(s_conv, 1)

                convolve(0, 0)
                convolve(0, 1)
                with turns(dve, 1, CT // 2, (dstep, 6)) as i:
                    convolve(i, 0)
                    convolve(i, 1)
                v.tensor_copy(ncol[:, :, 0:3], xrow[:, :, SEQ:FROW]).then_inc(s_nc, 1)
                v.tensor_copy(ncol[:, :, 3:27].rearrange("p c (b s) -> p c b s", s=3),
                              xrow[:, :, FROW:CROW].rearrange("p c (b s) -> p c b s", s=7)[:, :, :, 4:7]).then_inc(s_nc, 1)
                dve.wait_ge(s_dtp, 1)
                dve.wait_ge(s_wdt, 32)
                dve.wait_ge(s_zero, 2)
                for t, (_, rows) in enumerate(TILES):
                    v.tensor_tensor(dt[0:rows, t, :], ps[0:rows, 3, 32 * t:32 * t + 32], dtb[0:rows, :], ALU.add).then_inc(s_dte, 1)
                for h in range(2):
                    dve.wait_ge(s_nct, h + 1)
                    v.tensor_copy(nrows[:, 1536 * h:1536 * h + 1536].rearrange("p (c n) -> p c n", n=512),
                                  ps[0:27, 0:3, :]).then_inc(s_nce, 1)

            @block.tensor
            def _(pe):
                m = nc.tensor
                pe.wait_ge(s_const, 1)
                pe.wait_ge(s_in, 48)
                for k in range(KD):
                    if k >= 2:
                        pe.wait_ge(s_xte, k - 1)
                    for t, (t0, rows) in enumerate(TILES):
                        last = m.transpose(ps[:, k % 2, t0:t0 + rows], xtok[0:rows, t, k * P:(k + 1) * P], ident[0:rows, 0:rows])
                    last.then_inc(s_xtp, 1)
                pe.wait_ge(s_vec, 80)
                m.transpose(ps[:, 2, 0:P], vrows[0][:], ident[:])
                m.transpose(ps[:, 2, P:P + 24], vrows[1][:], ident[0:24, 0:24]).then_inc(s_vt, 1)
                pe.wait_ge(s_prev, 16)
                pe.wait_ge(s_xte, KD)
                for h in range(2):
                    for c in range(12):
                        last = m.transpose(ps[:, h, 24 * c:24 * c + 24], prev[:, (12 * h + c) * P:(12 * h + c + 1) * P], ident[0:24, 0:24])
                    last.then_inc(s_pt, 1)
                pe.wait_ge(s_wdt, 32)
                for t, (t0, rows) in enumerate(TILES):
                    for k in range(KD):
                        last = m.matmul(ps[0:rows, 3, 32 * t:32 * t + 32], xT[:, k, t0:t0 + rows], wdt[:, k, :],
                                        start=(k == 0), stop=(k == KD - 1))
                last.then_inc(s_dtp, 1)

                def columns(i, n):
                    pe.wait_ge(s_w[n], i * 16 + 16)
                    for mt in range(4):
                        if not (isinstance(i, int) and i == 0) or n > 0:
                            pe.wait_ge(s_me, i * 8 + (4 * n + mt - 3))
                        for k in range(KD):
                            last = m.matmul(ps[:, 4 + mt, 0:T], ring[n][:, k, mt * P:(mt + 1) * P], xT[:, k, :],
                                            start=(k == 0), stop=(k == KD - 1))
                        last.then_inc(s_mt, 1)

                columns(0, 0)
                columns(0, 1)
                with pe.Fori(1, CT // 8) as i:
                    columns(i, 0)
                    columns(i, 1)
                for c in range(INNER // CW):
                    n = c % 2
                    pe.wait_ge(s_w[n], 16 * (3 + c // 2 + 1))
                    for t, (t0, rows) in enumerate(TILES):
                        j = 3 * c + t
                        pe.wait_ge(s_me, CT + j - 3)
                        product(ps[:, 4 + j % 4, :], lambda k: xT[:, k, t0:t0 + rows], lambda k: ring[n][:, k, :], rows).then_inc(s_mt, 1)
                pe.wait_ge(s_nc, 2)
                for h in range(2):
                    if h == 1:
                        pe.wait_ge(s_nce, 1)
                    for c in range(12):
                        last = m.transpose(ps[0:27, c // 4, (c % 4) * P:(c % 4 + 1) * P], ncol[:, 12 * h + c, :], ident[:])
                    last.then_inc(s_nct, 1)

        if stop <= 1:
            return
        xtk = at("xtk", 0, [P, 3, INNER])
        xdt = at("xdt", 24, [P, 3, INNER])
        cbm = at("cbm", 48, [P, SG, SC])
        dbuf = [at(f"dbuf{i}", 55 + 1.75 * i, [P, SC]) for i in range(2)]
        wbuf = [at(f"wbuf{i}", 58.5 + 1.75 * i, [P, SC]) for i in range(2)]
        btok = at("btok", 62, [P, 3, SG * SN])
        xw2 = at("xw2", 68, [32, INNER])
        hst = [at(f"hst{i}", 76 + 8 * i, [P, XT_, SN]) for i in range(2)]
        dsk = at("dsk", 92, [P, SH])
        alog = at("alog", 92.125, [P, SH])
        av = at("av", 92.25, [P, 3, SH])
        wd = at("wd", 92.625, [P, 3, SH])
        dtv = at("dtv", 93, [P, 3, SH])
        dta = at("dta", 93.375, [P, 3, SH])
        dtmp = at("dtmp", 93.75, [P, 3, SH])
        dabs = at("dabs", 94.125, [P, 3, SH])
        eA = at("eA", 94.5, [32, SH])
        dec = at("dec", 94.625, [P, XT_ * NB])
        ss = at("ss", 95.125, [P, 3 * SG])
        ats = at("ats", 101.75, [32, T])
        ath = [at(f"ath{i}", 138 + 1.25 * i, [32, T]) for i in range(2)]
        hT = at("hT", 144, [P, XT_, P])
        yis = at("yis", 152, [P, 512])
        bm = [at(f"bm{i}", 125.5 + 2 * i, [32, SG * SN]) for i in range(2)]
        hp = at("hp", 130, [P, XT_, SN])
        sq = at("sq", 141, [P, GW])
        xw = at("xw", 188, [P, 2, INNER])

        q_h = [S(f"state_loaded{i}") for i in range(2)]
        q_par = S("ssd_parameters_loaded")
        q_xp = S("x_transposed")
        q_xa = S("x_copied_act")
        q_xv = S("x_copied_dve")
        q_dt = S("softplus_parts")
        q_dta = S("dta_ready")
        q_dx = S("dta_widened")
        q_A = S("A_ready")
        q_ac = S("A_copied")
        q_dif = S("decay_exponents_ready")
        q_exp = S("decays_ready")
        q_wd = S("state_weights_ready")
        q_xdt = S("xdt_ready")

        with nc.Block() as block:
            @block.sync
            def _(sp):
                sp.dma_start(dsk[:], row(d_skip[0])).then_inc(q_par, 16)
                sp.dma_start(alog[:], row(a_log[0])).then_inc(q_par, 16)
                for n in range(2):
                    sp.dma_start(hst[n][:], state_ssm[0, n].rearrange("h p n -> (h p) n").rearrange("(i q) n -> q i n", q=P)).then_inc(q_h[n], 16)

            @block.gpsimd
            def _(pool):
                g = nc.gpsimd
                pstep.on(pool)
                pstep(g.memset(xdt[:, 2, :], 0.0))
                pool.wait_ge(q_dta, 1)
                g.tensor_copy(xw2[:].rearrange("p (h d) -> p h d", d=SP_),
                              dta[0:32, 2, :].unsqueeze(2).broadcast_to([32, SH, SP_])).then_inc(q_dx, 1)
                for t, (_, rows) in enumerate(TILES):
                    pool.wait_ge(q_xa, 2 * t + 2)
                    pool.wait_ge(q_xv, 2 * t + 2)
                    g.tensor_tensor(xdt[0:rows, t, :].rearrange("p (h d) -> p h d", d=SP_),
                                    xtk[0:rows, t, :].rearrange("p (h d) -> p h d", d=SP_),
                                    dtv[0:rows, t, :].unsqueeze(2).broadcast_to([rows, SH, SP_]), ALU.mult).then_inc(q_xdt, 1)

            def copy_x(eng_copy, j):
                t = j // 4 if j < 12 else j - 12
                rows = TILES[t][1]
                dst = xtk[0:rows, t, (j % 4) * 512:(j % 4 + 1) * 512] if j < 12 else btok[0:rows, t, :]
                return eng_copy(dst, ps[0:rows, j % 4, :])

            @block.scalar
            def _(act):
                a = nc.scalar
                astep.on(act)
                act.wait_ge(q_par, 32)
                a.activation(alog[:], alog[:], ACT.Exp).then_inc(q_dt, 1)
                astep(a.activation(dabs[:], dt[:], ACT.Abs))
                astep(a.activation(dabs[:], dabs[:], ACT.Exp, scale=-1.0))
                a.activation(dabs[:], dabs[:], ACT.Ln, bias=1.0).then_inc(q_dt, 1)
                for j in range(0, 15, 2):
                    act.wait_ge(q_xp, j + 1)
                    copy_x(a.copy, j).then_inc(q_xa, 1)
                act.wait_ge(q_A, 1)
                act.wait_ge(q_ac, 3)
                a.activation(eA[:], av[0:32, 2, :], ACT.Exp)
                a.activation(dec[:], ps[:, 6, 0:XT_ * NB], ACT.Exp)
                a.copy(ats[:], ps[0:32, 5, 0:T])
                act.wait_ge(q_dif, 1)
                a.activation(dtmp[:], dtmp[:], ACT.Exp).then_inc(q_exp, 1)

            @block.vector
            def _(dve):
                v = nc.vector
                dstep.on(dve)
                dstep(v.tensor_scalar(dtv[:], dt[:], 0.0, None, ALU.max))
                dve.wait_ge(q_dt, 2)
                dstep(v.tensor_tensor(dtv[:], dtv[:], dabs[:], ALU.add))
                v.scalar_tensor_tensor(dta[:], dtv[:], -1.0, alog[:].unsqueeze(1).broadcast_to([P, 3, SH]),
                                       ALU.mult, ALU.mult).then_inc(q_dta, 1)
                v.memset(dtmp[:], 0.0)
                v.memset(av[:], 0.0)
                dstep(v.memset(cbm[:, :, 384:SC], 0.0))
                for j in range(1, 15, 2):
                    dve.wait_ge(q_xp, j + 1)
                    copy_x(v.tensor_copy, j).then_inc(q_xv, 1)
                dve.wait_ge(q_A, 1)
                for t, (_, rows) in enumerate(TILES):
                    v.tensor_copy(av[0:rows, t, :], ps[0:rows, 4, 32 * t:32 * t + 32]).then_inc(q_ac, 1)
                dve.wait_ge(q_ac, 3)
                for t, (_, rows) in enumerate(TILES):
                    last = v.tensor_tensor(dtmp[0:rows, t, :], ps[0:rows, 4, 96 + 32 * t:128 + 32 * t], av[0:rows, t, :], ALU.subtract)
                last.then_inc(q_dif, 1)
                dve.wait_ge(q_exp, 1)
                v.tensor_tensor(wd[:], dtmp[:], dtv[:], ALU.mult).then_inc(q_wd, 1)

            @block.tensor
            def _(pe):
                m = nc.tensor
                for j in range(15):
                    t = j // 4 if j < 12 else j - 12
                    t0, rows = TILES[t]
                    if j >= 4:
                        pe.wait_ge(q_xa if j % 2 == 0 else q_xv, (j - 4) // 2 + 1)
                    for c in range(4):
                        src = convX[:, 4 * (j % 4) + c, t0:t0 + rows] if j < 12 else convBC[:, c, t0:t0 + rows]
                        last = m.transpose(ps[0:rows, j % 4, c * P:(c + 1) * P], src, ident[:])
                    last.then_inc(q_xp, 1)
                pe.wait_ge(q_dta, 1)
                d0, d1, d2 = dta[:, 0, :], dta[:, 1, :], dta[0:32, 2, :]
                for o, l, r in ((0, tri, smask), (96, ones, sbatch)):
                    if o == 0:
                        m.matmul(ps[:, 4, 0:32], l[:], d0, start=True, stop=True)
                    else:
                        m.matmul(ps[:, 4, 96:128], ones[:], d0, start=True, stop=False)
                        m.matmul(ps[:, 4, 96:128], ones[:], d1, start=False, stop=True)
                    m.matmul(ps[:, 4, o + 32:o + 64], ones[:], d0, start=True, stop=False)
                    m.matmul(ps[:, 4, o + 32:o + 64], l[:], d1, start=False, stop=True)
                    m.matmul(ps[0:32, 4, o + 64:o + 96], r[:], d2, start=True, stop=True)
                m.matmul(ps[0:32, 5, 0:P], d0, tri[:], start=True, stop=True)
                m.matmul(ps[0:32, 5, P:2 * P], d0, ones[:], start=True, stop=False)
                m.matmul(ps[0:32, 5, P:2 * P], d1, tri[:], start=False, stop=True)
                m.matmul(ps[0:32, 5, 2 * P:T], d2, smask[:], start=True, stop=True)
                pe.wait_ge(q_dx, 1)
                for i in range(XT_):
                    last = m.matmul(ps[:, 6, NB * i:NB * i + NB], xw2[:, P * i:P * i + P], bsel[:], start=True, stop=True)
                last.then_inc(q_A, 1)

        if stop <= 2:
            return
        r_bm = S("masked_B_ready")
        r_tr = S("state_transposed")
        r_tc = S("state_copied")
        r_in = S("state_read_out")
        r_up = S("state_update_ready")
        r_ud = S("state_updated")
        r_dc = S("state_decayed")
        r_st = [S(f"state_stored{i}") for i in range(2)]
        r_yc = S("inter_copied")
        r_yt = S("inter_transposed")
        r_ya = S("inter_added")
        r_w = S("weighted_x_ready")
        r_sk = S("skip_ready")
        r_cb = S("scores_ready")
        r_cm = S("scores_masked")
        r_hp = S("final_state_ready")
        r_hc = S("final_state_copied")
        r_sel = S("head_A_ready")
        r_ab = S("head_A_spread")
        r_d = S("head_exponents_ready")
        r_e = S("head_decays_ready")
        r_W = S("head_weights_ready")
        r_z = S("group_y_gated")
        r_yh = S("head_y_done")

        with nc.Block() as block:
            @block.sync
            def _(sp):
                def rows_of(state, b):
                    return state[0, b].rearrange("h p n -> (h p) n").rearrange("(i q) n -> q i n", q=P)

                for b in range(NB):
                    sp.wait_ge(r_ud, 4 * b + 4)
                    sp.dma_start(rows_of(o_ssm_s, b), hst[b % 2][:]).then_inc(r_st[b % 2], 16)
                    if b + 2 < NB:
                        sp.wait_ge(r_st[b % 2], 16 * (b // 2 + 1))
                        sp.dma_start(hst[b % 2][:], rows_of(state_ssm, b + 2)).then_inc(q_h[b % 2], 16)
                sp.wait_ge(r_hc, 4)
                sp.dma_start(o_ssm_p[0, 0].rearrange("h p n -> (h p) n").rearrange("(i q) n -> q i n", q=P), hp[:]).then_inc(s_out, 16)
                sp.wait_ge(s_out, 32 + 16)
                for n in range(2):
                    sp.wait_ge(r_st[n], 16 * (NB // 2))

            @block.gpsimd
            def _(pool):
                g = nc.gpsimd
                g.tensor_tensor(xw2[:].rearrange("p (h d) -> p h d", d=SP_), xtk[0:32, 2, :].rearrange("p (h d) -> p h d", d=SP_),
                                wd[0:32, 2, :].unsqueeze(2).broadcast_to([32, SH, SP_]), ALU.mult).then_inc(r_w, 1)
                with pool.Fori(0, NB // 2) as i:
                    for n in range(2):
                        pool.wait_ge(r_tr, i * 8 + (4 * n + 4))
                        g.tensor_tensor(hst[n][:], hst[n][:], dec[:].rearrange("p (i b) -> p i b", b=NB)[:, :, bass.ds(i * 2 + n, 1)]
                                        .broadcast_to([P, XT_, SN]), ALU.mult).then_inc(r_dc, 1)
                for t in range(2):
                    g.tensor_tensor(xw[:, t, :].rearrange("p (h d) -> p h d", d=SP_), xtk[:, t, :].rearrange("p (h d) -> p h d", d=SP_),
                                    wd[:, t, :].unsqueeze(2).broadcast_to([P, SH, SP_]), ALU.mult).then_inc(r_w, 1)
                pool.wait_ge(r_w, 3)
                for t, (_, rows) in enumerate(TILES):
                    xv = xtk[0:rows, t, :].rearrange("p (h d) -> p h d", d=SP_)
                    g.tensor_tensor(xv, xv, dsk[0:rows, :].unsqueeze(2).broadcast_to([rows, SH, SP_]), ALU.mult).then_inc(r_sk, 1)

            @block.scalar
            def _(act):
                a = nc.scalar
                astep.on(act)
                with act.Fori(0, NB) as i:
                    for q in range(4):
                        act.wait_ge(r_tr, i * 4 + (q + 1))
                        if q == 0:
                            act.wait_ge(r_in, i)
                        a.copy(hT[:, 4 * q:4 * q + 4, :], ps[:, q % 2, :]).then_inc(r_tc, 1)
                act.wait_ge(r_in, NB)
                a.copy(yis[:], ps[:, 4, :]).then_inc(r_yc, 1)
                for q in range(4):
                    act.wait_ge(r_hp, q + 1)
                    a.copy(hp[:, 4 * q:4 * q + 4, :], ps[:, 5 + q % 2, :]).then_inc(r_hc, 1)

                with turns(act, 0, SG) as i:
                    for n in range(HPG + 1):
                        if n < HPG:
                            act.wait_ge(r_ab, i * HPG + max(n - 1, 0))
                            a.activation(ath[n % 2][:], ats[:], ACT.Identity, scale=ident[0:32, bass.ds(i * HPG + n, 1)]).then_inc(r_sel, 1)
                        if n > 0:
                            act.wait_ge(r_d, i * HPG + n)
                            act.wait_ge(r_yh, i * HPG + max(n - 2, 0))
                            a.activation(wbuf[(n - 1) % 2][:], dbuf[(n - 1) % 2][:], ACT.Exp).then_inc(r_e, 1)
                for g in range(SG):
                    for t, (_, rows) in enumerate(TILES):
                        act.wait_ge(r_z, 3 * g + t + 1)
                        astep(a.activation(sq[0:rows, :], z[0:rows, t, GW * g:GW * g + GW], ACT.Square,
                                           accum_out=ss[0:rows, SG * t + g:SG * t + g + 1]))

            @block.vector
            def _(dve):
                v = nc.vector
                dstep.on(dve)
                v.memset(ss[:], 1.0)
                dstep(v.memset(dbuf[0][:], 0.0))
                dstep(v.memset(dbuf[1][:], 0.0))
                with turns(dve, 0, NB // 2) as i:
                    for n in range(2):
                        dve.wait_ge(r_up, i * 8 + (4 * n if n == 0 else 0))
                        v.tensor_scalar(bm[n][:], btok[0:32, 2, :], bsel[:, bass.ds(i * 2 + n, 1)], None, ALU.mult).then_inc(r_bm, 1)
                    for n in range(2):
                        dve.wait_ge(r_dc, i * 2 + (n + 1))
                        for q in range(4):
                            dve.wait_ge(r_up, i * 8 + (4 * n + q + 1))
                            hq = hst[n][:, 4 * q:4 * q + 4, :].rearrange("p i n -> p (i n)")
                            v.tensor_tensor(hq, hq, ps[:, 2 + q % 2, :], ALU.add).then_inc(r_ud, 1)
                for g in range(SG):
                    dve.wait_ge(r_cb, g + 1)
                    b = ps[:, 6 + g % 2, :]
                    v.tensor_tensor(cbm[:, g, 0:P], b[:, 0:P], tri[:], ALU.mult)
                    v.tensor_copy(cbm[:, g, P:2 * P], b[:, P:2 * P])
                    v.tensor_tensor(cbm[:, g, 2 * P:3 * P], b[:, 2 * P:3 * P], tri[:], ALU.mult)
                    v.tensor_tensor(cbm[0:32, g, 3 * P:SC], b[0:32, 3 * P:SC], smask[:], ALU.mult).then_inc(r_cm, 1)
                dve.wait_ge(r_cm, SG)
                dve.wait_ge(r_sk, 3)
                for q in range(4):
                    dve.wait_ge(r_yt, q + 1)
                    if q > 0:
                        dve.wait_ge(r_ya, q)
                    dstep(v.tensor_tensor(sq[0:32, :].rearrange("p (h d) -> p h d", d=SP_), ps[0:32, q, :].rearrange("p (h d) -> p h d", d=SP_),
                                          eA[:, HPG * q:HPG * q + HPG].unsqueeze(2).broadcast_to([32, HPG, SP_]), ALU.mult))
                    xq = xtk[0:32, 2, 512 * q:512 * q + 512]
                    v.tensor_tensor(xq, xq, sq[0:32, :], ALU.add).then_inc(r_ya, 1)
                dve.wait_ge(r_ya, 4)
                with turns(dve, 0, SG, (dstep, 3)) as i:
                    for n in range(HPG + 1):
                        if n < HPG:
                            d, b = dbuf[n % 2], ps[:, n % 2, :]
                            h = bass.ds(i * HPG + n, 1)
                            dve.wait_ge(r_ab, i * HPG + (n + 1))
                            dve.wait_ge(r_W, i * HPG + max(n - 1, 0))
                            v.tensor_scalar(d[:, 0:2 * P], b[:, 0:2 * P], av[:, 0, h], 0.0, ALU.subtract, ALU.min)
                            v.tensor_scalar(d[:, 2 * P:3 * P], b[:, P:2 * P], av[:, 1, h], 0.0, ALU.subtract, ALU.min)
                            v.tensor_scalar(d[0:32, 3 * P:SC], b[0:32, 2 * P:T], av[0:32, 2, h], 0.0, ALU.subtract, ALU.min).then_inc(r_d, 1)
                        if n > 0:
                            dve.wait_ge(r_e, i * HPG + n)
                            v.tensor_tensor(wbuf[(n - 1) % 2][:], wbuf[(n - 1) % 2][:], cbm[:, bass.ds(i, 1), :].rearrange("p g s -> p (g s)"),
                                            ALU.mult).then_inc(r_W, 1)
                    dve.wait_ge(r_yh, i * HPG + HPG)
                    for t, (_, rows) in enumerate(TILES):
                        cols = bass.ds(i * GW, GW)
                        dstep(v.tensor_tensor(xtk[0:rows, t, cols], xtk[0:rows, t, cols], ps[0:rows, 2 + t, :], ALU.add))
                        v.tensor_tensor(z[0:rows, t, cols], z[0:rows, t, cols], xtk[0:rows, t, cols], ALU.mult).then_inc(r_z, 1)

            @block.tensor
            def _(pe):
                m = nc.tensor
                pe.wait_ge(r_w, 1)
                with pe.Fori(0, NB // 2) as i:
                    for n in range(2):
                        b = i * 2 + n
                        pe.wait_ge(q_h[n], i * 16 + 16)
                        for q in range(4):
                            pe.wait_ge(r_tc, i * 8 + max(4 * n + q - 1, 0))
                            for c in range(4):
                                last = m.transpose(ps[:, q % 2, c * P:(c + 1) * P], hst[n][:, 4 * q + c, :], ident[:])
                            last.then_inc(r_tr, 1)
                        pe.wait_ge(r_tc, i * 8 + (4 * n + 4))
                        for c in range(XT_):
                            last = m.matmul(ps[:, 4, bass.ds(i * 8 + (32 * c + 4 * n), NS)], hT[:, c, :],
                                            convBC[:, SG + c // 4, bass.ds(i * 8 + (SEQ + 4 * n), NS)], start=True, stop=True)
                        last.then_inc(r_in, 1)
                        pe.wait_ge(r_bm, i * 2 + (n + 1))
                        for q in range(4):
                            pe.wait_ge(r_ud, i * 8 + max(4 * n + q - 1, 0))
                            for c in range(4):
                                last = m.matmul(ps[:, 2 + q % 2, c * P:(c + 1) * P], xw2[:, (4 * q + c) * P:(4 * q + c + 1) * P],
                                                bm[n][:, q * SN:(q + 1) * SN], start=True, stop=True)
                            last.then_inc(r_up, 1)
                for g in range(SG):
                    bT, cT, b = convBC[:, g, :], convBC[:, SG + g, :], 6 + g % 2
                    if g >= 2:
                        pe.wait_ge(r_cm, g - 1)
                    m.matmul(ps[:, b, 0:2 * P], bT[:, 0:P], cT[:, 0:2 * P], start=True, stop=True)
                    m.matmul(ps[:, b, 2 * P:3 * P], bT[:, P:2 * P], cT[:, P:2 * P], start=True, stop=True)
                    m.matmul(ps[0:32, b, 3 * P:SC], bT[:, 2 * P:T], cT[:, 2 * P:T], start=True, stop=True).then_inc(r_cb, 1)
                pe.wait_ge(r_yc, 1)
                for q in range(4):
                    for c in range(4):
                        k = 4 * q + c
                        last = m.transpose(ps[0:32, q, c * P:(c + 1) * P], yis[:, 32 * k:32 * k + 32], ident[:])
                    last.then_inc(r_yt, 1)
                pe.wait_ge(r_w, 3)
                pe.wait_ge(r_cm, SG)
                for q in range(4):
                    if q >= 2:
                        pe.wait_ge(r_hc, q - 1)
                    for c in range(4):
                        k = 4 * q + c
                        for t in range(2):
                            last = m.matmul(ps[:, 5 + q % 2, c * P:(c + 1) * P], xw[:, t, k * P:(k + 1) * P],
                                            btok[:, t, q * SN:(q + 1) * SN], start=(t == 0), stop=(t == 1))
                    last.then_inc(r_hp, 1)
                pe.wait_ge(r_ya, 4)

                with pe.Fori(0, SG) as i:
                    for n in range(HPG + 2):
                        if n < HPG:
                            pe.wait_ge(r_sel, i * HPG + (n + 1))
                            pe.wait_ge(r_d, i * HPG + max(n - 1, 0))
                            m.matmul(ps[:, n % 2, 0:T], ones[0:32, :], ath[n % 2][:], start=True, stop=True).then_inc(r_ab, 1)
                        if n >= 2:
                            h = n - 2
                            if h == 0:
                                pe.wait_ge(r_z, i * 3)
                            pe.wait_ge(r_W, i * HPG + (h + 1))
                            w, cols = wbuf[h % 2], slice(SP_ * h, SP_ * h + SP_)
                            x = [xdt[:, t, bass.ds(i * GW + SP_ * h, SP_)] for t in range(3)]
                            m.matmul(ps[:, 2, cols], w[:, 0:P], x[0], start=True, stop=True)
                            m.matmul(ps[:, 3, cols], w[:, P:2 * P], x[0], start=True, stop=False)
                            m.matmul(ps[:, 3, cols], w[:, 2 * P:3 * P], x[1], start=False, stop=True)
                            m.matmul(ps[0:32, 4, cols], w[:, 3 * P:SC], x[2], start=True, stop=True).then_inc(r_yh, 1)

        n_rs = S("group_rms_ready")
        n_sq = S("group_rms_rooted")
        n_y = S("y_normalised")
        n_t = S("y_transposed")
        n_c = S("y_copied")
        with nc.Block() as block:
            @block.scalar
            def _(act):
                act.wait_ge(n_rs, 1)
                nc.scalar.activation(ss[:], ss[:], ACT.Sqrt).then_inc(n_sq, 1)
                for c in range(XT_):
                    act.wait_ge(n_t, c + 1)
                    nc.scalar.activation(ynT[:, c, :], ps[:, c % 4, 0:T], ACT.Copy, scale=ssdw[:, c:c + 1]).then_inc(n_c, 1)

            @block.vector
            def _(dve):
                v = nc.vector
                dstep.on(dve)
                v.tensor_scalar(ss[:], ss[:], 1.0 / GW, RMS_EPS, ALU.mult, ALU.add).then_inc(n_rs, 1)
                dve.wait_ge(n_sq, 1)
                dstep(v.reciprocal(ss[:], ss[:]))
                for g in range(SG):
                    for t, (_, rows) in enumerate(TILES):
                        y = z[0:rows, t, GW * g:GW * g + GW]
                        v.tensor_scalar(y, y, ss[0:rows, SG * t + g:SG * t + g + 1], None, ALU.mult).then_inc(n_y, 1)

            @block.tensor
            def _(pe):
                for c in range(XT_):
                    pe.wait_ge(n_y, 3 * (c // 4 + 1))
                    if c >= 4:
                        pe.wait_ge(n_c, c - 3)
                    for t, (t0, rows) in enumerate(TILES):
                        last = nc.tensor.transpose(ps[:, c % 4, t0:t0 + rows], z[0:rows, t, c * P:(c + 1) * P], ident[0:rows, 0:rows])
                    last.then_inc(n_t, 1)

        if stop <= 3:
            return
        qT = at("qT", 32, [P, HH, T])
        kT = at("kT", 41.5, [P, HH, T])
        bT = at("bT", 51, [P, HH, T])
        eT = at("eT", 60.5, [P, HH, T])
        vtok = at("vtok", 70, [P, 3, D])
        gtok = at("gtok", 82, [P, 3, D])
        otok = at("otok", 0, [P, 3, D])
        U = [at(f"U{i}", 12 + 4 * i, [P, HH, P]) for i in range(2)]
        vm = [at(f"vm{i}", 20 + 4 * i, [32, NB, P]) for i in range(2)]
        scm = at("scm", 28, [P, 3, HH * CH])
        oiT = at("oiT", 31, [P, HH * 32])
        Sb = at("Sb", 154, [P, NB, HH, P])
        kpt = at("kpt", 186, [P, 3, D])
        mid = at("mid", 198, [P, HH, 16])
        lst = at("lst", 198.5, [P, HH, 16])
        dl = at("dl", 199, [P, HH, 16])
        gate = at("gate", 199.5, [P, HH, 8])
        qs = at("qs", 200, [P, HH, 32])
        lb4 = at("lb4", 201, [P, 4, HH])
        hss = at("hss", 201.25, [P, 3 * HH])
        sq3 = at("sq3", 202, [P, D])

        w_z = 16 * ((XBC + INNER) // CW // 2)
        h_S = S("hg_state_loaded")
        h_p = S("hg_projection_ready")
        h_c = S("hg_projection_copied")
        h_lb = S("lower_bound_step")
        h_f = S("forget_gate_ready")
        h_ln = S("log_gate_ready")
        h_ek = S("k_exponents_ready")
        h_eq = S("q_exponents_ready")
        h_x = S("hg_exponentials_ready")
        h_xe = S("hg_factor_exponents_ready")
        h_k = S("kq_weighted")
        h_kt = S("k_transposed")
        h_kc = S("k_copied")
        h_sc = S("hg_scores_ready")
        h_sm = S("hg_scores_masked")
        h_P = S("chunk_sum_ready")
        h_U = S("state_carried")
        h_o = S("o_ready")
        h_oc = S("o_copied")
        h_oi = S("sample_inter_ready")
        h_oic = S("sample_inter_copied")
        h_vm = S("masked_v_ready")
        h_sd = S("sample_state_decayed")
        h_su = S("sample_sum_ready")
        h_sa = S("sample_state_updated")
        h_n = S("o_normalised")
        h_nt = S("o_transposed")
        h_nc = S("o_transposed_copied")
        NPROJ = 2 * HH + 12

        def chunks32(x):
            return x[:, :, 0:SEQ].rearrange("p h (c s) -> p h c s", s=CH)

        def chunks4(x):
            return x[:, :, SEQ:T].rearrange("p h (c s) -> p h c s", s=NS)

        with nc.Block() as block:
            @block.sync
            def _(sp):
                for n in range(2):
                    sp.dma_start(ring[n][:], chunk_src(C_Q + n * CW)).then_inc(s_w[n], 16)
                for b in range(NB):
                    sp.dma_start(Sb[:, b], state_hgrn[0, b].rearrange("h k v -> k h v")).then_inc(h_S, 16)
                for c in range(2, 8):
                    sp.wait_ge(h_p, 4 * (c - 1) if c <= 5 else 16 + 3 * (c - 5))
                    sp.dma_start(ring[c % 2][:], chunk_src(C_Q + c * CW)).then_inc(s_w[c % 2], 16)
                sp.wait_ge(h_U, 8)
                sp.dma_start(o_hg_p[0, 0].rearrange("h k v -> k h v"), U[0][:]).then_inc(s_out, 16)
                sp.wait_ge(h_sa, 2 * HH)
                for b in range(NB):
                    sp.dma_start(o_hg_s[0, b].rearrange("h k v -> k h v"), Sb[:, b]).then_inc(s_out, 16)
                sp.wait_ge(s_out, 48 + 16 * (NB + 1))

            @block.gpsimd
            def _(pool):
                g = nc.gpsimd
                pool.wait_ge(h_c, NPROJ)
                for h in range(HH):
                    if h >= 2:
                        pool.wait_ge(h_su, 2 * (h - 1))
                    g.tensor_tensor(vm[h % 2][:], vtok[0:32, 2, h * P:(h + 1) * P].unsqueeze(1).broadcast_to([32, NB, P]),
                                    bsel[:].unsqueeze(2).broadcast_to([32, NB, P]), ALU.mult).then_inc(h_vm, 1)
                    if h == 0:
                        pool.wait_ge(h_oi, 1)
                        pool.wait_ge(h_x, 5)
                    s = Sb[:, :, h, :]
                    g.tensor_tensor(s, s, lst[:, h, 8:16].unsqueeze(2).broadcast_to([P, NB, P]), ALU.mult).then_inc(h_sd, 1)

            @block.scalar
            def _(act):
                a = nc.scalar
                astep.on(act)
                act.wait_ge(h_lb, 1)
                a.activation(lb4[:, 1, :], lb4[:, 0, :], ACT.Exp).then_inc(h_lb, 1)
                with act.Fori(0, 2) as i:
                    for n in range(4):
                        act.wait_ge(h_p, i * 4 + (n + 1))
                        a.activation(qT[:, bass.ds(i * 4 + n, 1), :], ps[:, 4 + n:5 + n, 0:T], ACT.Silu).then_inc(h_c, 1)
                with act.Fori(0, 2) as i:
                    for n in range(4):
                        act.wait_ge(h_p, i * 4 + (HH + n + 1))
                        a.activation(eT[:, bass.ds(i * 4 + n, 1), :], ps[:, 4 + n:5 + n, 0:T], ACT.Sigmoid).then_inc(h_c, 1)
                act.wait_ge(h_f, 1)
                a.activation(bT[:], eT[:], ACT.Ln).then_inc(h_ln, 1)
                for j in range(6):
                    t, rows = j % 3, TILES[j % 3][1]
                    act.wait_ge(h_p, 2 * HH + j + 1)
                    for pr, pc, cols in pieces(rows):
                        last = a.copy(vtok[0:rows, t, CW * (j // 3):CW * (j // 3) + CW][:, cols], ps[pr, 4 + j % 4, pc])
                    last.then_inc(h_c, 1)
                act.wait_ge(h_ek, 1)
                a.activation(eT[:], eT[:], ACT.Exp).then_inc(h_x, 1)
                act.wait_ge(h_eq, 1)
                a.activation(bT[:], bT[:], ACT.Exp).then_inc(h_x, 1)
                act.wait_ge(h_xe, 2)
                a.activation(mid[:], mid[:], ACT.Exp).then_inc(h_x, 1)
                a.activation(gate[:], gate[:], ACT.Exp).then_inc(h_x, 1)
                a.activation(lst[:], lst[:], ACT.Exp).then_inc(h_x, 1)
                a.activation(dl[:], dl[:], ACT.Exp).then_inc(h_x, 1)
                for j in range(6, 12):
                    t, rows = j % 3, TILES[j % 3][1]
                    act.wait_ge(h_p, 2 * HH + j + 1)
                    for pr, pc, cols in pieces(rows):
                        last = a.activation(gtok[0:rows, t, CW * (j // 3 - 2):CW * (j // 3 - 1)][:, cols], ps[pr, 4 + j % 4, pc], ACT.Sigmoid)
                    last.then_inc(h_c, 1)
                for j in range(6):
                    rows = TILES[j // 2][1]
                    act.wait_ge(h_kt, j + 1)
                    a.copy(kpt[0:rows, j // 2, 512 * (j % 2):512 * (j % 2) + 512], ps[0:rows, j % 4, :]).then_inc(h_kc, 1)
                act.wait_ge(h_oi, 1)
                a.copy(oiT[:], ps[:, 4, 0:256]).then_inc(h_oic, 1)
                for t in range(3):
                    rows = TILES[t][1]
                    act.wait_ge(h_o, (4, 8, 9)[t])
                    a.copy(otok[0:rows, t, :].rearrange("p (b n) -> p b n", b=2), ps[0:rows, 6:8, :]).then_inc(h_oc, 1)
                act.wait_ge(n_rs, 2)
                a.activation(hss[:], hss[:], ACT.Sqrt).then_inc(n_sq, 1)
                for h in range(HH):
                    act.wait_ge(h_nt, h + 1)
                    a.activation(onT[:, h, :], ps[:, h % 2, 0:T], ACT.Copy, scale=hgw[:, h:h + 1]).then_inc(h_nc, 1)

            @block.vector
            def _(dve):
                v = nc.vector
                dstep.on(dve)
                v.tensor_tensor(lb4[:, 0, :], lbv, lbv, ALU.subtract).then_inc(h_lb, 1)
                dve.wait_ge(h_lb, 2)
                dstep(v.reciprocal(lb4[:, 2, :], lb4[:, 1, :]))
                dstep(v.tensor_tensor(lb4[:, 3, :], lb4[:, 1, :], lb4[:, 2, :], ALU.mult))
                dstep(v.tensor_tensor(lb4[:, 0, :], lb4[:, 3, :], lb4[:, 3, :], ALU.subtract))
                dstep(v.tensor_scalar(lb4[:, 1, :], lb4[:, 0, :], -1.0, 1.0, ALU.mult, ALU.add))
                for h in range(HH):
                    dve.wait_ge(h_c, HH + h + 1)
                    dstep(v.tensor_scalar(eT[:, h, :], eT[:, h, :], lb4[:, 1, h:h + 1], lb4[:, 0, h:h + 1], ALU.mult, ALU.add))
                dstep(v.tensor_scalar(kT[:], eT[:], -1.0, 1.0, ALU.mult, ALU.add))
                v.tensor_scalar(eT[:], eT[:], FMIN, None, ALU.max).then_inc(h_f, 1)
                dve.wait_ge(h_ln, 1)
                for h in range(HH):
                    last = v.tensor_tensor_scan(eT[:, h, :], keep[:], bT[:, h, :], 0.0, ALU.mult, ALU.add)
                dstep(last)
                for x, at32, at4 in ((mid, CH // 2 - 1, 1), (lst, CH - 1, NS - 1)):
                    dstep(v.tensor_copy(x[:, :, 0:8].unsqueeze(3), chunks32(eT)[:, :, :, at32:at32 + 1]))
                    dstep(v.tensor_copy(x[:, :, 8:16].unsqueeze(3), chunks4(eT)[:, :, :, at4:at4 + 1]))
                dstep(v.tensor_tensor(chunks32(bT), chunks32(eT), mid[:, :, 0:8].unsqueeze(3).broadcast_to([P, HH, 8, CH]), ALU.subtract))
                dstep(v.tensor_tensor(chunks4(bT), chunks4(eT), mid[:, :, 8:16].unsqueeze(3).broadcast_to([P, HH, 8, NS]), ALU.subtract))
                v.tensor_scalar(eT[:], bT[:], -1.0, EXPMAX, ALU.mult, ALU.min).then_inc(h_ek, 1)
                dve.wait_ge(h_ek, 1)
                v.tensor_scalar(bT[:], bT[:], EXPMAX, None, ALU.min).then_inc(h_eq, 1)
                dstep(v.tensor_tensor(dl[:], lst[:], mid[:], ALU.subtract))
                v.tensor_tensor(gate[:, :, 0:7], dl[:, :, 0:7], mid[:, :, 1:8], ALU.add).then_inc(h_xe, 1)
                v.tensor_copy(gate[:, :, 7:8], dl[:, :, 7:8]).then_inc(h_xe, 1)
                dstep(v.memset(hss[:], 1.0))
                dve.wait_ge(h_x, 1)
                v.tensor_tensor(kT[:], kT[:], eT[:], ALU.mult).then_inc(h_k, 1)
                dve.wait_ge(h_x, 2)
                v.tensor_tensor(qT[:], qT[:], bT[:], ALU.mult).then_inc(h_k, 1)
                dve.wait_ge(h_x, 6)
                dve.wait_ge(h_k, 2)
                v.tensor_tensor(qs[:].rearrange("p h (c s) -> p h c s", s=NS), chunks4(qT), mid[:, :, 8:16].unsqueeze(3)
                                .broadcast_to([P, HH, 8, NS]), ALU.mult).then_inc(h_k, 1)
                v.tensor_tensor(chunks4(eT), chunks4(kT), dl[:, :, 8:16].unsqueeze(3).broadcast_to([P, HH, 8, NS]), ALU.mult).then_inc(h_k, 1)
                dve.wait_ge(h_c, NPROJ)
                dstep(v.memset(U[0][:], 0.0))
                for t in range(2):
                    dve.wait_ge(h_sc, t + 1)
                    v.tensor_tensor(scm[:, t, :].rearrange("p (h s) -> p h s", s=CH), ps[:, 4 + t, 0:256].rearrange("p (h s) -> p h s", s=CH),
                                    cmask[:].unsqueeze(1).broadcast_to([P, HH, CH]), ALU.mult).then_inc(h_sm, 1)
                dve.wait_ge(h_sc, 3)
                v.tensor_tensor(scm[0:32, 2, :].rearrange("p (h s) -> p h s", s=CH), ps[0:32, 5, 256:512].rearrange("p (h s) -> p h s", s=CH),
                                smask[:].unsqueeze(1).broadcast_to([32, HH, CH]), ALU.mult).then_inc(h_sm, 1)
                for c in range(8):
                    dve.wait_ge(h_P, c + 1)
                    if c >= 1:
                        dve.wait_ge(h_o, c)
                    b0, o, n = 2 * (c % 2), U[c % 2], U[(c + 1) % 2]
                    dstep(v.tensor_tensor(n[:].rearrange("p (b h) v -> p b (h v)", b=2), o[:].rearrange("p (b h) v -> p b (h v)", b=2),
                                          ps[:, b0:b0 + 2, :], ALU.add))
                    v.tensor_tensor(n[:], n[:], gate[:, :, c:c + 1].broadcast_to([P, HH, P]), ALU.mult).then_inc(h_U, 1)
                    dve.wait_ge(h_U, c + 1)
                for j in range(2 * HH):
                    h, half = j // 2, j % 2
                    dve.wait_ge(h_su, j + 1)
                    dve.wait_ge(h_sd, h + 1)
                    s = Sb[:, 4 * half:4 * half + 4, h, :]
                    v.tensor_tensor(s, s, ps[:, j % 4, :].rearrange("p (b v) -> p b v", b=4), ALU.add).then_inc(h_sa, 1)
                for t, (_, rows) in enumerate(TILES):
                    dve.wait_ge(h_oc, t + 1)
                    o = otok[0:rows, t, :]
                    dstep(v.tensor_tensor(sq3[0:rows, :], o, o, ALU.mult))
                    dstep(v.tensor_reduce(hss[0:rows, HH * t:HH * t + HH], sq3[0:rows, :].rearrange("p (h v) -> p h v", v=P), AX_X, ALU.add))
                v.tensor_scalar(hss[:], hss[:], 1.0 / P, RMS_EPS, ALU.mult, ALU.add).then_inc(n_rs, 1)
                dve.wait_ge(n_sq, 2)
                dstep(v.reciprocal(hss[:], hss[:]))
                for t, (_, rows) in enumerate(TILES):
                    o = otok[0:rows, t, :].rearrange("p (h v) -> p h v", v=P)
                    dstep(v.tensor_tensor(o, o, hss[0:rows, HH * t:HH * t + HH].unsqueeze(2).broadcast_to([rows, HH, P]), ALU.mult))
                    v.tensor_tensor(otok[0:rows, t, :], otok[0:rows, t, :], gtok[0:rows, t, :], ALU.mult).then_inc(h_n, 1)

            @block.tensor
            def _(pe):
                m = nc.tensor

                def columns(i, n):
                    pe.wait_ge(s_w[n], i * 16 + (w_z + 16))
                    for mt in range(4):
                        if not (isinstance(i, int) and i == 0) or n > 0:
                            pe.wait_ge(h_c, i * 8 + (4 * n + mt - 3))
                        for k in range(KD):
                            last = m.matmul(ps[:, 4 + mt, 0:T], ring[n][:, k, mt * P:(mt + 1) * P], xT[:, k, :],
                                            start=(k == 0), stop=(k == KD - 1))
                        last.then_inc(h_p, 1)

                columns(0, 0)
                columns(0, 1)
                columns(1, 0)
                columns(1, 1)
                for c in range(4):
                    n = c % 2
                    pe.wait_ge(s_w[n], w_z + 16 * (c // 2 + 3))
                    for t, (t0, rows) in enumerate(TILES):
                        j = 3 * c + t
                        pe.wait_ge(h_c, 2 * HH + j - 3)
                        product(ps[:, 4 + j % 4, :], lambda k: xT[:, k, t0:t0 + rows], lambda k: ring[n][:, k, :], rows).then_inc(h_p, 1)
                pe.wait_ge(h_k, 4)
                for j in range(6):
                    t0, rows = TILES[j // 2]
                    if j >= 4:
                        pe.wait_ge(h_kc, j - 3)
                    for c in range(4):
                        src = (kT if j < 4 else eT)[:, 4 * (j % 2) + c, t0:t0 + rows]
                        last = m.transpose(ps[0:rows, j % 4, c * P:(c + 1) * P], src, ident[:])
                    last.then_inc(h_kt, 1)
                pe.wait_ge(h_c, NPROJ)
                for t in range(2):
                    for h in range(HH):
                        for r in range(4):
                            s = slice(P * t + CH * r, P * t + CH * r + CH)
                            last = m.matmul(ps[CH * r:CH * r + CH, 4 + t, CH * h:CH * h + CH], kT[:, h, s], qT[:, h, s], start=True, stop=True)
                    last.then_inc(h_sc, 1)
                pe.wait_ge(h_sm, 2)
                for h in range(HH):
                    last = m.matmul(ps[0:32, 5, 256 + 32 * h:288 + 32 * h], kT[:, h, SEQ:T], qT[:, h, SEQ:T], start=True, stop=True)
                last.then_inc(h_sc, 1)
                pe.wait_ge(h_S, 16 * NB)
                for h in range(HH):
                    for b in range(NB):
                        last = m.matmul(ps[:, 4, 32 * h + NS * b:32 * h + NS * b + NS], Sb[:, b, h, :], qs[:, h, NS * b:NS * b + NS], start=True, stop=True)
                last.then_inc(h_oi, 1)

                def chunk_sum(c):
                    r = slice(CH * (c % 4), CH * (c % 4) + CH)
                    if c >= 2:
                        pe.wait_ge(h_U, c - 1)
                    for h in range(HH):
                        last = m.matmul(ps[:, 2 * (c % 2) + h // 4, (h % 4) * P:(h % 4 + 1) * P], kpt[r, c // 4, h * P:(h + 1) * P],
                                        vtok[r, c // 4, h * P:(h + 1) * P], start=True, stop=True)
                    last.then_inc(h_P, 1)

                pe.wait_ge(h_kc, 6)
                chunk_sum(0)
                pe.wait_ge(h_sm, 3)
                for c in range(8):
                    if c + 1 < 8:
                        chunk_sum(c + 1)
                    t, r = c // 4, slice(CH * (c % 4), CH * (c % 4) + CH)
                    if c == 4:
                        pe.wait_ge(h_oc, 1)
                    if c > 0:
                        pe.wait_ge(h_U, c)
                    for h in range(HH):
                        o = ps[r, 6 + h // 4, (h % 4) * P:(h % 4 + 1) * P]
                        last = m.matmul(o, scm[r, t, CH * h:CH * h + CH], vtok[r, t, h * P:(h + 1) * P], start=True, stop=(c == 0),
                                        tile_position=(CH * (c % 4), CH * (c % 4)))
                        if c > 0:
                            last = m.matmul(o, qT[:, h, CH * c:CH * c + CH], U[c % 2][:, h, :], start=False, stop=True)
                    last.then_inc(h_o, 1)
                pe.wait_ge(h_oc, 2)
                pe.wait_ge(h_oic, 1)
                for h in range(HH):
                    o = ps[0:32, 6 + h // 4, (h % 4) * P:(h % 4 + 1) * P]
                    m.matmul(o, scm[0:32, 2, 32 * h:32 * h + 32], vtok[0:32, 2, h * P:(h + 1) * P], start=True, stop=False)
                    last = m.matmul(o, oiT[:, 32 * h:32 * h + 32], ident[:], start=False, stop=True)
                last.then_inc(h_o, 1)
                pe.wait_ge(h_U, 8)
                for j in range(2 * HH):
                    h, half = j // 2, j % 2
                    if j >= 4:
                        pe.wait_ge(h_sa, j - 3)
                    pe.wait_ge(h_vm, h + 1)
                    m.matmul(ps[:, j % 4, :], kpt[0:32, 2, h * P:(h + 1) * P], vm[h % 2][:, 4 * half:4 * half + 4, :].rearrange("p b v -> p (b v)"),
                             start=True, stop=True).then_inc(h_su, 1)
                pe.wait_ge(h_sa, 2 * HH)
                for h in range(HH):
                    if h >= 2:
                        pe.wait_ge(h_nc, h - 1)
                    for t, (t0, rows) in enumerate(TILES):
                        pe.wait_ge(h_n, t + 1)
                        last = m.transpose(ps[:, h % 2, t0:t0 + rows], otok[0:rows, t, h * P:(h + 1) * P], ident[0:rows, 0:rows])
                    last.then_inc(h_nt, 1)

        if stop <= 4:
            return
        wSSD = at("wSSD", 32, [P, XT_, D])
        wHG = at("wHG", 154, [P, KD, D])
        wOUT = at("wOUT", 0, [P, KD, D])
        gA = at("gA", 186, [P, KD, T])
        gB = at("gB", 195.25, [P, KD, T])
        mT = at("mT", 116, [P, KD, T])
        tmpA = [at(f"tmpA{i}", 204.5 + 1.25 * i, [P, T]) for i in range(2)]
        lnw = at("lnw", 125.5, [P, D])
        lnb = at("lnb", 129.5, [P, D])
        lnq = at("lnq", 133.5, [P, D])
        lst4 = at("lst4", 137.5, [P, 3, 8])
        lmu = at("lmu", 137.625, [P, 3])
        lvar = at("lvar", 137.75, [P, 3])

        w_g = w_z + 16 * (4 * D // CW // 2)
        g_ws, g_wh, g_wo, g_ln = S("ssd_proj_loaded"), S("hg_proj_loaded"), S("w_out_loaded"), S("ln_loaded")
        g_p, g_c = S("output_gate_ready"), S("output_gate_copied")
        g_ab, g_m = S("branches_ready"), S("merged_ready")
        g_mx, g_x = S("mix_ready"), S("residual_added")
        ln_c, ln_v, ln_r, ln_s = S("ln_centred"), S("ln_squares_ready"), S("ln_variance_ready"), S("ln_rooted")
        ln_done = S("ln_done")

        def ln_vector(dve, dstep, n):
            v = nc.vector
            dstep(v.tensor_reduce(lmu[:], lst4[:], AX_X, ALU.add))
            dstep(v.tensor_scalar(lmu[:], lmu[:], 1.0 / D, None, ALU.mult))
            for t, (_, rows) in enumerate(TILES):
                x = xtok[0:rows, t, :]
                v.tensor_scalar(x, x, lmu[0:rows, t:t + 1], None, ALU.subtract).then_inc(ln_c, 1)
            dve.wait_ge(ln_v, 3 * n)
            v.tensor_scalar(lvar[:], lvar[:], 1.0 / D, LN_EPS, ALU.mult, ALU.add).then_inc(ln_r, 1)
            dve.wait_ge(ln_s, n)
            dstep(v.reciprocal(lvar[:], lvar[:]))
            dve.wait_ge(ln_c, 3 * n)
            for t, (_, rows) in enumerate(TILES):
                x = xtok[0:rows, t, :]
                dstep(v.scalar_tensor_tensor(x, x, lvar[0:rows, t:t + 1], lnw[0:rows, :], ALU.mult, ALU.mult))
                v.tensor_tensor(x, x, lnb[0:rows, :], ALU.add).then_inc(ln_done, 1)

        def ln_scalar(act, n):
            for t, (_, rows) in enumerate(TILES):
                act.wait_ge(ln_c, 3 * (n - 1) + t + 1)
                if t > 0 or n > 1:
                    act.wait_ge(ln_v, 3 * (n - 1) + t)
                nc.scalar.activation(lnq[0:rows, :], xtok[0:rows, t, :], ACT.Square, accum_out=lvar[0:rows, t:t + 1]).then_inc(ln_v, 1)
            act.wait_ge(ln_r, n)
            nc.scalar.activation(lvar[:], lvar[:], ACT.Sqrt).then_inc(ln_s, 1)

        with nc.Block() as block:
            @block.sync
            def _(sp):
                for n in range(2):
                    sp.dma_start(ring[n][:], chunk_src(C_GA + n * CW)).then_inc(s_w[n], 16)
                sp.dma_start(wHG[:], hg_proj[0].rearrange("(k p) n -> p k n", p=P)).then_inc(g_wh, 16)
                for n in range(2):
                    sp.wait_ge(g_p, 4 * n + 4)
                    sp.dma_start(ring[n][:], chunk_src(C_GB + n * CW)).then_inc(s_w[n], 16)
                sp.dma_start(wSSD[:], ssd_proj[0].rearrange("(k p) n -> p k n", p=P)).then_inc(g_ws, 16)
                sp.wait_ge(g_p, 16)
                sp.dma_start(wOUT[:], w_out[0].rearrange("(k p) n -> p k n", p=P)).then_inc(g_wo, 16)
                sp.wait_ge(g_ab, KD)
                sp.dma_start(lnw[:], row(ln1_g[0])).then_inc(g_ln, 16)
                sp.dma_start(lnb[:], row(ln1_b[0])).then_inc(g_ln, 16)

            @block.scalar
            def _(act):
                for dst, first in ((gA, 0), (gB, KD)):
                    with act.Fori(0, 2) as i:
                        for n in range(4):
                            act.wait_ge(g_p, i * 4 + (first + n + 1))
                            nc.scalar.activation(dst[:, bass.ds(i * 4 + n, 1), :], ps[:, 4 + n:5 + n, 0:T], ACT.Sigmoid).then_inc(g_c, 1)
                ln_scalar(act, 1)

            @block.vector
            def _(dve):
                v = nc.vector
                dstep.on(dve)
                for c in range(KD):
                    dve.wait_ge(g_ab, c + 1)
                    if c == 0:
                        dve.wait_ge(g_c, 2 * KD)
                    if c >= 2:
                        dve.wait_ge(g_m, c - 1)
                    b = 2 * (c % 2)
                    dstep(v.tensor_tensor(tmpA[c % 2][:], ps[:, b, 0:T], gA[:, c, :], ALU.mult))
                    dstep(v.tensor_tensor(mT[:, c, :], ps[:, b + 1, 0:T], gB[:, c, :], ALU.mult))
                    v.tensor_tensor(mT[:, c, :], mT[:, c, :], tmpA[c % 2][:], ALU.add).then_inc(g_m, 1)
                v.memset(lvar[:], 1.0)
                dstep(v.memset(lst4[:], 0.0))
                for j in range(6):
                    t, n, rows = j // 2, j % 2, TILES[j // 2][1]
                    dve.wait_ge(g_mx, j + 1)
                    for i, (pr, pc, cols) in enumerate(pieces(rows)):
                        x = xtok[0:rows, t, 512 * n:512 * n + 512][:, cols]
                        last = v.scalar_tensor_tensor(x, x, ALPHA, ps[pr, 4 + j % 4, pc], ALU.mult, ALU.add,
                                                      accum_out=lst4[0:rows, t, 4 * n + i:4 * n + i + 1])
                    last.then_inc(g_x, 1)
                dve.wait_ge(g_x, 6)
                dve.wait_ge(g_ln, 32)
                ln_vector(dve, dstep, 1)

            @block.tensor
            def _(pe):
                m = nc.tensor
                for c in range(4):
                    pe.wait_ge(s_w[c % 2], w_g + 16 * (c // 2 + 1))
                    for mt in range(4):
                        if c > 0:
                            pe.wait_ge(g_c, 4 * c + mt - 3)
                        for k in range(KD):
                            last = m.matmul(ps[:, 4 + mt, 0:T], ring[c % 2][:, k, mt * P:(mt + 1) * P], xT[:, k, :],
                                            start=(k == 0), stop=(k == KD - 1))
                        last.then_inc(g_p, 1)
                pe.wait_ge(g_wh, 16)
                pe.wait_ge(g_ws, 16)
                for c in range(KD):
                    if c >= 2:
                        pe.wait_ge(g_m, c - 1)
                    b, cols = 2 * (c % 2), slice(c * P, (c + 1) * P)
                    for k in range(HH):
                        m.matmul(ps[:, b, 0:T], wHG[:, k, cols], onT[:, k, :], start=(k == 0), stop=(k == HH - 1))
                    for k in range(XT_):
                        last = m.matmul(ps[:, b + 1, 0:T], wSSD[:, k, cols], ynT[:, k, :], start=(k == 0), stop=(k == XT_ - 1))
                    last.then_inc(g_ab, 1)
                pe.wait_ge(g_wo, 16)
                pe.wait_ge(g_m, KD)
                pe.wait_ge(g_c, 2 * KD)
                for j in range(6):
                    (t0, rows), n = TILES[j // 2], j % 2
                    if j >= 4:
                        pe.wait_ge(g_x, j - 3)
                    product(ps[:, 4 + j % 4, :], lambda k: mT[:, k, t0:t0 + rows], lambda k: wOUT[:, k, 512 * n:512 * n + 512], rows).then_inc(g_mx, 1)

        if stop <= 5:
            return
        yacc = at("yacc", 154, [P, 3, D])
        psel = at("psel", 166, [P, 3, BLK])
        gsel = at("gsel", 167, [P, 3, 2, BLK])
        xs = at("xs", 170, [P, CW])
        xe = at("xe", 172, [P, 4, 2, BLK])
        gl = at("gl", 174, [P, CW])
        up = at("up", 176, [P, CW])
        sg = at("sg", 178, [P, CW])
        av_ = at("act_values", 180, [P, CW])
        aT = at("aT", 182, [P, 4, 2, BLK])
        ysb = at("ysb", 184, [P, CW])
        gT = at("gT", 148, [P, 3 * P])
        esel = at("esel", 150, [P, BLK])
        dsel = at("dsel", 150.25, [P, 3])
        boff = at("boff", 150.375, [P, 1])
        dest = at("dest", 187, [P, 3, E_])
        gm = at("gm", 187.5, [P, 3, E_])
        tab = at("tab", 188, [1, 96], I32)
        TAB_N = 64
        hT_ = at("h_T", 116, [P, KD, T])
        wr = at("wr", 189, [P, KD, E_])
        rbr = at("rbr", 190, [P, E_])
        lg = at("lg", 190.25, [P, 3, E_])
        mx8 = at("mx8", 190.75, [P, 3, 8])
        ix8 = at("ix8", 191, [P, 3, 8], U32)
        gt4 = at("gt4", 191.25, [P, 3, TOPK])
        id4 = at("id4", 191.375, [P, 3, TOPK])
        gsum = at("gsum", 191.5, [P, 3])
        msk = at("msk", 188.5, [P, 3, E_])
        eq = at("eq", 192, [P, 3, TOPK, E_])
        eg = at("eg", 193.5, [P, 3, TOPK, E_])
        cum = at("cum", 195, [P, 3, E_])
        cnt = at("cnt", 195.5, [P, E_])
        nbl = at("nbl", 195.75, [P, E_])
        binc = at("binc", 196, [P, E_])
        st64 = at("st64", 196.25, [P, E_])
        ebc = at("ebc", 196.5, [P, 1])
        gmT = at("gmT", 197, [E_, T])
        bgr = at("bgr", 198.25, [P, 2 * D])
        bdr = at("bdr", 144, [E_, D])

        wq = [at(f"wGU{i}", 16 * i, [P, 2, 2 * D]) for i in range(4)]
        wd_ = [at(f"wD{i}", 64 + 16 * i, [P, 4, D]) for i in range(2)]
        m_w = [S(f"expert_piece_loaded{i}") for i in range(6)]
        m_re = S("first_expert_reloaded")

        def load_piece(sp, e, i, sem):
            src, n = (w_gu, 256) if i < 4 else (w_down, 512)
            dst, k = (wq[i], i) if i < 4 else (wd_[i - 4], i - 4)
            sp.dma_start(dst[:], src[0, bass.ds(e, 1), n * k:n * k + n, :].rearrange("a (k p) n -> p (a k) n", p=P)).then_inc(sem, 16)

        t_wr, t_b, t_ht, t_hc = S("router_loaded"), S("expert_biases_loaded"), S("h_transposed"), S("h_copied")
        t_lg, t_e, t_ex, t_mk = S("logits_ready"), S("top_values_ready"), S("top_exp_ready"), S("choices_ready")
        t_cm, t_eb, t_tb = S("token_counts_ready"), S("block_experts_ready"), S("block_table_row")
        t_bz, t_gt, t_gc = S("padding_cleared"), S("gates_transposed"), S("gates_copied")
        t_y, t_yc = S("bias_sum_ready"), S("bias_sum_copied")

        with nc.Block() as block:
            @block.sync
            def _(sp):
                sp.dma_start(wr[:], router_w[0].rearrange("(k p) n -> p k n", p=P)).then_inc(t_wr, 16)
                sp.dma_start(rbr[:], row(router_b[0])).then_inc(t_wr, 16)
                sp.dma_start(bdr[:], b_down[0]).then_inc(t_b, 16)
                sp.wait_ge(t_bz, 1)
                sp.dma_start(bgr[0:E_, :], b_gu[0]).then_inc(t_b, 16)
                for i in range(6):
                    load_piece(sp, 0, i, m_w[i])

            @block.scalar
            def _(act):
                a = nc.scalar
                for k in range(KD):
                    act.wait_ge(t_ht, k + 1)
                    a.copy(hT_[:, k, :], ps[:, k % 2, 0:T]).then_inc(t_hc, 1)
                act.wait_ge(t_e, 1)
                a.activation(gt4[:], gt4[:], ACT.Exp).then_inc(t_ex, 1)
                act.wait_ge(t_gt, 1)
                a.copy(gmT[:], ps[0:E_, 0, 0:T]).then_inc(t_gc, 1)
                for j in range(6):
                    rows = TILES[j // 2][1]
                    act.wait_ge(t_y, j + 1)
                    a.copy(yacc[0:rows, j // 2, 512 * (j % 2):512 * (j % 2) + 512], ps[0:rows, 4 + j % 4, :]).then_inc(t_yc, 1)

            @block.vector
            def _(dve):
                v = nc.vector
                dstep.on(dve)
                v.memset(bgr[:], 0.0).then_inc(t_bz, 1)
                v.memset(mx8[:], 0.0)
                v.memset(cum[:], 0.0)
                dstep(v.memset(ix8[:], 0))
                dve.wait_ge(t_wr, 32)
                dve.wait_ge(t_lg, 1)
                for t, (_, rows) in enumerate(TILES):
                    dstep(v.tensor_tensor(lg[0:rows, t, :], ps[0:rows, 2, 32 * t:32 * t + 32], rbr[0:rows, :], ALU.add))
                    dstep(v.max(mx8[0:rows, t, :], lg[0:rows, t, :]))
                    dstep(v.max_index(ix8[0:rows, t, :], mx8[0:rows, t, :], lg[0:rows, t, :]))
                v.tensor_tensor(gt4[:], mx8[:, :, 0:TOPK], mx8[:, :, 0:1].broadcast_to([P, 3, TOPK]), ALU.subtract).then_inc(t_e, 1)
                dstep(v.tensor_copy(id4[:], ix8[:, :, 0:TOPK]))
                dve.wait_ge(t_ex, 1)
                dstep(v.tensor_reduce(gsum[:], gt4[:], AX_X, ALU.add))
                dstep(v.reciprocal(gsum[:], gsum[:]))
                dstep(v.tensor_tensor(gt4[:], gt4[:], gsum[:].unsqueeze(2).broadcast_to([P, 3, TOPK]), ALU.mult))
                dstep(v.tensor_tensor(eq[:], ecol[:].unsqueeze(1).unsqueeze(1).broadcast_to([P, 3, TOPK, E_]),
                                      id4[:].unsqueeze(3).broadcast_to([P, 3, TOPK, E_]), ALU.is_equal))
                dstep(v.tensor_tensor(eg[:], eq[:], gt4[:].unsqueeze(3).broadcast_to([P, 3, TOPK, E_]), ALU.mult))
                v.tensor_reduce(msk[:], eq[:].rearrange("p t k e -> p t e k"), AX_X, ALU.add).then_inc(t_mk, 1)
                v.tensor_reduce(gm[:], eg[:].rearrange("p t k e -> p t e k"), AX_X, ALU.add).then_inc(t_mk, 1)
                dve.wait_ge(t_cm, 1)
                for t, (_, rows) in enumerate(TILES):
                    v.tensor_copy(cum[0:rows, t, :], ps[0:rows, 2, 128 + 32 * t:160 + 32 * t])
                dstep(v.tensor_copy(cnt[:], ps[:, 2, 224:256]))
                dstep(v.tensor_scalar(nbl[:], cnt[:], 0.0, None, ALU.is_gt))
                for j in range(1, (T + BLK - 1) // BLK):
                    dstep(v.scalar_tensor_tensor(nbl[:], cnt[:], float(BLK * j), nbl[:], ALU.is_gt, ALU.add))
                dstep(v.tensor_tensor_scan(binc[:], ones[:, 0:E_], nbl[:], 0.0, ALU.mult, ALU.add))
                dstep(v.tensor_tensor(st64[:], binc[:], nbl[:], ALU.subtract))
                dstep(v.tensor_scalar(st64[:], st64[:], float(BLK), None, ALU.mult))
                dstep(v.tensor_tensor(dest[:], cum[:], st64[:].unsqueeze(1).broadcast_to([P, 3, E_]), ALU.add))
                dve.wait_ge(t_mk, 2)
                dstep(v.tensor_tensor(dest[:], dest[:], msk[:], ALU.mult))
                dstep(v.tensor_scalar(dest[:], dest[:], -1.0, None, ALU.add))
                dstep(v.tensor_scalar(lg[:, 0, :], binc[:], prow[:, 0:1], None, ALU.is_le))
                dstep(v.tensor_reduce(ebc[:], lg[:, 0, :], AX_X, ALU.add))
                v.tensor_scalar(ebc[:], ebc[:], float(E_ - 1), None, ALU.min).then_inc(t_eb, 1)
                dve.wait_ge(t_tb, 1)
                v.tensor_copy(tab[0:1, 0:64], ps[0:1, 2, 256:320])
                v.tensor_scalar(tab[0:1, TAB_N:TAB_N + 1], binc[0:1, E_ - 1:E_], -1.0, None, ALU.add)

            @block.tensor
            def _(pe):
                m = nc.tensor
                for k in range(KD):
                    if k >= 2:
                        pe.wait_ge(t_hc, k - 1)
                    for t, (t0, rows) in enumerate(TILES):
                        last = m.transpose(ps[:, k % 2, t0:t0 + rows], xtok[0:rows, t, k * P:(k + 1) * P], ident[0:rows, 0:rows])
                    last.then_inc(t_ht, 1)
                pe.wait_ge(t_hc, KD)
                pe.wait_ge(t_wr, 32)
                for t, (t0, rows) in enumerate(TILES):
                    for k in range(KD):
                        last = m.matmul(ps[0:rows, 2, 32 * t:32 * t + 32], hT_[:, k, t0:t0 + rows], wr[:, k, :], start=(k == 0), stop=(k == KD - 1))
                last.then_inc(t_lg, 1)
                pe.wait_ge(t_mk, 2)
                for o, lhs in ((128, (tri,)), (160, (ones, tri)), (192, (ones, ones, tri)), (224, (ones, ones, ones))):
                    rows = 32 if o == 192 else P
                    for t, l in enumerate(lhs):
                        kk = TILES[t][1]
                        last = m.matmul(ps[0:rows, 2, o:o + 32], l[0:kk, 0:rows], msk[0:kk, t, :], start=(t == 0), stop=(t == len(lhs) - 1))
                last.then_inc(t_cm, 1)
                for t, (t0, rows) in enumerate(TILES):
                    last = m.transpose(ps[0:E_, 0, t0:t0 + rows], gm[0:rows, t, :], ident[0:rows, 0:rows])
                last.then_inc(t_gt, 1)
                pe.wait_ge(t_eb, 1)
                m.matmul(ps[0:1, 2, 256:320], ebc[0:64, 0:1], ident[0:64, 0:64], start=True, stop=True).then_inc(t_tb, 1)
                pe.wait_ge(t_b, 32)
                pe.wait_ge(t_gc, 1)
                for j in range(6):
                    (t0, rows), n = TILES[j // 2], j % 2
                    if j >= 4:
                        pe.wait_ge(t_yc, j - 3)
                    m.matmul(ps[0:rows, 4 + j % 4, :], gmT[:, t0:t0 + rows], bdr[:, 512 * n:512 * n + 512], start=True, stop=True).then_inc(t_y, 1)

        if stop <= 6:
            return
        m_f = S("expert_piece_used")
        m_p, m_g = S("block_tokens_selected"), S("block_gates_selected")
        m_x, m_xs, m_xt, m_xc = S("block_gathered"), S("block_copied"), S("block_transposed"), S("block_transposed_copied")
        m_u = S("gate_up_ready")
        m_gl, m_sg, m_a = S("gate_limited"), S("gate_sigmoid_ready"), S("activation_ready")
        m_at, m_ac = S("activation_transposed"), S("activation_copied")
        m_gt, m_gc = S("block_gates_transposed"), S("block_gates_copied")
        m_yc = S("block_output_copied")
        m_s, m_sa = S("scattered"), S("scattered_added")
        PER = 4
        B_X, B_XT, B_G, B_U, B_Y, B_S = 0, 1, 2, 3, 4, 5
        B_GT, B_AT = B_S, B_S + 1

        with nc.Block() as block:
            @block.sync
            def _(sp):
                e = sp.value_load(tab[0:1, 0:1], min_val=0, max_val=E_ - 1)
                with sp.If(e > 0):
                    for i in range(6):
                        sp.wait_ge(m_w[i], 16)
                        load_piece(sp, e, i, m_re)
                    sp.wait_ge(m_re, 16 * 6)

        with nc.Block() as block:
            def last_block(eng):
                return eng.value_load(tab[0:1, TAB_N:TAB_N + 1], min_val=0, max_val=NBLK - 1)

            def expert(eng, b):
                return eng.value_load(tab[0:1, bass.ds(b, 1)], min_val=0, max_val=E_ - 1)

            @block.sync
            def _(sp):
                end = last_block(sp)

                with sp.Fori(0, NBLK - 1) as c:
                    with sp.If(c < end):
                        e = expert(sp, c + 1)
                        for i in range(6):
                            sp.wait_ge(m_f, c * 6 + (i + 1))
                            load_piece(sp, e, i, m_w[i])

            @block.scalar
            def _(act):
                a = nc.scalar
                end = last_block(act)
                act.wait_ge(m_x, 1)
                a.copy(xs[:], ps[:, B_X, :]).then_inc(m_xs, 1)
                act.wait_ge(m_xt, 1)
                a.copy(xe[:].rearrange("p f h j -> p (f h j)"), ps[:, B_XT, :]).then_inc(m_xc, 1)

                def run(b, c):
                    act.wait_ge(m_gl, b + 1)
                    a.activation(sg[:], gl[:], ACT.Sigmoid, scale=SALPHA).then_inc(m_sg, 1)
                    act.wait_ge(m_x, b + 2)
                    a.copy(xs[:], ps[:, B_X, :]).then_inc(m_xs, 1)
                    if c is not None:
                        act.wait_ge(m_s, b * 6)
                    act.wait_ge(m_gt, b + 1)
                    a.copy(gT[:, 0:T], ps[:, B_GT, 0:T]).then_inc(m_gc, 1)
                    act.wait_ge(m_u, b + 1)
                    act.wait_ge(m_xt, b + 2)
                    a.copy(xe[:].rearrange("p f h j -> p (f h j)"), ps[:, B_XT, :]).then_inc(m_xc, 1)
                    act.wait_ge(m_at, b + 1)
                    a.copy(aT[:].rearrange("p f h j -> p (f h j)"), ps[:, B_AT, :]).then_inc(m_ac, 1)
                    act.wait_ge(m_f, b * 6 + 6)
                    a.copy(ysb[:], ps[:, B_Y, :]).then_inc(m_yc, 1)

                run(0, None)
                with act.Fori(0, NBLK - 1) as c:
                    with act.If(c < end):
                        run(c + 1, c)

            @block.vector
            def _(dve):
                v = nc.vector
                dstep.on(dve)
                end = last_block(dve)
                v.memset(gT[:, T:3 * P], 0.0).then_inc(t_bz, 1)
                dstep(v.memset(boff[:], 0.0))

                def tokens(e):
                    dstep(v.tensor_scalar(dsel[:].unsqueeze(2), dest[:, :, bass.ds(e, 1)], boff[:, 0:1], None, ALU.subtract))
                    v.tensor_tensor(psel[:], jcol[:].unsqueeze(1).broadcast_to([P, 3, BLK]), dsel[:].unsqueeze(2).broadcast_to([P, 3, BLK]),
                                    ALU.is_equal).then_inc(m_p, 1)

                def add(j, n):
                    rows = TILES[j // 2][1]
                    y = yacc[0:rows, j // 2, 512 * (j % 2):512 * (j % 2) + 512]
                    dve.wait_ge(m_s, n + (j + 1))
                    v.tensor_tensor(y, y, ps[0:rows, B_S + j % 3, :], ALU.add).then_inc(m_sa, 1)

                def run(b, c):
                    e = expert(dve, b)
                    if c is not None:
                        dve.wait_ge(m_gt, b)
                        dve.wait_ge(m_u, b)
                    dve.wait_ge(m_p, b + 1)
                    v.tensor_tensor(gsel[:], psel[:].unsqueeze(2).broadcast_to([P, 3, 2, BLK]),
                                    gm[:, :, bass.ds(e, 1)].unsqueeze(3).broadcast_to([P, 3, 2, BLK]), ALU.mult).then_inc(m_g, 1)
                    v.tensor_copy(esel[:], ident[:, bass.ds(e, 1)].broadcast_to([P, BLK])).then_inc(m_g, 1)
                    dstep(v.tensor_scalar(boff[:], boff[:], float(BLK), None, ALU.add))
                    dve.wait_ge(m_x, b + 1)
                    dve.wait_ge(m_g, b * 2 + 2)
                    tokens(expert(dve, b + 1))
                    if c is not None:
                        for j in range(6):
                            add(j, c * 6)
                        dve.wait_ge(m_sa, b * 6)
                        dve.wait_ge(m_a, b)
                        dve.wait_ge(m_at, b)
                    dve.wait_ge(m_u, b + 1)
                    v.tensor_scalar(gl[:], ps[:, B_G, :], LIMIT, None, ALU.min).then_inc(m_gl, 1)
                    dstep(v.tensor_scalar(up[:], ps[:, B_U, :], LIMIT, -LIMIT, ALU.min, ALU.max))
                    dve.wait_ge(m_gl, b + 1)
                    dstep(v.scalar_tensor_tensor(up[:], up[:], 1.0, gl[:], ALU.add, ALU.mult))
                    dve.wait_ge(m_sg, b + 1)
                    v.tensor_tensor(av_[:], up[:], sg[:], ALU.mult).then_inc(m_a, 1)

                tokens(expert(dve, 0))
                run(0, None)
                with turns(dve, 0, NBLK - 1, (dstep, PER)) as c:
                    with dve.If(c < end):
                        run(c + 1, c)
                for j in range(6):
                    add(j, end * 6)

            @block.tensor
            def _(pe):
                m = nc.tensor
                end = last_block(pe)
                half = [slice(0, BLK), slice(BLK, 2 * BLK)]

                def gather():
                    for t, (_, rows) in enumerate(TILES):
                        for h in range(2):
                            last = m.matmul(ps[half[h], B_X, :], psel[0:rows, t, :], xtok[0:rows, t, CW * h:CW * h + CW],
                                            start=(t == 0), stop=(t == 2))
                    last.then_inc(m_x, 1)

                def turn(bank, src, signal):
                    for f in range(4):
                        last = m.transpose(ps[:, bank, f * P:(f + 1) * P], src[:, f * P:(f + 1) * P], ident[:])
                    last.then_inc(signal, 1)

                def scatter(n):
                    for j in range(6):
                        t, h = j // 2, j % 2
                        if j >= 3:
                            pe.wait_ge(m_sa, n + (j - 2))
                        m.matmul(ps[:, B_S + j % 3, :], gT[half[h], t * P:(t + 1) * P], ysb[half[h], :],
                                 start=True, stop=True).then_inc(m_s, 1)

                def run(b, c):
                    pe.wait_ge(m_g, b * 2 + 2)
                    pe.wait_ge(m_xc, b + 1)
                    for i in range(4):
                        if i == 1 and c is not None:
                            pe.wait_ge(m_gc, b)
                            pe.wait_ge(m_yc, b)
                            scatter(c * 6)
                        pe.wait_ge(m_w[i], b * 16 + 16)
                        for k in range(2 * i, 2 * i + 2):
                            for bank, col in ((B_G, 0), (B_U, D)):
                                for h in range(2):
                                    last = m.matmul(ps[half[h], bank, :], xe[:, k % 4, k // 4, :],
                                                    wq[i][:, k % 2, col + CW * h:col + CW * h + CW], start=(k == 0), stop=False)
                        last.then_inc(m_f, 1)
                    for bank, col in ((B_G, 0), (B_U, D)):
                        for h in range(2):
                            last = m.matmul(ps[half[h], bank, :], esel[:], bgr[:, col + CW * h:col + CW * h + CW], start=False, stop=True)
                    last.then_inc(m_u, 1)
                    pe.wait_ge(m_p, b + 2)
                    pe.wait_ge(m_xs, b + 1)
                    gather()
                    if c is not None:
                        pe.wait_ge(m_sa, b * 6)
                    for t, (t0, rows) in enumerate(TILES):
                        last = m.matmul(ps[:, B_GT, t0:t0 + rows], gsel[0:rows, t, :, :].rearrange("p h j -> p (h j)"),
                                        ident[0:rows, 0:rows], start=True, stop=True)
                    last.then_inc(m_gt, 1)
                    pe.wait_ge(m_xs, b + 2)
                    turn(B_XT, xs, m_xt)
                    pe.wait_ge(m_a, b + 1)
                    turn(B_AT, av_, m_at)
                    pe.wait_ge(m_ac, b + 1)
                    for i in range(2):
                        pe.wait_ge(m_w[4 + i], b * 16 + 16)
                        for k in range(4 * i, 4 * i + 4):
                            for h in range(2):
                                last = m.matmul(ps[half[h], B_Y, :], aT[:, k % 4, k // 4, :], wd_[i][:, k % 4, CW * h:CW * h + CW],
                                                start=(k == 0), stop=(k == KD - 1))
                        last.then_inc(m_f, 1)

                pe.wait_ge(t_bz, 2)
                pe.wait_ge(m_p, 1)
                gather()
                pe.wait_ge(m_xs, 1)
                turn(B_XT, xs, m_xt)
                run(0, None)
                with pe.Fori(0, NBLK - 1) as c:
                    with pe.If(c < end):
                        run(c + 1, c)
                pe.wait_ge(m_gc, end + 1)
                pe.wait_ge(m_yc, end + 1)
                scatter(end * 6)

        if stop <= 7:
            return
        dstep = Steps(S("last_dve_step"))
        with nc.Block() as block:
            @block.sync
            def _(sp):
                sp.dma_start(lnw[:], row(ln2_g[0])).then_inc(g_ln, 16)
                sp.dma_start(lnb[:], row(ln2_b[0])).then_inc(g_ln, 16)
                sp.wait_ge(ln_done, 6)
                for t in range(2):
                    sp.dma_start(y_prompt[0, P * t:P * t + P, :], xtok[:, t, :]).then_inc(s_out, 16)
                sp.dma_start(y_sample.rearrange("b s d -> (b s) d"), xtok[0:32, 2, :]).then_inc(s_out, 16)
                sp.wait_ge(s_out, 48 + 16 * (NB + 1) + 48)

            @block.scalar
            def _(act):
                ln_scalar(act, 2)

            @block.vector
            def _(dve):
                v = nc.vector
                dstep.on(dve)
                dstep(v.memset(lst4[:], 0.0))
                for t, (_, rows) in enumerate(TILES):
                    x = xtok[0:rows, t, :]
                    dstep(v.scalar_tensor_tensor(x, x, ALPHA, yacc[0:rows, t, :], ALU.mult, ALU.add,
                                                 accum_out=lst4[0:rows, t, 0:1]))
                dve.wait_ge(g_ln, 64)
                ln_vector(dve, dstep, 2)


_INS = ["x_prompt", "x_sample", "state_hgrn", "state_ssm", "state_conv", "hg_lower_bounds", "w_in", "hg_norm_w",
        "hg_proj", "conv_w", "conv_b", "dt_bias", "a_log", "d_skip", "ssd_norm_w", "ssd_proj", "w_out", "ln1_g",
        "ln1_b", "router_w", "router_b", "w_gu", "b_gu", "w_down", "b_down", "ln2_g", "ln2_b"]
_OUTS = [(1, SEQ, D), (NB, NS, D), (1, 1, HH, P, P), (1, 1, SH, SP_, SN), (1, 1, CK - 1, XBC),
         (1, NB, HH, P, P), (1, NB, SH, SP_, SN), (1, NB, CK - 1, XBC)]


def kernel(**inputs):
    import numpy as _np
    import concourse.bacc as _bacc
    from concourse.bass_utils import run_bass_kernel_spmd as _run

    nc = _bacc.Bacc("TRN2", target_bir_lowering=False, num_devices=1)
    arrays, args = {}, []
    for name in _INS:
        a = _np.ascontiguousarray(inputs[name])
        arrays[f"in_{name}"] = a
        args.append(nc.dram_tensor(f"in_{name}", a.shape, mybir.dt.from_np(a.dtype), kind="ExternalInput").ap())
    for i, shape in enumerate(_OUTS):
        args.append(nc.dram_tensor(f"out_{i}", shape, F32, kind="ExternalOutput").ap())
    build(nc, *args)
    r = _run(nc, [arrays], core_ids=[0])
    return tuple(r.results[0][f"out_{i}"] for i in range(len(_OUTS)))
```

```python
from contextlib import ExitStack, contextmanager

import concourse.bass as bass
from concourse import mybir

F32 = mybir.dt.float32
BF16 = mybir.dt.bfloat16
I32 = mybir.dt.int32
U32 = mybir.dt.uint32
ALU = mybir.AluOpType
ACT = mybir.ActivationFunctionType
AX_X = mybir.AxisListType.X

P = 128
D = 1024
SEQ = 256
NB, NS = 8, 4
T = SEQ + NB * NS
TILES = ((0, 128), (128, 128), (256, 32))
KD = D // P
HH = 8
CH = 32
SH, SP_, SG, SN = 32, 64, 4, 128
INNER = SH * SP_
HPG = SH // SG
GW = INNER // SG
XBC = INNER + 2 * SG * SN
CT = XBC // P
XT_ = INNER // P
CK = 4
E_, TOPK = 32, 4
BLK = 64
NBLK = (T * TOPK + E_ * (BLK - 1)) // BLK
LIMIT, SALPHA = 7.0, 1.702
ALPHA = 2.0 ** 0.25
LN_EPS, RMS_EPS = 1e-5, 1e-6
C_Q, C_F, C_V, C_G, C_Z = 0, D, 2 * D, 3 * D, 4 * D
C_X = C_Z + INNER
C_DT = C_X + XBC
C_GA = C_DT + SH
C_GB = C_GA + D
CW = 512
FROW = 3 + SEQ
CROW = FROW + NB * (CK - 1 + NS)
CO = CROW - (CK - 1)
SC = 416
EXPMAX = 80.0
FMIN = 2.0 ** -62


class Steps:

    def __init__(self, sem):
        self.sem, self.n = sem, 0

    def on(self, eng):
        self.eng = eng
        return self

    def __call__(self, ins):
        ins.then_inc(self.sem, 1)
        self.n = self.n + 1
        self.eng.wait_ge(self.sem, self.n)


@contextmanager
def turns(eng, first, end, *counts):
    base = [s.n - first * per for s, per in counts]
    with eng.Fori(first, end) as i:
        for (s, per), b in zip(counts, base):
            s.n = i * per + b
        yield i
    for (s, per), b in zip(counts, base):
        s.n = b + end * per


def build(nc, x_prompt, x_sample, state_hgrn, state_ssm, state_conv, hg_lower_bounds, w_in, hg_norm_w, hg_proj,
          conv_w, conv_b, dt_bias, a_log, d_skip, ssd_norm_w, ssd_proj, w_out, ln1_g, ln1_b, router_w,
          router_b, w_gu, b_gu, w_down, b_down, ln2_g, ln2_b,
          y_prompt, y_sample, o_hg_p, o_ssm_p, o_conv_p, o_hg_s, o_ssm_s, o_conv_s, stop=99):
    ctx = ExitStack()
    base = (nc.sbuf_base + 31) // 32 * 32

    def at(name, kb, shape, dt=F32):
        return nc.alloc_sbuf_tensor_at(name, shape, dt, offset=base + int(kb * 1024))

    def S(name):
        return ctx.enter_context(nc.semaphore(name))

    def row(v):
        return v.partition_broadcast(P)

    def product(out, lhs, rhs, rows):
        for k in range(KD):
            if rows == P:
                last = nc.tensor.matmul(out[:], lhs(k), rhs(k), start=(k == 0), stop=(k == KD - 1))
            else:
                for r in range(4):
                    last = nc.tensor.matmul(out[32 * r:32 * r + 32, 0:P], lhs(k), rhs(k)[:, P * r:P * r + P],
                                            start=(k == 0), stop=(k == KD - 1))
        return last

    def pieces(rows):
        if rows == P:
            return ((slice(0, P), slice(0, CW), slice(0, CW)),)
        return tuple((slice(32 * r, 32 * r + 32), slice(0, P), slice(P * r, P * r + P)) for r in range(4))

    with ctx:
        ps = ctx.enter_context(nc.psum_tensor("ps", [P, 8, 512], F32))

        ident = at("ident", 96, [P, P])
        tri = at("tri", 96.5, [P, P])
        ones = at("ones", 97, [P, P])
        smask = at("smask", 97.5, [32, 32])
        sbatch = at("sbatch", 97.625, [32, 32])
        bsel = at("bsel", 97.75, [32, NB])
        cmask = at("cmask", 97.875, [P, CH])
        keep = at("keep", 98, [P, T])
        vecs = at("vecs", 99.25, [P, 160])
        jcol = at("jcol", 100, [P, BLK])
        ecol = at("ecol", 100.25, [P, E_])
        prow = at("prow", 100.5, [P, 1])
        sm4 = at("sm4", 100.625, [P, 32])
        bs2 = at("bs2", 100.75, [P, NB])
        cm8 = at("cm8", 153, [P, NB, 32])
        xtok = at("xtok", 104, [P, 3, D])
        xT = at("xT", 116, [P, KD, T])
        ynT = at("ynT", 125.5, [P, XT_, T])
        onT = at("onT", 144, [P, HH, T])
        ring = [at(f"ring{i}", 16 * i, [P, KD, CW]) for i in range(2)]
        z = at("z", 154, [P, 3, INNER])
        convBC = at("convBC", 178, [P, CT - XT_, T])
        convX = at("convX", 188, [P, XT_, T])
        wconv = vecs[:, 0:CK * CT].rearrange("p (j c) -> p j c", c=CT)
        bconv = vecs[:, CK * CT:CK * CT + CT]
        hgw = vecs[:, 120:128]
        ssdw = vecs[:, 128:144]
        lbv = vecs[:, 144:152]
        w_k = w_in[0].rearrange("(k p) n -> p k n", p=P)

        def chunk_src(c):
            return w_k[:, :, bass.ds(c, CW)]

        xrow = at("xrow", 32, [P, CT, CROW])
        prev = at("prev", 62, [NB * 3, XBC])
        ncol = at("ncol", 74, [P, CT, 27])
        nrows = at("nrows", 80, [27, XBC])
        acc = [at(f"acc{i}", 92 + 1.25 * i, [P, CROW]) for i in range(2)]
        vrows = [at("vrows0", 94.5, [P, P]), at("vrows1", 95, [24, P])]
        wdt = at("wdt", 103, [P, KD, SH])
        dtb = at("dtb", 102, [P, SH])
        dt = at("dt", 101.25, [P, 3, SH])

        s_in = S("x_loaded")
        s_vec = S("vectors_loaded")
        s_prev = S("conv_state_loaded")
        s_wdt = S("dt_weights_loaded")
        s_w = [S(f"chunk_loaded{i}") for i in range(2)]
        s_const = S("constants_ready")
        s_zero = S("xrow_cleared")
        s_xtp = S("xT_transposed")
        s_xte = S("xT_copied")
        s_vt = S("vectors_transposed")
        s_ve = S("vectors_copied")
        s_pt = S("conv_state_transposed")
        s_pe_ = S("conv_state_copied")
        s_mt = S("projection_ready")
        s_me = S("projection_copied")
        s_conv = S("conv_ready")
        s_silu = S("conv_activated")
        s_dtp = S("dt_ready")
        s_nc = S("conv_tail_gathered")
        s_nct = S("conv_tail_transposed")
        s_nce = S("conv_tail_copied")
        s_out = S("outputs_stored")
        dstep, astep, pstep = Steps(S("dve_step")), Steps(S("act_step")), Steps(S("pool_step"))
        stored = 0

        with nc.Block() as block:
            @block.sync
            def _(sp):
                for t in range(2):
                    sp.dma_start(xtok[:, t, :], x_prompt[0, P * t:P * t + P, :]).then_inc(s_in, 16)
                sp.dma_start(xtok[0:32, 2, :], x_sample.rearrange("b s d -> (b s) d")).then_inc(s_in, 16)
                sp.dma_start(ring[0][:], chunk_src(C_X)).then_inc(s_w[0], 16)
                sp.dma_start(ring[1][:], chunk_src(C_X + CW)).then_inc(s_w[1], 16)
                with sp.Fori(1, 3) as i:
                    for n in range(2):
                        sp.wait_ge(s_mt, i * 8 + (4 * n - 4))
                        sp.dma_start(ring[n][:], chunk_src(i * (2 * CW) + (C_X + n * CW))).then_inc(s_w[n], 16)
                for c in range(INNER // CW):
                    sp.wait_ge(s_mt, CT - 4 + 4 * c if c < 2 else CT + 3 * (c - 1))
                    sp.dma_start(ring[c % 2][:], chunk_src(C_Z + c * CW)).then_inc(s_w[c % 2], 16)
                sp.wait_ge(s_nce, 2)
                sp.dma_start(o_conv_p[0, 0], nrows[0:3, :]).then_inc(s_out, 16)
                sp.dma_start(o_conv_s[0].rearrange("b r c -> (b r) c"), nrows[3:27, :]).then_inc(s_out, 16)
                sp.wait_ge(s_out, 32)

            @block.gpsimd
            def _(pool):
                g = nc.gpsimd
                pstep.on(pool)
                g.memset(xrow[:, :, 0:3], 0.0).then_inc(s_zero, 1)
                g.memset(dt[:], 0.0).then_inc(s_zero, 1)
                pstep(g.memset(ones[:], 1.0))
                pstep(g.memset(ident[:], 0.0))
                pstep(g.memset(keep[:], 1.0))
                pstep(g.memset(sbatch[:], 1.0))
                pstep(g.memset(cm8[:], 1.0))
                pstep(g.iota(jcol[:], [[1, BLK]], base=0, channel_multiplier=0, allow_small_or_imprecise_dtypes=True))
                pstep(g.iota(ecol[:], [[1, E_]], base=0, channel_multiplier=0, allow_small_or_imprecise_dtypes=True))
                pstep(g.iota(prow[:], [[1, 1]], base=0, channel_multiplier=1, allow_small_or_imprecise_dtypes=True))
                pstep(g.affine_select(out=ident[:], in_=ident[:], compare_op=ALU.not_equal, fill=1.0, base=0,
                                pattern=[[-1, P]], channel_multiplier=1))
                pstep(g.affine_select(out=tri[:], in_=ones[:], compare_op=ALU.is_ge, fill=0.0, base=0,
                                pattern=[[1, P]], channel_multiplier=-1))
                for r in range(4):
                    pstep(g.affine_select(out=cmask[32 * r:32 * r + 32, :], in_=ones[32 * r:32 * r + 32, 0:CH],
                                    compare_op=ALU.is_ge, fill=0.0, base=0, pattern=[[1, CH]],
                                    channel_multiplier=-1))
                pstep(g.memset(keep[:, 0:SEQ].rearrange("p (c s) -> p c s", s=CH)[:, :, 0:1], 0.0))
                pstep(g.memset(keep[:, SEQ:T].rearrange("p (c s) -> p c s", s=NS)[:, :, 0:1], 0.0))
                sb3 = sbatch[:].rearrange("p (b s) -> p b s", s=NS)
                pstep(g.affine_select(out=sb3, in_=sb3, compare_op=ALU.is_ge, fill=0.0, base=0,
                                      pattern=[[-NS, NB], [0, NS]], channel_multiplier=1))
                pstep(g.affine_select(out=sb3, in_=sb3, compare_op=ALU.is_ge, fill=0.0, base=NS - 1,
                                      pattern=[[NS, NB], [0, NS]], channel_multiplier=-1))
                pstep(g.tensor_copy(bsel[:], sb3[:, :, 0]))
                pstep(g.affine_select(out=cm8[:], in_=cm8[:], compare_op=ALU.is_ge, fill=0.0, base=0,
                                      pattern=[[-NS, NB], [1, 32]], channel_multiplier=0))
                pstep(g.affine_select(out=cm8[:], in_=cm8[:], compare_op=ALU.is_ge, fill=0.0, base=NS - 1,
                                      pattern=[[NS, NB], [-1, 32]], channel_multiplier=0))
                g.tensor_tensor(smask[:], sbatch[:], tri[0:32, 0:32], ALU.mult).then_inc(s_const, 1)

            @block.scalar
            def _(act):
                a = nc.scalar
                vr = vrows[0]
                act.dma_start(vr[0:96, :], conv_w[0].rearrange("j (c p) -> (j c) p", p=P)).then_inc(s_vec, 16)
                act.dma_start(vr[96:120, :], conv_b[0].rearrange("(c p) -> c p", p=P)).then_inc(s_vec, 16)
                act.dma_start(vr[120:128, :], hg_norm_w[0].rearrange("(c p) -> c p", p=P)).then_inc(s_vec, 16)
                act.dma_start(vrows[1][0:16, :], ssd_norm_w[0].rearrange("(c p) -> c p", p=P)).then_inc(s_vec, 16)
                act.dma_start(vrows[1][16:24, :], hg_lower_bounds[0].rearrange("(c p) -> c p", p=P)).then_inc(s_vec, 16)
                act.dma_start(prev[:], state_conv[0].rearrange("b r c -> (b r) c")).then_inc(s_prev, 16)
                act.dma_start(wdt[:], w_k[:, :, C_DT:C_DT + SH]).then_inc(s_wdt, 16)
                act.dma_start(dtb[:], row(dt_bias[0])).then_inc(s_wdt, 16)
                for k in range(KD):
                    act.wait_ge(s_xtp, k + 1)
                    a.copy(xT[:, k, :], ps[:, k % 2, 0:T]).then_inc(s_xte, 1)
                for c in range(CT + 2):
                    if c < CT:
                        act.wait_ge(s_mt, c + 1)
                        a.copy(xrow[:, c, 3:3 + SEQ], ps[:, 4 + c % 4, 0:SEQ])
                        a.copy(xrow[:, c, FROW:CROW].rearrange("p (b s) -> p b s", s=7)[:, :, 3:7],
                               ps[:, 4 + c % 4, SEQ:T].rearrange("p (b s) -> p b s", s=NS)).then_inc(s_me, 1)
                    if c >= 2:
                        k = c - 2
                        act.wait_ge(s_conv, k + 1)
                        out = convX[:, k, :] if k < XT_ else convBC[:, k - XT_, :]
                        a.activation(out[:, 0:SEQ], acc[k % 2][:, 0:SEQ], ACT.Silu)
                        a.activation(out[:, SEQ:T].rearrange("p (b s) -> p b s", s=NS),
                                     acc[k % 2][:, FROW:CROW].rearrange("p (b s) -> p b s", s=7)[:, :, 0:NS],
                                     ACT.Silu).then_inc(s_silu, 1)
                for j in range(3 * INNER // CW):
                    n, (t, (_, rows)) = j // 3, (j % 3, TILES[j % 3])
                    act.wait_ge(s_mt, CT + j + 1)
                    for pr, pc, cols in pieces(rows):
                        last = a.activation(z[0:rows, t, n * CW:(n + 1) * CW][:, cols], ps[pr, 4 + j % 4, pc], ACT.Silu)
                    last.then_inc(s_me, 1)

            @block.vector
            def _(dve):
                v = nc.vector
                dstep.on(dve)
                dve.wait_ge(s_vt, 1)
                v.tensor_copy(vecs[:, 0:152], ps[:, 2, 0:152]).then_inc(s_ve, 1)
                dve.wait_ge(s_zero, 1)
                for h in range(2):
                    dve.wait_ge(s_pt, h + 1)
                    v.tensor_copy(xrow[:, 12 * h:12 * h + 12, FROW:CROW].rearrange("p c (b s) -> p c b s", s=7)[:, :, :, 0:3],
                                  ps[:, h, 0:288].rearrange("p (c b s) -> p c b s", b=NB, s=3)).then_inc(s_pe_, 1)
                dve.wait_ge(s_ve, 1)
                dve.wait_ge(s_pe_, 2)
                def convolve(i, n, first=False):
                    dve.wait_ge(s_me, i * 2 + (n + 1))
                    if not first:
                        dve.wait_ge(s_silu, i * 2 + (n - 1))
                    c = bass.ds(i * 2 + n, 1)
                    o = acc[n][:, 0:CO]
                    tap = [xrow[:, c, j:j + CO].rearrange("p c l -> p (c l)") for j in range(CK)]
                    w = [wconv[:, j, c] for j in range(CK)]
                    dstep(v.tensor_scalar(o, tap[0], w[0], bconv[:, c], ALU.mult, ALU.add))
                    dstep(v.scalar_tensor_tensor(o, tap[1], w[1], o, ALU.mult, ALU.add))
                    dstep(v.scalar_tensor_tensor(o, tap[2], w[2], o, ALU.mult, ALU.add))
                    v.scalar_tensor_tensor(o, tap[3], w[3], o, ALU.mult, ALU.add).then_inc(s_conv, 1)

                convolve(0, 0, True)
                convolve(0, 1, True)
                with turns(dve, 1, CT // 2, (dstep, 6)) as i:
                    convolve(i, 0)
                    convolve(i, 1)
                v.tensor_copy(ncol[:, :, 0:3], xrow[:, :, SEQ:FROW]).then_inc(s_nc, 1)
                v.tensor_copy(ncol[:, :, 3:27].rearrange("p c (b s) -> p c b s", s=3),
                              xrow[:, :, FROW:CROW].rearrange("p c (b s) -> p c b s", s=7)[:, :, :, 4:7]).then_inc(s_nc, 1)
                dve.wait_ge(s_dtp, 1)
                dve.wait_ge(s_wdt, 32)
                dve.wait_ge(s_zero, 2)
                for t, (_, rows) in enumerate(TILES):
                    v.tensor_tensor(dt[0:rows, t, :], ps[0:rows, 3, 32 * t:32 * t + 32], dtb[0:rows, :], ALU.add)
                for h in range(2):
                    dve.wait_ge(s_nct, h + 1)
                    v.tensor_copy(nrows[:, 1536 * h:1536 * h + 1536].rearrange("p (c n) -> p c n", n=512),
                                  ps[0:27, 0:3, :]).then_inc(s_nce, 1)

            @block.tensor
            def _(pe):
                m = nc.tensor
                pe.wait_ge(s_const, 1)
                pe.wait_ge(s_in, 48)
                for k in range(KD):
                    if k >= 2:
                        pe.wait_ge(s_xte, k - 1)
                    for t, (t0, rows) in enumerate(TILES):
                        last = m.transpose(ps[:, k % 2, t0:t0 + rows], xtok[0:rows, t, k * P:(k + 1) * P], ident[0:rows, 0:rows])
                    last.then_inc(s_xtp, 1)

                def columns(i, n, first=False):
                    pe.wait_ge(s_w[n], i * 16 + 16)
                    for mt in range(4):
                        if not first:
                            pe.wait_ge(s_me, i * 8 + (4 * n + mt - 3))
                        for k in range(KD):
                            last = m.matmul(ps[:, 4 + mt, 0:T], ring[n][:, k, mt * P:(mt + 1) * P], xT[:, k, :],
                                            start=(k == 0), stop=(k == KD - 1))
                        last.then_inc(s_mt, 1)

                pe.wait_ge(s_xte, KD)
                columns(0, 0, True)
                pe.wait_ge(s_vec, 80)
                m.transpose(ps[:, 2, 0:P], vrows[0][:], ident[:])
                m.transpose(ps[:, 2, P:P + 24], vrows[1][:], ident[0:24, 0:24]).then_inc(s_vt, 1)
                pe.wait_ge(s_prev, 16)
                for h in range(2):
                    for c in range(12):
                        last = m.transpose(ps[:, h, 24 * c:24 * c + 24], prev[:, (12 * h + c) * P:(12 * h + c + 1) * P], ident[0:24, 0:24])
                    last.then_inc(s_pt, 1)
                pe.wait_ge(s_wdt, 32)
                for t, (t0, rows) in enumerate(TILES):
                    for k in range(KD):
                        last = m.matmul(ps[0:rows, 3, 32 * t:32 * t + 32], xT[:, k, t0:t0 + rows], wdt[:, k, :],
                                        start=(k == 0), stop=(k == KD - 1))
                last.then_inc(s_dtp, 1)

                columns(0, 1)
                with pe.Fori(1, CT // 8) as i:
                    columns(i, 0)
                    columns(i, 1)
                for c in range(INNER // CW):
                    n = c % 2
                    pe.wait_ge(s_w[n], 16 * (3 + c // 2 + 1))
                    for t, (t0, rows) in enumerate(TILES):
                        j = 3 * c + t
                        pe.wait_ge(s_me, CT + j - 3)
                        product(ps[:, 4 + j % 4, :], lambda k: xT[:, k, t0:t0 + rows], lambda k: ring[n][:, k, :], rows).then_inc(s_mt, 1)
                    if c == 1:
                        pe.wait_ge(s_nc, 2)
                        for h in range(2):
                            if h == 1:
                                pe.wait_ge(s_nce, 1)
                            for c in range(12):
                                last = m.transpose(ps[0:27, c // 4, (c % 4) * P:(c % 4 + 1) * P], ncol[:, 12 * h + c, :], ident[:])
                            last.then_inc(s_nct, 1)

        if stop <= 1:
            return
        xtk = at("xtk", 0, [P, 3, INNER])
        xdt = at("xdt", 24, [P, 3, INNER])
        cbm = at("cbm", 48, [P, SG, SC])
        WB, DW, DY = 6, 2, 4
        wbuf = [at(f"wbuf{i}", kb, [P, SC]) for i, kb in enumerate((55, 56.75, 58.5, 60.25, 130, 131.75))]
        btok = at("btok", 62, [P, 3, SG * SN])
        dtaw = at("dtaw", 68, [32, INNER])
        hst = [at(f"hst{i}", kb, [P, XT_, SN]) for i, kb in enumerate((76, 84, 48, 68))]
        xw2 = at("xw2", 56, [P, GW])
        b2 = at("b2", 58, [P, SN])
        cmk = at("cmk", 125.5, [P, NB, SG, 32])
        dsk = at("dsk", 92, [P, SH])
        alog = at("alog", 92.125, [P, SH])
        av = at("av", 92.25, [P, 3, SH])
        wd = at("wd", 92.625, [P, 3, SH])
        dtv = at("dtv", 93, [P, 3, SH])
        dta = at("dta", 93.375, [P, 3, SH])
        dtmp = at("dtmp", 93.75, [P, 3, SH])
        dabs = at("dabs", 94.125, [P, 3, SH])
        eA = at("eA", 94.5, [32, SH])
        dec = at("dec", 94.625, [P, XT_ * NB])
        ss = at("ss", 95.125, [P, 3 * SG])
        ats = at("ats", 101.75, [32, T])
        part = at("part", 138, [32, T], BF16)
        rest = at("rest", 138.75, [32, T])
        a3 = at("a3", 140, [96, T], BF16)
        m3 = at("m3", 140.625, [96, SH])
        sel = at("sel", 144, [96, SH, P], BF16)
        hT = at("hT", 144, [P, XT_, P])
        bm = [at(f"bm{i}", 59 + 0.5 * i, [P, SN]) for i in range(2)]
        hp = at("hp", 76, [P, XT_, SN])
        sq = at("sq", 141, [P, GW])
        xw = at("xw", 188, [P, 2, INNER])

        q_h = [S(f"state_moved{i}") for i in range(4)]
        q_par = S("ssd_parameters_loaded")
        q_xp = S("x_transposed")
        q_xa = S("x_copied_act")
        q_xv = S("x_copied_dve")
        q_dt = S("softplus_parts")
        q_dta = S("dta_ready")
        q_dx = S("dta_widened")
        q_A = S("A_ready")
        q_ac = S("A_copied")
        q_dif = S("decay_exponents_ready")
        q_exp = S("decays_ready")
        q_wd = S("state_weights_ready")
        q_xdt = S("xdt_ready")

        with nc.Block() as block:
            @block.sync
            def _(sp):
                sp.dma_start(dsk[:], row(d_skip[0])).then_inc(q_par, 16)
                sp.dma_start(alog[:], row(a_log[0])).then_inc(q_par, 16)
                for n in range(3):
                    sp.dma_start(hst[n][:], state_ssm[0, n].rearrange("h p n -> (h p) n").rearrange("(i q) n -> q i n", q=P)).then_inc(q_h[n], 16)

            @block.gpsimd
            def _(pool):
                g = nc.gpsimd
                pstep.on(pool)
                pstep(g.memset(xdt[:, 2, :], 0.0))
                pstep(g.memset(cmk[:], 0.0))
                for b in range(NB):
                    g.tensor_copy(cmk[:, b, :, NS * b:NS * b + NS], convBC[:, SG:2 * SG, SEQ + NS * b:SEQ + NS * b + NS])
                pool.wait_ge(q_dta, 1)
                g.tensor_copy(dtaw[:].rearrange("p (h d) -> p h d", d=SP_),
                              dta[0:32, 2, :].unsqueeze(2).broadcast_to([32, SH, SP_])).then_inc(q_dx, 1)
                for t, (_, rows) in enumerate(TILES):
                    pool.wait_ge(q_xa, 2 * t + 2)
                    pool.wait_ge(q_xv, 2 * t + 2)
                    g.tensor_tensor(xdt[0:rows, t, :].rearrange("p (h d) -> p h d", d=SP_),
                                    xtk[0:rows, t, :].rearrange("p (h d) -> p h d", d=SP_),
                                    dtv[0:rows, t, :].unsqueeze(2).broadcast_to([rows, SH, SP_]), ALU.mult).then_inc(q_xdt, 1)

            def copy_x(eng_copy, j):
                t = j // 4 if j < 12 else j - 12
                rows = TILES[t][1]
                dst = xtk[0:rows, t, (j % 4) * 512:(j % 4 + 1) * 512] if j < 12 else btok[0:rows, t, :]
                return eng_copy(dst, ps[0:rows, j % 4, :])

            @block.scalar
            def _(act):
                a = nc.scalar
                astep.on(act)
                act.wait_ge(q_par, 32)
                a.activation(alog[:], alog[:], ACT.Exp).then_inc(q_dt, 1)
                astep(a.activation(dabs[:], dt[:], ACT.Abs))
                astep(a.activation(dabs[:], dabs[:], ACT.Exp, scale=-1.0))
                a.activation(dabs[:], dabs[:], ACT.Ln, bias=1.0).then_inc(q_dt, 1)
                for j in range(0, 15, 2):
                    act.wait_ge(q_xp, j + 1)
                    copy_x(a.copy, j).then_inc(q_xa, 1)
                act.wait_ge(q_A, 1)
                act.wait_ge(q_ac, 3)
                a.activation(eA[:], av[0:32, 2, :], ACT.Exp)
                a.activation(dec[:], ps[:, 6, 0:XT_ * NB], ACT.Exp)
                a.copy(ats[:], ps[0:32, 5, 0:T])
                act.wait_ge(q_dif, 1)
                a.activation(dtmp[:], dtmp[:], ACT.Exp).then_inc(q_exp, 1)

            @block.vector
            def _(dve):
                v = nc.vector
                dstep.on(dve)
                dstep(v.tensor_scalar(dtv[:], dt[:], 0.0, None, ALU.max))
                dve.wait_ge(q_dt, 2)
                dstep(v.tensor_tensor(dtv[:], dtv[:], dabs[:], ALU.add))
                v.scalar_tensor_tensor(dta[:], dtv[:], -1.0, alog[:].unsqueeze(1).broadcast_to([P, 3, SH]),
                                       ALU.mult, ALU.mult).then_inc(q_dta, 1)
                v.memset(dtmp[:], 0.0)
                v.memset(av[:], 0.0)
                for q in range(SG):
                    v.tensor_copy(sm4[32 * q:32 * q + 32, :], smask[:])
                    last = v.tensor_copy(bs2[32 * q:32 * q + 32, :], bsel[:])
                dstep(last)
                for j in range(1, 15, 2):
                    dve.wait_ge(q_xp, j + 1)
                    copy_x(v.tensor_copy, j).then_inc(q_xv, 1)
                dve.wait_ge(q_A, 1)
                for t, (_, rows) in enumerate(TILES):
                    v.tensor_copy(av[0:rows, t, :], ps[0:rows, 4, 32 * t:32 * t + 32]).then_inc(q_ac, 1)
                dve.wait_ge(q_ac, 3)
                for t, (_, rows) in enumerate(TILES):
                    last = v.tensor_tensor(dtmp[0:rows, t, :], ps[0:rows, 4, 96 + 32 * t:128 + 32 * t], av[0:rows, t, :], ALU.subtract)
                last.then_inc(q_dif, 1)
                dve.wait_ge(q_exp, 1)
                v.tensor_tensor(wd[:], dtmp[:], dtv[:], ALU.mult).then_inc(q_wd, 1)
                dve.wait_ge(q_wd, 1)
                dve.wait_ge(q_xa, 8)
                dve.wait_ge(q_xv, 7)
                for q in range(SG):
                    band, heads = slice(32 * q, 32 * q + 32), slice(HPG * q, HPG * q + HPG)
                    v.tensor_copy(b2[band, :], btok[0:32, 2, SN * q:SN * q + SN])
                    v.tensor_tensor(xw2[band, :].rearrange("p (h d) -> p h d", d=SP_),
                                    xtk[0:32, 2, GW * q:GW * q + GW].rearrange("p (h d) -> p h d", d=SP_),
                                    wd[0:32, 2, heads].unsqueeze(2).broadcast_to([32, HPG, SP_]), ALU.mult)

            @block.tensor
            def _(pe):
                m = nc.tensor
                for j in range(15):
                    t = j // 4 if j < 12 else j - 12
                    t0, rows = TILES[t]
                    if j >= 4:
                        pe.wait_ge(q_xa if j % 2 == 0 else q_xv, (j - 4) // 2 + 1)
                    for c in range(4):
                        src = convX[:, 4 * (j % 4) + c, t0:t0 + rows] if j < 12 else convBC[:, c, t0:t0 + rows]
                        last = m.transpose(ps[0:rows, j % 4, c * P:(c + 1) * P], src, ident[:])
                    last.then_inc(q_xp, 1)
                pe.wait_ge(q_dta, 1)
                d0, d1, d2 = dta[:, 0, :], dta[:, 1, :], dta[0:32, 2, :]
                for o, l, r in ((0, tri, smask), (96, ones, sbatch)):
                    if o == 0:
                        m.matmul(ps[:, 4, 0:32], l[:], d0, start=True, stop=True)
                    else:
                        m.matmul(ps[:, 4, 96:128], ones[:], d0, start=True, stop=False)
                        m.matmul(ps[:, 4, 96:128], ones[:], d1, start=False, stop=True)
                    m.matmul(ps[:, 4, o + 32:o + 64], ones[:], d0, start=True, stop=False)
                    m.matmul(ps[:, 4, o + 32:o + 64], l[:], d1, start=False, stop=True)
                    m.matmul(ps[0:32, 4, o + 64:o + 96], r[:], d2, start=True, stop=True)
                m.matmul(ps[0:32, 5, 0:P], d0, tri[:], start=True, stop=True)
                m.matmul(ps[0:32, 5, P:2 * P], d0, ones[:], start=True, stop=False)
                m.matmul(ps[0:32, 5, P:2 * P], d1, tri[:], start=False, stop=True)
                m.matmul(ps[0:32, 5, 2 * P:T], d2, smask[:], start=True, stop=True)
                pe.wait_ge(q_dx, 1)
                for i in range(XT_):
                    last = m.matmul(ps[:, 6, NB * i:NB * i + NB], dtaw[:, P * i:P * i + P], bsel[:], start=True, stop=True)
                last.then_inc(q_A, 1)

        if stop <= 2:
            return
        r_bm = S("masked_B_ready")
        r_tr = S("state_transposed")
        r_tc = S("state_copied")
        r_in = S("state_read_out")
        r_up = S("state_update_ready")
        r_ud = S("state_updated")
        r_dc = S("state_decayed")
        r_ya = S("inter_added")
        r_w = S("weighted_x_ready")
        r_sk = S("skip_ready")
        r_cb = S("scores_ready")
        r_cm = S("scores_masked")
        r_hp = S("final_state_ready")
        r_hc = S("final_state_copied")
        r_sel, r_a3 = S("head_selectors_ready"), S("A_parts_ready")
        r_ab = S("head_A_spread")
        r_d = S("head_exponents_ready")
        r_e = S("head_decays_ready")
        r_W = S("head_weights_ready")
        r_z = S("group_y_gated")
        r_yh = S("head_y_done")

        with nc.Block() as block:
            @block.sync
            def _(sp):
                def rows_of(state, b):
                    return state[0, b].rearrange("h p n -> (h p) n").rearrange("(i q) n -> q i n", q=P)

                sp.dma_start(hst[3][:], rows_of(state_ssm, 3)).then_inc(q_h[3], 16)
                for b in range(NB):
                    sp.wait_ge(r_ud, b + 1)
                    sp.dma_start(rows_of(o_ssm_s, b), hst[b % 4][:]).then_inc(q_h[b % 4], 16)
                    if b >= 1 and b + 3 < NB:
                        n = (b - 1) % 4
                        sp.wait_ge(q_h[n], 32)
                        sp.dma_start(hst[n][:], rows_of(state_ssm, b + 3)).then_inc(q_h[n], 16)
                for n in range(4):
                    sp.wait_ge(q_h[n], 64)
                sp.wait_ge(r_hc, 4)
                sp.dma_start(o_ssm_p[0, 0].rearrange("h p n -> (h p) n").rearrange("(i q) n -> q i n", q=P), hp[:]).then_inc(s_out, 16)

            @block.gpsimd
            def _(pool):
                g = nc.gpsimd
                for b in range(NB):
                    pool.wait_ge(r_tr, 4 * b + 4)
                    g.tensor_tensor(hst[b % 4][:], hst[b % 4][:], dec[:].rearrange("p (i b) -> p i b", b=NB)[:, :, b:b + 1]
                                    .broadcast_to([P, XT_, SN]), ALU.mult).then_inc(r_dc, 1)
                for t in range(2):
                    g.tensor_tensor(xw[:, t, :].rearrange("p (h d) -> p h d", d=SP_), xtk[:, t, :].rearrange("p (h d) -> p h d", d=SP_),
                                    wd[:, t, :].unsqueeze(2).broadcast_to([P, SH, SP_]), ALU.mult).then_inc(r_w, 1)
                pool.wait_ge(r_w, 2)
                for t, (_, rows) in enumerate(TILES):
                    xv = xtk[0:rows, t, :].rearrange("p (h d) -> p h d", d=SP_)
                    g.tensor_tensor(xv, xv, dsk[0:rows, :].unsqueeze(2).broadcast_to([rows, SH, SP_]), ALU.mult).then_inc(r_sk, 1)

            @block.scalar
            def _(act):
                a = nc.scalar
                astep.on(act)

                def squares(g):
                    for t, (_, rows) in enumerate(TILES):
                        act.wait_ge(r_z, 3 * g + t + 1)
                        astep(a.activation(sq[0:rows, :], z[0:rows, t, GW * g:GW * g + GW], ACT.Square,
                                           accum_out=ss[0:rows, SG * t + g:SG * t + g + 1]))

                for b in range(NB):
                    if b > 0:
                        act.wait_ge(r_in, b)
                    for q in range(4):
                        act.wait_ge(r_tr, 4 * b + q + 1)
                        a.copy(hT[:, 4 * q:4 * q + 4, :], ps[:, q % 2, :]).then_inc(r_tc, 1)
                act.wait_ge(r_in, NB)
                act.wait_ge(r_a3, 1)
                a.copy(sel[:, SH // 2:SH, :], m3[:, SH // 2:SH].unsqueeze(2).broadcast_to([96, SH // 2, P])).then_inc(r_sel, 1)
                for n in range(SH + DY + 2):
                    if 1 <= n <= SH:
                        act.wait_ge(r_d, n)
                        w = wbuf[(n - 1) % WB]
                        a.activation(w[:], w[:], ACT.Exp).then_inc(r_e, 1)
                    g, h = divmod(n - DY - 1, HPG)
                    if h == 0 and g > 0:
                        squares(g - 1)
                act.wait_ge(q_h[0], 64)
                for q in range(4):
                    act.wait_ge(r_hp, q + 1)
                    a.copy(hp[:, 4 * q:4 * q + 4, :], ps[:, q % 2, :]).then_inc(r_hc, 1)

            @block.vector
            def _(dve):
                v = nc.vector
                dstep.on(dve)
                v.memset(ss[:], 1.0)
                last = ats
                for i in range(3):
                    band = slice(32 * i, 32 * i + 32)
                    dstep(v.tensor_copy(part[:], last[:]))
                    v.tensor_copy(a3[band, :], part[:])
                    copied = v.tensor_copy(m3[band, :], ident[0:32, 0:SH])
                    if i < 2:
                        dstep(v.tensor_tensor(rest[:], last[:], part[:], ALU.subtract))
                        last = rest
                copied.then_inc(r_a3, 1)

                def mask(b):
                    if b >= 2:
                        dve.wait_ge(r_up, b - 1)
                    v.tensor_scalar(bm[b % 2][:], b2[:], bs2[:, b:b + 1], None, ALU.mult).then_inc(r_bm, 1)

                mask(0)
                for b in range(NB):
                    if b + 1 < NB:
                        mask(b + 1)
                    dve.wait_ge(r_dc, b + 1)
                    dve.wait_ge(r_up, b + 1)
                    h = hst[b % 4][:].rearrange("p (q c) n -> p q (c n)", c=4)
                    v.tensor_tensor(h, h, ps[:, 2:6, :], ALU.add).then_inc(r_ud, 1)
                dve.wait_ge(q_h[2], 64)
                dve.wait_ge(r_bm, NB)
                v.memset(cbm[:, :, 384:SC], 0.0)
                for w in wbuf:
                    dstep(v.memset(w[:], 0.0))
                dve.wait_ge(r_in, NB)
                dve.wait_ge(r_a3, 1)
                v.tensor_copy(sel[:, 0:SH // 2, :], m3[:, 0:SH // 2].unsqueeze(2).broadcast_to([96, SH // 2, P])).then_inc(r_sel, 1)
                for g in range(SG):
                    dve.wait_ge(r_cb, g + 1)
                    b = ps[:, g % 2, :]
                    v.tensor_tensor(cbm[:, g, 0:P], b[:, 0:P], tri[:], ALU.mult)
                    v.tensor_copy(cbm[:, g, P:2 * P], b[:, P:2 * P])
                    v.tensor_tensor(cbm[:, g, 2 * P:3 * P], b[:, 2 * P:3 * P], tri[:], ALU.mult)
                    v.tensor_tensor(cbm[0:32, g, 3 * P:SC], b[0:32, 3 * P:SC], smask[:], ALU.mult).then_inc(r_cm, 1)
                dve.wait_ge(r_cm, SG)

                def add_inter():
                    dve.wait_ge(r_sk, 3)
                    for q in range(4):
                        dve.wait_ge(r_in, NB)
                        if q > 0:
                            dve.wait_ge(r_ya, q)
                        dstep(v.tensor_tensor(sq[0:32, :].rearrange("p (h d) -> p h d", d=SP_), ps[32 * q:32 * q + 32, 6, :].rearrange("p (h d) -> p h d", d=SP_),
                                              eA[:, HPG * q:HPG * q + HPG].unsqueeze(2).broadcast_to([32, HPG, SP_]), ALU.mult))
                        xq = xtk[0:32, 2, 512 * q:512 * q + 512]
                        v.tensor_tensor(xq, xq, sq[0:32, :], ALU.add).then_inc(r_ya, 1)
                    dve.wait_ge(r_ya, 4)

                for n in range(SH + DY + 1):
                    if n < SH:
                        w, b = wbuf[n % WB], ps[:, n % 2, :]
                        dve.wait_ge(r_ab, n + 1)
                        if n >= WB:
                            dve.wait_ge(r_yh, n - WB + 1)
                        v.tensor_scalar(w[:, 0:2 * P], b[:, 0:2 * P], av[:, 0, n:n + 1], 0.0, ALU.subtract, ALU.min)
                        v.tensor_scalar(w[:, 2 * P:3 * P], b[:, P:2 * P], av[:, 1, n:n + 1], 0.0, ALU.subtract, ALU.min)
                        v.tensor_scalar(w[0:32, 3 * P:SC], b[0:32, 2 * P:T], av[0:32, 2, n:n + 1], 0.0, ALU.subtract, ALU.min).then_inc(r_d, 1)
                    if DW <= n < SH + DW:
                        h = n - DW
                        dve.wait_ge(r_e, h + 1)
                        w = wbuf[h % WB]
                        v.tensor_tensor(w[:], w[:], cbm[:, h // HPG, :], ALU.mult).then_inc(r_W, 1)
                    g, h = divmod(n - DY, HPG)
                    if h == 0 and g > 0:
                        g = g - 1
                        if g == 0:
                            add_inter()
                        dve.wait_ge(r_yh, HPG * g + HPG)
                        for t, (_, rows) in enumerate(TILES):
                            cols = slice(GW * g, GW * g + GW)
                            dstep(v.tensor_tensor(xtk[0:rows, t, cols], xtk[0:rows, t, cols], ps[0:rows, 2 + 3 * (g % 2) + t, :], ALU.add))
                            v.tensor_tensor(z[0:rows, t, cols], z[0:rows, t, cols], xtk[0:rows, t, cols], ALU.mult).then_inc(r_z, 1)

            @block.tensor
            def _(pe):
                m = nc.tensor
                for b in range(NB):
                    pe.wait_ge(q_h[b % 4], 32 * (b // 4) + 16)
                    for q in range(4):
                        if 4 * b + q >= 2:
                            pe.wait_ge(r_tc, 4 * b + q - 1)
                        for c in range(4):
                            last = m.transpose(ps[:, q % 2, c * P:(c + 1) * P], hst[b % 4][:, 4 * q + c, :], ident[:])
                        last.then_inc(r_tr, 1)
                    pe.wait_ge(r_bm, b + 1)
                    if b > 0:
                        pe.wait_ge(r_ud, b)
                    for c in range(4):
                        for q in range(4):
                            band = slice(32 * q, 32 * q + 32)
                            last = m.matmul(ps[:, 2 + q, c * P:(c + 1) * P], xw2[band, c * P:(c + 1) * P], bm[b % 2][band, :],
                                            start=True, stop=True, tile_position=(32 * q, 0))
                    last.then_inc(r_up, 1)
                    pe.wait_ge(r_tc, 4 * b + 4)
                    for q in range(4):
                        last = m.matmul(ps[32 * q:32 * q + 32, 6, :], cmk[:, b, q, :], hT[:, 4 * q:4 * q + 4, :].rearrange("p c n -> p (c n)"),
                                        start=(b == 0), stop=(b == NB - 1))
                    last.then_inc(r_in, 1)
                for g in range(SG):
                    bT, cT, b = convBC[:, g, :], convBC[:, SG + g, :], g % 2
                    if g >= 2:
                        pe.wait_ge(r_cm, g - 1)
                    m.matmul(ps[:, b, 0:2 * P], bT[:, 0:P], cT[:, 0:2 * P], start=True, stop=True)
                    m.matmul(ps[:, b, 2 * P:3 * P], bT[:, P:2 * P], cT[:, P:2 * P], start=True, stop=True)
                    m.matmul(ps[0:32, b, 3 * P:SC], bT[:, 2 * P:T], cT[:, 2 * P:T], start=True, stop=True).then_inc(r_cb, 1)

                pe.wait_ge(r_a3, 1)
                pe.wait_ge(r_sel, 2)
                pe.wait_ge(r_cm, SG)
                pe.wait_ge(r_ud, NB)
                for n in range(SH + DY):
                    if n < SH:
                        if n >= 2:
                            pe.wait_ge(r_d, n - 1)
                        m.matmul(ps[:, n % 2, 0:T], sel[:, n, :], a3[:], start=True, stop=True).then_inc(r_ab, 1)
                    if n >= DY:
                        g, h = divmod(n - DY, HPG)
                        if h == 0 and g == 1:
                            pe.wait_ge(r_ya, 4)
                        elif h == 0 and g > 1:
                            pe.wait_ge(r_z, 3 * (g - 1))
                        pe.wait_ge(r_W, n - DY + 1)
                        w, cols, y = wbuf[(n - DY) % WB], slice(SP_ * h, SP_ * h + SP_), 2 + 3 * (g % 2)
                        x = [xdt[:, t, GW * g + SP_ * h:GW * g + SP_ * h + SP_] for t in range(3)]
                        m.matmul(ps[:, y, cols], w[:, 0:P], x[0], start=True, stop=True)
                        m.matmul(ps[:, y + 1, cols], w[:, P:2 * P], x[0], start=True, stop=False)
                        m.matmul(ps[:, y + 1, cols], w[:, 2 * P:3 * P], x[1], start=False, stop=True)
                        m.matmul(ps[0:32, y + 2, cols], w[:, 3 * P:SC], x[2], start=True, stop=True).then_inc(r_yh, 1)
                pe.wait_ge(r_w, 2)
                pe.wait_ge(r_d, SH)
                for q in range(4):
                    if q >= 2:
                        pe.wait_ge(r_hc, q - 1)
                    for c in range(4):
                        k = 4 * q + c
                        for t in range(2):
                            last = m.matmul(ps[:, q % 2, c * P:(c + 1) * P], xw[:, t, k * P:(k + 1) * P],
                                            btok[:, t, q * SN:(q + 1) * SN], start=(t == 0), stop=(t == 1))
                    last.then_inc(r_hp, 1)

        n_rs = S("group_rms_ready")
        n_sq = S("group_rms_rooted")
        n_y = S("y_normalised")
        n_t = S("y_transposed")
        n_c = S("y_copied")
        with nc.Block() as block:
            @block.sync
            def _(sp):
                for n in range(2):
                    sp.dma_start(ring[n][:], chunk_src(C_Q + n * CW)).then_inc(s_w[n], 16)
                sp.wait_ge(s_out, 32 + 16)

            @block.scalar
            def _(act):
                act.wait_ge(n_rs, 1)
                nc.scalar.activation(ss[:], ss[:], ACT.Sqrt).then_inc(n_sq, 1)
                for c in range(XT_):
                    act.wait_ge(n_t, c + 1)
                    nc.scalar.activation(ynT[:, c, :], ps[:, c % 4, 0:T], ACT.Copy, scale=ssdw[:, c:c + 1]).then_inc(n_c, 1)

            @block.vector
            def _(dve):
                v = nc.vector
                dstep.on(dve)
                v.tensor_scalar(ss[:], ss[:], 1.0 / GW, RMS_EPS, ALU.mult, ALU.add).then_inc(n_rs, 1)
                dve.wait_ge(n_sq, 1)
                dstep(v.reciprocal(ss[:], ss[:]))
                for g in range(SG):
                    for t, (_, rows) in enumerate(TILES):
                        y = z[0:rows, t, GW * g:GW * g + GW]
                        v.tensor_scalar(y, y, ss[0:rows, SG * t + g:SG * t + g + 1], None, ALU.mult).then_inc(n_y, 1)

            @block.tensor
            def _(pe):
                for c in range(XT_):
                    pe.wait_ge(n_y, 3 * (c // 4 + 1))
                    if c >= 4:
                        pe.wait_ge(n_c, c - 3)
                    for t, (t0, rows) in enumerate(TILES):
                        last = nc.tensor.transpose(ps[:, c % 4, t0:t0 + rows], z[0:rows, t, c * P:(c + 1) * P], ident[0:rows, 0:rows])
                    last.then_inc(n_t, 1)

        if stop <= 3:
            return
        qT = at("qT", 32, [P, HH, T])
        kT = at("kT", 41.5, [P, HH, T])
        bT = at("bT", 51, [P, HH, T])
        eT = at("eT", 60.5, [P, HH, T])
        vtok = at("vtok", 70, [P, 2, D])
        gtok = at("gtok", 82, [P, 2, D])
        otok = at("otok", 0, [P, 2, D])
        vts = at("vts", 78, [P, 2, P])
        gts = at("gts", 90, [P, 2, P])
        ots = at("ots", 8, [P, 2, P])
        kps = at("kps", 194, [P, 2, P])
        scs = at("scs", 30, [P, 2, 32])
        U = [at(f"U{i}", 12 + 4 * i, [P, HH, P]) for i in range(2)]
        vm = [at(f"vm{i}", 20 + 4 * i, [P, NB, P]) for i in range(2)]
        scm = at("scm", 28, [P, 2, HH * CH])
        qsm = at("qsm", 144, [P, NB, HH, 32])
        Sb = at("Sb", 154, [P, NB, HH, P])
        kpt = at("kpt", 186, [P, 2, D])
        mid = at("mid", 198, [P, HH, 16])
        lst = at("lst", 198.5, [P, HH, 16])
        dl = at("dl", 199, [P, HH, 16])
        gate = at("gate", 199.5, [P, HH, 8])
        qs = at("qs", 200, [P, HH, 32])
        lb4 = at("lb4", 201, [P, 4, HH])
        hss = at("hss", 201.25, [P, 3 * HH])
        sq3 = at("sq3", 202, [P, D])

        w_z = 16 * ((XBC + INNER) // CW // 2)
        h_S = S("hg_state_loaded")
        h_p = S("hg_projection_ready")
        h_c = S("hg_projection_copied")
        h_lb = S("lower_bound_step")
        h_f = S("forget_gate_ready")
        h_ln = S("log_gate_ready")
        h_ek = S("k_exponents_ready")
        h_eq = S("q_exponents_ready")
        h_x = S("hg_exponentials_ready")
        h_xe = S("hg_factor_exponents_ready")
        h_k = S("kq_weighted")
        h_kt = S("k_transposed")
        h_kc = S("k_copied")
        h_sc = S("hg_scores_ready")
        h_sm = S("hg_scores_masked")
        h_P = S("chunk_sum_ready")
        h_U = S("state_carried")
        h_o = S("o_ready")
        h_oc = S("o_copied")
        h_oi = S("sample_inter_ready")
        h_oic = S("sample_inter_copied")
        h_vm = S("masked_v_ready")
        h_sd = S("sample_state_decayed")
        h_su = S("sample_sum_ready")
        h_sa = S("sample_state_updated")
        h_n = S("o_normalised")
        h_nt = S("o_transposed")
        h_nc = S("o_transposed_copied")
        NPROJ = 2 * HH + 12

        def chunks32(x):
            return x[:, :, 0:SEQ].rearrange("p h (c s) -> p h c s", s=CH)

        def chunks4(x):
            return x[:, :, SEQ:T].rearrange("p h (c s) -> p h c s", s=NS)

        with nc.Block() as block:
            @block.sync
            def _(sp):
                for b in range(NB):
                    sp.dma_start(Sb[:, b], state_hgrn[0, b].rearrange("h k v -> k h v")).then_inc(h_S, 16)
                for c in range(2, 8):
                    sp.wait_ge(h_p, 4 * (c - 1) if c <= 5 else 16 + 3 * (c - 5))
                    sp.dma_start(ring[c % 2][:], chunk_src(C_Q + c * CW)).then_inc(s_w[c % 2], 16)
                sp.wait_ge(h_U, 8)
                sp.dma_start(o_hg_p[0, 0].rearrange("h k v -> k h v"), U[0][:]).then_inc(s_out, 16)
                sp.wait_ge(s_out, 48 + 16)

            @block.gpsimd
            def _(pool):
                g = nc.gpsimd
                pool.wait_ge(h_c, NPROJ)
                for i in range(2):
                    g.tensor_tensor(vm[i][:], vts[:, i, :].unsqueeze(1).broadcast_to([P, NB, P]),
                                    bs2[:].unsqueeze(2).broadcast_to([P, NB, P]), ALU.mult).then_inc(h_vm, 1)
                pool.wait_ge(h_oi, 1)
                pool.wait_ge(h_x, 5)
                for h in range(HH):
                    s = Sb[:, :, h, :]
                    g.tensor_tensor(s, s, lst[:, h, 8:16].unsqueeze(2).broadcast_to([P, NB, P]), ALU.mult).then_inc(h_sd, 1)

            @block.scalar
            def _(act):
                a = nc.scalar
                astep.on(act)
                act.wait_ge(h_lb, 1)
                a.activation(lb4[:, 1, :], lb4[:, 0, :], ACT.Exp).then_inc(h_lb, 1)
                with act.Fori(0, 2) as i:
                    for n in range(4):
                        act.wait_ge(h_p, i * 4 + (n + 1))
                        a.activation(qT[:, bass.ds(i * 4 + n, 1), :], ps[:, 4 + n:5 + n, 0:T], ACT.Silu).then_inc(h_c, 1)
                with act.Fori(0, 2) as i:
                    for n in range(4):
                        act.wait_ge(h_p, i * 4 + (HH + n + 1))
                        a.activation(eT[:, bass.ds(i * 4 + n, 1), :], ps[:, 4 + n:5 + n, 0:T], ACT.Sigmoid).then_inc(h_c, 1)
                act.wait_ge(h_f, 1)
                a.activation(bT[:], eT[:], ACT.Ln).then_inc(h_ln, 1)
                for j in range(6):
                    t, rows = j % 3, TILES[j % 3][1]
                    act.wait_ge(h_p, 2 * HH + j + 1)
                    if t < 2:
                        a.copy(vtok[:, t, CW * (j // 3):CW * (j // 3) + CW], ps[:, 4 + j % 4, :]).then_inc(h_c, 1)
                    else:
                        a.copy(vts[:, j // 3, :], ps[:, 4 + j % 4, 0:P]).then_inc(h_c, 1)
                act.wait_ge(h_ek, 1)
                a.activation(eT[:], eT[:], ACT.Exp).then_inc(h_x, 1)
                act.wait_ge(h_eq, 1)
                a.activation(bT[:], bT[:], ACT.Exp).then_inc(h_x, 1)
                act.wait_ge(h_xe, 2)
                a.activation(mid[:], mid[:], ACT.Exp).then_inc(h_x, 1)
                a.activation(gate[:], gate[:], ACT.Exp).then_inc(h_x, 1)
                a.activation(lst[:], lst[:], ACT.Exp).then_inc(h_x, 1)
                a.activation(dl[:], dl[:], ACT.Exp).then_inc(h_x, 1)
                for j in range(6, 12):
                    t, rows = j % 3, TILES[j % 3][1]
                    act.wait_ge(h_p, 2 * HH + j + 1)
                    if t < 2:
                        a.activation(gtok[:, t, CW * (j // 3 - 2):CW * (j // 3 - 1)], ps[:, 4 + j % 4, :], ACT.Sigmoid).then_inc(h_c, 1)
                    else:
                        a.activation(gts[:, j // 3 - 2, :], ps[:, 4 + j % 4, 0:P], ACT.Sigmoid).then_inc(h_c, 1)
                for j in range(4):
                    act.wait_ge(h_kt, j + 1)
                    a.copy(kpt[:, j // 2, 512 * (j % 2):512 * (j % 2) + 512], ps[:, j, :]).then_inc(h_kc, 1)
                act.wait_ge(h_kt, 5)
                a.copy(kps[:].rearrange("p c v -> p (c v)"), ps[:, 0, 0:2 * P]).then_inc(h_kc, 1)
                act.wait_ge(h_oi, 1)
                a.copy(ots[:].rearrange("p c v -> p (c v)"), ps[:, 4, 2 * P:4 * P]).then_inc(h_oic, 1)
                for t in range(2):
                    act.wait_ge(h_o, 4 * t + 4)
                    a.copy(otok[:, t, :].rearrange("p (b n) -> p b n", b=2), ps[:, 6:8, :]).then_inc(h_oc, 1)
                act.wait_ge(n_rs, 2)
                a.activation(hss[:], hss[:], ACT.Sqrt).then_inc(n_sq, 1)
                for h in range(HH):
                    act.wait_ge(h_nt, h + 1)
                    a.activation(onT[:, h, :], ps[:, 4 + h % 2, 0:T], ACT.Copy, scale=hgw[:, h:h + 1]).then_inc(h_nc, 1)

            @block.vector
            def _(dve):
                v = nc.vector
                dstep.on(dve)
                v.tensor_tensor(lb4[:, 0, :], lbv, lbv, ALU.subtract).then_inc(h_lb, 1)
                dve.wait_ge(h_lb, 2)
                dstep(v.reciprocal(lb4[:, 2, :], lb4[:, 1, :]))
                dstep(v.tensor_tensor(lb4[:, 3, :], lb4[:, 1, :], lb4[:, 2, :], ALU.mult))
                dstep(v.tensor_tensor(lb4[:, 0, :], lb4[:, 3, :], lb4[:, 3, :], ALU.subtract))
                dstep(v.tensor_scalar(lb4[:, 1, :], lb4[:, 0, :], -1.0, 1.0, ALU.mult, ALU.add))
                for h in range(HH):
                    dve.wait_ge(h_c, HH + h + 1)
                    dstep(v.tensor_scalar(eT[:, h, :], eT[:, h, :], lb4[:, 1, h:h + 1], lb4[:, 0, h:h + 1], ALU.mult, ALU.add))
                dstep(v.tensor_scalar(kT[:], eT[:], -1.0, 1.0, ALU.mult, ALU.add))
                v.tensor_scalar(eT[:], eT[:], FMIN, None, ALU.max).then_inc(h_f, 1)
                dve.wait_ge(h_ln, 1)
                for h in range(HH):
                    last = v.tensor_tensor_scan(eT[:, h, :], keep[:], bT[:, h, :], 0.0, ALU.mult, ALU.add)
                dstep(last)
                for x, at32, at4 in ((mid, CH // 2 - 1, 1), (lst, CH - 1, NS - 1)):
                    dstep(v.tensor_copy(x[:, :, 0:8].unsqueeze(3), chunks32(eT)[:, :, :, at32:at32 + 1]))
                    dstep(v.tensor_copy(x[:, :, 8:16].unsqueeze(3), chunks4(eT)[:, :, :, at4:at4 + 1]))
                dstep(v.tensor_tensor(chunks32(bT), chunks32(eT), mid[:, :, 0:8].unsqueeze(3).broadcast_to([P, HH, 8, CH]), ALU.subtract))
                dstep(v.tensor_tensor(chunks4(bT), chunks4(eT), mid[:, :, 8:16].unsqueeze(3).broadcast_to([P, HH, 8, NS]), ALU.subtract))
                v.tensor_scalar(eT[:], bT[:], -1.0, EXPMAX, ALU.mult, ALU.min).then_inc(h_ek, 1)
                dve.wait_ge(h_ek, 1)
                v.tensor_scalar(bT[:], bT[:], EXPMAX, None, ALU.min).then_inc(h_eq, 1)
                dstep(v.tensor_tensor(dl[:], lst[:], mid[:], ALU.subtract))
                v.tensor_tensor(gate[:, :, 0:7], dl[:, :, 0:7], mid[:, :, 1:8], ALU.add).then_inc(h_xe, 1)
                v.tensor_copy(gate[:, :, 7:8], dl[:, :, 7:8]).then_inc(h_xe, 1)
                dstep(v.memset(hss[:], 1.0))
                dve.wait_ge(h_x, 1)
                v.tensor_tensor(kT[:], kT[:], eT[:], ALU.mult).then_inc(h_k, 1)
                dve.wait_ge(h_x, 2)
                v.tensor_tensor(qT[:], qT[:], bT[:], ALU.mult).then_inc(h_k, 1)
                dve.wait_ge(h_x, 6)
                dve.wait_ge(h_k, 2)
                v.tensor_tensor(qs[:].rearrange("p h (c s) -> p h c s", s=NS), chunks4(qT), mid[:, :, 8:16].unsqueeze(3)
                                .broadcast_to([P, HH, 8, NS]), ALU.mult).then_inc(h_k, 1)
                v.tensor_tensor(chunks4(eT), chunks4(kT), dl[:, :, 8:16].unsqueeze(3).broadcast_to([P, HH, 8, NS]), ALU.mult).then_inc(h_k, 1)
                dve.wait_ge(h_k, 4)
                v.tensor_tensor(qsm[:], qs[:].unsqueeze(1).broadcast_to([P, NB, HH, 32]),
                                cm8[:].unsqueeze(2).broadcast_to([P, NB, HH, 32]), ALU.mult).then_inc(h_k, 1)
                dve.wait_ge(h_c, NPROJ)
                dstep(v.memset(U[0][:], 0.0))
                for t in range(2):
                    dve.wait_ge(h_sc, t + 1)
                    v.tensor_tensor(scm[:, t, :].rearrange("p (h s) -> p h s", s=CH), ps[:, 4 + t, 0:256].rearrange("p (h s) -> p h s", s=CH),
                                    cmask[:].unsqueeze(1).broadcast_to([P, HH, CH]), ALU.mult).then_inc(h_sm, 1)
                dve.wait_ge(h_sc, 3)
                v.tensor_tensor(scs[:], ps[:, 5, 256:320].rearrange("p (c s) -> p c s", s=32),
                                sm4[:].unsqueeze(1).broadcast_to([P, 2, 32]), ALU.mult).then_inc(h_sm, 1)
                for c in range(8):
                    dve.wait_ge(h_P, c + 1)
                    if c >= 1:
                        dve.wait_ge(h_o, c)
                    b0, o, n = 2 * (c % 2), U[c % 2], U[(c + 1) % 2]
                    dstep(v.tensor_tensor(n[:].rearrange("p (b h) v -> p b (h v)", b=2), o[:].rearrange("p (b h) v -> p b (h v)", b=2),
                                          ps[:, b0:b0 + 2, :], ALU.add))
                    v.tensor_tensor(n[:], n[:], gate[:, :, c:c + 1].broadcast_to([P, HH, P]), ALU.mult).then_inc(h_U, 1)
                    dve.wait_ge(h_U, c + 1)
                heads = []
                for t in range(2):
                    heads.append((otok[:, t, :].rearrange("p (h v) -> p h v", v=P), gtok[:, t, :].rearrange("p (h v) -> p h v", v=P),
                                  hss[:, HH * t:HH * t + HH], HH))
                heads.append((ots[:], gts[:], hss[:, 2 * HH:2 * HH + 2], 2))
                for t, (o, _, hs, n) in enumerate(heads):
                    if t < 2:
                        dve.wait_ge(h_oc, t + 1)
                    else:
                        dve.wait_ge(h_oic, 1)
                    dstep(v.tensor_tensor(sq3[:, 0:n * P].rearrange("p (h v) -> p h v", v=P), o, o, ALU.mult))
                    dstep(v.tensor_reduce(hs, sq3[:, 0:n * P].rearrange("p (h v) -> p h v", v=P), AX_X, ALU.add))
                v.tensor_scalar(hss[:], hss[:], 1.0 / P, RMS_EPS, ALU.mult, ALU.add).then_inc(n_rs, 1)
                dve.wait_ge(n_sq, 2)
                dstep(v.reciprocal(hss[:], hss[:]))
                for o, gt, hs, n in heads:
                    dstep(v.tensor_tensor(o, o, hs.unsqueeze(2).broadcast_to([P, n, P]), ALU.mult))
                    v.tensor_tensor(o, o, gt, ALU.mult).then_inc(h_n, 1)
                for j in range(4):
                    c, half = j // 2, j % 2
                    dve.wait_ge(h_su, j + 1)
                    dve.wait_ge(h_sd, 4 * c + 4)
                    s = Sb[:, 4 * half:4 * half + 4, 4 * c:4 * c + 4, :].rearrange("p b h v -> p h b v")
                    v.tensor_tensor(s, s, ps[:, 4 * half:4 * half + 4, :].rearrange("p h (b v) -> p h b v", b=4), ALU.add).then_inc(h_sa, 1)

            @block.tensor
            def _(pe):
                m = nc.tensor

                def columns(i, n, first=False):
                    pe.wait_ge(s_w[n], i * 16 + (w_z + 16))
                    for mt in range(4):
                        if not first:
                            pe.wait_ge(h_c, i * 8 + (4 * n + mt - 3))
                        for k in range(KD):
                            last = m.matmul(ps[:, 4 + mt, 0:T], ring[n][:, k, mt * P:(mt + 1) * P], xT[:, k, :],
                                            start=(k == 0), stop=(k == KD - 1))
                        last.then_inc(h_p, 1)

                columns(0, 0, True)
                columns(0, 1)
                columns(1, 0)
                columns(1, 1)
                for c in range(4):
                    n = c % 2
                    pe.wait_ge(s_w[n], w_z + 16 * (c // 2 + 3))
                    for t, (t0, rows) in enumerate(TILES):
                        j = 3 * c + t
                        pe.wait_ge(h_c, 2 * HH + j - 3)
                        product(ps[:, 4 + j % 4, :], lambda k: xT[:, k, t0:t0 + rows], lambda k: ring[n][:, k, :], rows).then_inc(h_p, 1)
                pe.wait_ge(h_k, 4)
                for j in range(4):
                    for c in range(4):
                        last = m.transpose(ps[:, j, c * P:(c + 1) * P], kT[:, 4 * (j % 2) + c, P * (j // 2):P * (j // 2) + P], ident[:])
                    last.then_inc(h_kt, 1)
                bands = [slice(32 * i, 32 * i + 32) for i in range(4)]
                pe.wait_ge(h_kc, 1)
                for h in range(HH):
                    last = m.matmul(ps[bands[h % 4], 0, P * (h // 4):P * (h // 4) + P], eT[:, h, SEQ:T], ident[:], start=True, stop=True)
                last.then_inc(h_kt, 1)
                pe.wait_ge(h_c, NPROJ)
                for t in range(2):
                    for h in range(HH):
                        for r in range(4):
                            s = slice(P * t + CH * r, P * t + CH * r + CH)
                            last = m.matmul(ps[CH * r:CH * r + CH, 4 + t, CH * h:CH * h + CH], kT[:, h, s], qT[:, h, s], start=True, stop=True)
                    last.then_inc(h_sc, 1)
                pe.wait_ge(h_sm, 2)
                for h in range(HH):
                    last = m.matmul(ps[bands[h % 4], 5, 256 + 32 * (h // 4):288 + 32 * (h // 4)], kT[:, h, SEQ:T], qT[:, h, SEQ:T], start=True, stop=True)
                last.then_inc(h_sc, 1)
                pe.wait_ge(h_S, 16 * NB)
                pe.wait_ge(h_k, 5)
                pe.wait_ge(h_sm, 3)
                for c in range(2):
                    out = slice(P * (2 + c), P * (3 + c))
                    for b in range(NB):
                        for i in range(4):
                            m.matmul(ps[bands[i], 4, out], qsm[:, b, 4 * c + i, :], Sb[:, b, 4 * c + i, :], start=(b == 0), stop=False)
                    for i in range(4):
                        last = m.matmul(ps[bands[i], 4, out], scs[bands[i], c, :], vts[bands[i], c, :], start=False, stop=True,
                                        tile_position=(32 * i, 32 * i))
                last.then_inc(h_oi, 1)

                def chunk_sum(c):
                    r = slice(CH * (c % 4), CH * (c % 4) + CH)
                    if c >= 2:
                        pe.wait_ge(h_U, c - 1)
                    for h in range(HH):
                        last = m.matmul(ps[:, 2 * (c % 2) + h // 4, (h % 4) * P:(h % 4 + 1) * P], kpt[r, c // 4, h * P:(h + 1) * P],
                                        vtok[r, c // 4, h * P:(h + 1) * P], start=True, stop=True)
                    last.then_inc(h_P, 1)

                pe.wait_ge(h_kc, 5)
                chunk_sum(0)
                for c in range(8):
                    if c + 1 < 8:
                        chunk_sum(c + 1)
                    t, r = c // 4, slice(CH * (c % 4), CH * (c % 4) + CH)
                    if c == 4:
                        pe.wait_ge(h_oc, 1)
                    if c > 0:
                        pe.wait_ge(h_U, c)
                    for h in range(HH):
                        o = ps[r, 6 + h // 4, (h % 4) * P:(h % 4 + 1) * P]
                        last = m.matmul(o, scm[r, t, CH * h:CH * h + CH], vtok[r, t, h * P:(h + 1) * P], start=True, stop=(c == 0),
                                        tile_position=(CH * (c % 4), CH * (c % 4)))
                        if c > 0:
                            last = m.matmul(o, qT[:, h, CH * c:CH * c + CH], U[c % 2][:, h, :], start=False, stop=True)
                    last.then_inc(h_o, 1)
                def state_sum(j):
                    c, half = j // 2, j % 2
                    pe.wait_ge(h_vm, c + 1)
                    for i in range(4):
                        last = m.matmul(ps[:, 4 * half + i, :], kps[bands[i], c, :], vm[c][bands[i], 4 * half:4 * half + 4, :].rearrange("p b v -> p (b v)"),
                                        start=True, stop=True, tile_position=(32 * i, 0))
                    last.then_inc(h_su, 1)

                pe.wait_ge(h_U, 8)
                state_sum(0)
                pe.wait_ge(h_oc, 2)
                pe.wait_ge(h_oic, 1)
                pe.wait_ge(h_n, 3)
                for h in range(HH):
                    if h >= 2:
                        pe.wait_ge(h_nc, h - 1)
                    for t in range(2):
                        m.transpose(ps[:, 4 + h % 2, P * t:P * t + P], otok[:, t, h * P:(h + 1) * P], ident[:])
                    band = bands[h % 4]
                    m.matmul(ps[:, 4 + h % 2, SEQ:T], ots[band, h // 4, :], ident[band, band], start=True, stop=True,
                             tile_position=(32 * (h % 4), 0)).then_inc(h_nt, 1)
                pe.wait_ge(h_nc, HH)
                for j in range(1, 4):
                    if j >= 2:
                        pe.wait_ge(h_sa, j - 1)
                    state_sum(j)

        if stop <= 4:
            return
        wSSD = at("wSSD", 32, [P, XT_, D])
        wHG = at("wHG", 154, [P, KD, D])
        wOUT = at("wOUT", 0, [P, KD, D])
        gA = at("gA", 186, [P, KD, T])
        gB = at("gB", 195.25, [P, KD, T])
        mT = at("mT", 116, [P, KD, T])
        tmpA = [at(f"tmpA{i}", 204.5 + 1.25 * i, [P, T]) for i in range(2)]
        lnw = at("lnw", 125.5, [P, D])
        lnb = at("lnb", 129.5, [P, D])
        lnq = at("lnq", 133.5, [P, D])
        lst4 = at("lst4", 137.5, [P, 3, 8])
        lmu = at("lmu", 137.625, [P, 3])
        lvar = at("lvar", 137.75, [P, 3])

        w_g = w_z + 16 * (4 * D // CW // 2)
        g_ws, g_wh, g_wo, g_ln = S("ssd_proj_loaded"), S("hg_proj_loaded"), S("w_out_loaded"), S("ln_loaded")
        g_p, g_c = S("output_gate_ready"), S("output_gate_copied")
        g_ab, g_m = S("branches_ready"), S("merged_ready")
        g_mx, g_x = S("mix_ready"), S("residual_added")
        ln_c, ln_v, ln_r, ln_s = S("ln_mean_ready"), S("ln_squares_ready"), S("ln_variance_ready"), S("ln_rooted")
        ln_done = S("ln_done")

        def ln_vector(dve, dstep, n):
            v = nc.vector
            dstep(v.tensor_reduce(lmu[:], lst4[:], AX_X, ALU.add))
            v.tensor_scalar(lmu[:], lmu[:], -1.0 / D, None, ALU.mult).then_inc(ln_c, 1)
            dve.wait_ge(ln_c, n)
            for t, (_, rows) in enumerate(TILES):
                x = xtok[0:rows, t, :]
                dve.wait_ge(ln_v, 3 * (n - 1) + t + 1)
                dstep(v.scalar_tensor_tensor(x, x, lmu[0:rows, t:t + 1], lnw[0:rows, :], ALU.add, ALU.mult))
            v.tensor_scalar(lvar[:], lvar[:], 1.0 / D, LN_EPS, ALU.mult, ALU.add).then_inc(ln_r, 1)
            dve.wait_ge(ln_s, n)
            dstep(v.reciprocal(lvar[:], lvar[:]))
            for t, (_, rows) in enumerate(TILES):
                x = xtok[0:rows, t, :]
                v.scalar_tensor_tensor(x, x, lvar[0:rows, t:t + 1], lnb[0:rows, :], ALU.mult, ALU.add).then_inc(ln_done, 1)

        def ln_scalar(act, n):
            for t, (_, rows) in enumerate(TILES):
                act.wait_ge(ln_c, n)
                if t > 0 or n > 1:
                    act.wait_ge(ln_v, 3 * (n - 1) + t)
                nc.scalar.activation(lnq[0:rows, :], xtok[0:rows, t, :], ACT.Square, bias=lmu[0:rows, t:t + 1], accum_out=lvar[0:rows, t:t + 1]).then_inc(ln_v, 1)
            act.wait_ge(ln_r, n)
            nc.scalar.activation(lvar[:], lvar[:], ACT.Sqrt).then_inc(ln_s, 1)

        with nc.Block() as block:
            @block.sync
            def _(sp):
                for n in range(2):
                    sp.dma_start(ring[n][:], chunk_src(C_GA + n * CW)).then_inc(s_w[n], 16)
                for b in range(NB):
                    sp.dma_start(o_hg_s[0, b].rearrange("h k v -> k h v"), Sb[:, b]).then_inc(s_out, 16)
                sp.wait_ge(s_out, 48 + 16 * (NB + 1))
                sp.dma_start(wHG[:], hg_proj[0].rearrange("(k p) n -> p k n", p=P)).then_inc(g_wh, 16)
                for n in range(2):
                    sp.wait_ge(g_p, 4 * n + 4)
                    sp.dma_start(ring[n][:], chunk_src(C_GB + n * CW)).then_inc(s_w[n], 16)
                sp.dma_start(wSSD[:], ssd_proj[0].rearrange("(k p) n -> p k n", p=P)).then_inc(g_ws, 16)
                sp.wait_ge(g_p, 16)
                sp.dma_start(wOUT[:], w_out[0].rearrange("(k p) n -> p k n", p=P)).then_inc(g_wo, 16)
                sp.wait_ge(g_ab, KD)
                sp.dma_start(lnw[:], row(ln1_g[0])).then_inc(g_ln, 16)
                sp.dma_start(lnb[:], row(ln1_b[0])).then_inc(g_ln, 16)

            @block.scalar
            def _(act):
                for dst, first in ((gA, 0), (gB, KD)):
                    with act.Fori(0, 2) as i:
                        for n in range(4):
                            act.wait_ge(g_p, i * 4 + (first + n + 1))
                            nc.scalar.activation(dst[:, bass.ds(i * 4 + n, 1), :], ps[:, 4 + n:5 + n, 0:T], ACT.Sigmoid).then_inc(g_c, 1)
                ln_scalar(act, 1)

            @block.vector
            def _(dve):
                v = nc.vector
                dstep.on(dve)
                for c in range(KD):
                    dve.wait_ge(g_ab, c + 1)
                    if c == 0:
                        dve.wait_ge(g_c, 2 * KD)
                    if c >= 2:
                        dve.wait_ge(g_m, c - 1)
                    b = 2 * (c % 2)
                    dstep(v.tensor_tensor(tmpA[c % 2][:], ps[:, b, 0:T], gA[:, c, :], ALU.mult))
                    dstep(v.tensor_tensor(mT[:, c, :], ps[:, b + 1, 0:T], gB[:, c, :], ALU.mult))
                    v.tensor_tensor(mT[:, c, :], mT[:, c, :], tmpA[c % 2][:], ALU.add).then_inc(g_m, 1)
                v.memset(lvar[:], 1.0)
                dstep(v.memset(lst4[:], 0.0))
                for j in range(6):
                    t, n, rows = j // 2, j % 2, TILES[j // 2][1]
                    dve.wait_ge(g_mx, j + 1)
                    for i, (pr, pc, cols) in enumerate(pieces(rows)):
                        x = xtok[0:rows, t, 512 * n:512 * n + 512][:, cols]
                        last = v.scalar_tensor_tensor(x, x, ALPHA, ps[pr, 4 + j % 4, pc], ALU.mult, ALU.add,
                                                      accum_out=lst4[0:rows, t, 4 * n + i:4 * n + i + 1])
                    last.then_inc(g_x, 1)
                dve.wait_ge(g_x, 6)
                dve.wait_ge(g_ln, 32)
                ln_vector(dve, dstep, 1)

            @block.tensor
            def _(pe):
                m = nc.tensor
                for c in range(4):
                    pe.wait_ge(s_w[c % 2], w_g + 16 * (c // 2 + 1))
                    for mt in range(4):
                        if c > 0:
                            pe.wait_ge(g_c, 4 * c + mt - 3)
                        for k in range(KD):
                            last = m.matmul(ps[:, 4 + mt, 0:T], ring[c % 2][:, k, mt * P:(mt + 1) * P], xT[:, k, :],
                                            start=(k == 0), stop=(k == KD - 1))
                        last.then_inc(g_p, 1)
                pe.wait_ge(g_wh, 16)
                pe.wait_ge(g_ws, 16)
                for c in range(KD):
                    if c >= 2:
                        pe.wait_ge(g_m, c - 1)
                    b, cols = 2 * (c % 2), slice(c * P, (c + 1) * P)
                    for k in range(HH):
                        m.matmul(ps[:, b, 0:T], wHG[:, k, cols], onT[:, k, :], start=(k == 0), stop=(k == HH - 1))
                    for k in range(XT_):
                        last = m.matmul(ps[:, b + 1, 0:T], wSSD[:, k, cols], ynT[:, k, :], start=(k == 0), stop=(k == XT_ - 1))
                    last.then_inc(g_ab, 1)
                pe.wait_ge(g_wo, 16)
                pe.wait_ge(g_m, KD)
                pe.wait_ge(g_c, 2 * KD)
                for j in range(6):
                    (t0, rows), n = TILES[j // 2], j % 2
                    if j >= 4:
                        pe.wait_ge(g_x, j - 3)
                    product(ps[:, 4 + j % 4, :], lambda k: mT[:, k, t0:t0 + rows], lambda k: wOUT[:, k, 512 * n:512 * n + 512], rows).then_inc(g_mx, 1)

        if stop <= 5:
            return
        yacc = at("yacc", 154, [P, 3, D])
        psel = at("psel", 166, [P, 3, BLK])
        gsel = at("gsel", 167, [P, 3, 2, BLK])
        xs = at("xs", 170, [P, CW])
        xe = at("xe", 172, [P, 4, 2, BLK])
        gl = at("gl", 174, [P, CW])
        up = at("up", 176, [P, CW])
        sg = at("sg", 178, [P, CW])
        av_ = at("act_values", 180, [P, CW])
        aT = at("aT", 182, [P, 4, 2, BLK])
        ysb = at("ysb", 184, [P, CW])
        gT = at("gT", 152, [P, 3 * P])
        esel = at("esel", 153.5, [P, BLK])
        dsel = at("dsel", 153.75, [P, 3])
        boff = at("boff", 153.875, [P, 1])
        dest = at("dest", 187, [P, 3, E_])
        gm = at("gm", 187.5, [P, 3, E_])
        tab = at("tab", 188, [1, 96], I32)
        TAB_N = 64
        hT_ = at("h_T", 116, [P, KD, T])
        wr = at("wr", 189, [P, KD, E_])
        rbr = at("rbr", 190, [P, E_])
        lg = at("lg", 190.25, [P, 3, E_])
        mx8 = at("mx8", 190.75, [P, 3, 8])
        ix8 = at("ix8", 191, [P, 3, 8], U32)
        gt4 = at("gt4", 191.25, [P, 3, TOPK])
        id4 = at("id4", 191.375, [P, 3, TOPK])
        gsum = at("gsum", 191.5, [P, 3])
        msk = at("msk", 188.5, [P, 3, E_])
        eq = at("eq", 192, [P, 3, TOPK, E_])
        eg = at("eg", 193.5, [P, 3, TOPK, E_])
        cum = at("cum", 195, [P, 3, E_])
        cnt = at("cnt", 195.5, [P, E_])
        nbl = at("nbl", 195.75, [P, E_])
        binc = at("binc", 196, [P, E_])
        st64 = at("st64", 196.25, [P, E_])
        ebc = at("ebc", 196.5, [P, 1])
        gmT = at("gmT", 197, [E_, T])
        bgr = at("bgr", 198.25, [P, 2 * D])
        bdr = at("bdr", 148, [E_, D])

        wq = [at(f"wGU{i}", 16 * i, [P, 2, 2 * D]) for i in range(4)]
        wd_ = [at(f"wD{i}", 64 + 16 * i, [P, 4, D]) for i in range(2)]
        wodd = [at(f"wGUodd{i}", 116 + 16 * i, [P, 2, 2 * D]) for i in range(2)]
        m_w = [S(f"expert_piece_loaded{i}") for i in range(6)]
        m_wo = [S(f"odd_expert_piece_loaded{i}") for i in range(2)]
        m_re = S("first_expert_reloaded")

        def load_piece(sp, e, i, sem, odd=False):
            src, n = (w_gu, 256) if i < 4 else (w_down, 512)
            dst, k = (wq[i], i) if i < 4 else (wd_[i - 4], i - 4)
            if odd:
                dst = wodd[i]
            sp.dma_start(dst[:], src[0, bass.ds(e, 1), n * k:n * k + n, :].rearrange("a (k p) n -> p (a k) n", p=P)).then_inc(sem, 16)

        t_wr, t_b, t_ht, t_hc = S("router_loaded"), S("expert_biases_loaded"), S("h_transposed"), S("h_copied")
        t_lg, t_e, t_ex, t_mk = S("logits_ready"), S("top_values_ready"), S("top_exp_ready"), S("choices_ready")
        t_cm, t_eb, t_tb = S("token_counts_ready"), S("block_experts_ready"), S("block_table_row")
        t_bz, t_gt, t_gc = S("padding_cleared"), S("gates_transposed"), S("gates_copied")
        t_y, t_yc = S("bias_sum_ready"), S("bias_sum_copied")

        with nc.Block() as block:
            @block.sync
            def _(sp):
                sp.dma_start(wr[:], router_w[0].rearrange("(k p) n -> p k n", p=P)).then_inc(t_wr, 16)
                sp.dma_start(rbr[:], row(router_b[0])).then_inc(t_wr, 16)
                sp.dma_start(bdr[:], b_down[0]).then_inc(t_b, 16)
                sp.wait_ge(t_bz, 1)
                sp.dma_start(bgr[0:E_, :], b_gu[0]).then_inc(t_b, 16)
                for i in range(6):
                    load_piece(sp, 0, i, m_w[i])

            @block.scalar
            def _(act):
                a = nc.scalar
                for k in range(KD):
                    act.wait_ge(t_ht, k + 1)
                    a.copy(hT_[:, k, :], ps[:, k % 2, 0:T]).then_inc(t_hc, 1)
                act.wait_ge(t_e, 1)
                a.activation(gt4[:], gt4[:], ACT.Exp).then_inc(t_ex, 1)
                act.wait_ge(t_gt, 1)
                a.copy(gmT[:], ps[0:E_, 0, 0:T]).then_inc(t_gc, 1)

            @block.vector
            def _(dve):
                v = nc.vector
                dstep.on(dve)
                v.memset(bgr[:], 0.0).then_inc(t_bz, 1)
                v.memset(mx8[:], 0.0)
                v.memset(cum[:], 0.0)
                dstep(v.memset(ix8[:], 0))
                dve.wait_ge(t_wr, 32)
                dve.wait_ge(t_lg, 1)
                for t, (_, rows) in enumerate(TILES):
                    dstep(v.tensor_tensor(lg[0:rows, t, :], ps[0:rows, 2, 32 * t:32 * t + 32], rbr[0:rows, :], ALU.add))
                    dstep(v.max(mx8[0:rows, t, :], lg[0:rows, t, :]))
                    dstep(v.max_index(ix8[0:rows, t, :], mx8[0:rows, t, :], lg[0:rows, t, :]))
                v.tensor_tensor(gt4[:], mx8[:, :, 0:TOPK], mx8[:, :, 0:1].broadcast_to([P, 3, TOPK]), ALU.subtract).then_inc(t_e, 1)
                dstep(v.tensor_copy(id4[:], ix8[:, :, 0:TOPK]))
                dve.wait_ge(t_ex, 1)
                dstep(v.tensor_reduce(gsum[:], gt4[:], AX_X, ALU.add))
                dstep(v.reciprocal(gsum[:], gsum[:]))
                dstep(v.tensor_tensor(gt4[:], gt4[:], gsum[:].unsqueeze(2).broadcast_to([P, 3, TOPK]), ALU.mult))
                dstep(v.tensor_tensor(eq[:], ecol[:].unsqueeze(1).unsqueeze(1).broadcast_to([P, 3, TOPK, E_]),
                                      id4[:].unsqueeze(3).broadcast_to([P, 3, TOPK, E_]), ALU.is_equal))
                dstep(v.tensor_tensor(eg[:], eq[:], gt4[:].unsqueeze(3).broadcast_to([P, 3, TOPK, E_]), ALU.mult))
                v.tensor_reduce(msk[:], eq[:].rearrange("p t k e -> p t e k"), AX_X, ALU.add).then_inc(t_mk, 1)
                v.tensor_reduce(gm[:], eg[:].rearrange("p t k e -> p t e k"), AX_X, ALU.add).then_inc(t_mk, 1)
                dve.wait_ge(t_cm, 1)
                for t, (_, rows) in enumerate(TILES):
                    v.tensor_copy(cum[0:rows, t, :], ps[0:rows, 2, 128 + 32 * t:160 + 32 * t])
                dstep(v.tensor_copy(cnt[:], ps[:, 2, 224:256]))
                dstep(v.tensor_scalar(nbl[:], cnt[:], 0.0, None, ALU.is_gt))
                for j in range(1, (T + BLK - 1) // BLK):
                    dstep(v.scalar_tensor_tensor(nbl[:], cnt[:], float(BLK * j), nbl[:], ALU.is_gt, ALU.add))
                dstep(v.tensor_tensor_scan(binc[:], ones[:, 0:E_], nbl[:], 0.0, ALU.mult, ALU.add))
                dstep(v.tensor_tensor(st64[:], binc[:], nbl[:], ALU.subtract))
                dstep(v.tensor_scalar(st64[:], st64[:], float(BLK), None, ALU.mult))
                dstep(v.tensor_tensor(dest[:], cum[:], st64[:].unsqueeze(1).broadcast_to([P, 3, E_]), ALU.add))
                dve.wait_ge(t_mk, 2)
                dstep(v.tensor_tensor(dest[:], dest[:], msk[:], ALU.mult))
                dstep(v.tensor_scalar(dest[:], dest[:], -1.0, None, ALU.add))
                dstep(v.tensor_scalar(lg[:, 0, :], binc[:], prow[:, 0:1], None, ALU.is_le))
                dstep(v.tensor_reduce(ebc[:], lg[:, 0, :], AX_X, ALU.add))
                v.tensor_scalar(ebc[:], ebc[:], float(E_ - 1), None, ALU.min).then_inc(t_eb, 1)
                dve.wait_ge(t_tb, 1)
                v.tensor_copy(tab[0:1, 0:64], ps[0:1, 2, 256:320])
                v.tensor_scalar(tab[0:1, TAB_N:TAB_N + 1], binc[0:1, E_ - 1:E_], -1.0, None, ALU.add)

            @block.tensor
            def _(pe):
                m = nc.tensor
                for k in range(KD):
                    if k >= 2:
                        pe.wait_ge(t_hc, k - 1)
                    for t, (t0, rows) in enumerate(TILES):
                        last = m.transpose(ps[:, k % 2, t0:t0 + rows], xtok[0:rows, t, k * P:(k + 1) * P], ident[0:rows, 0:rows])
                    last.then_inc(t_ht, 1)
                pe.wait_ge(t_hc, KD)
                pe.wait_ge(t_wr, 32)
                for t, (t0, rows) in enumerate(TILES):
                    for k in range(KD):
                        last = m.matmul(ps[0:rows, 2, 32 * t:32 * t + 32], hT_[:, k, t0:t0 + rows], wr[:, k, :], start=(k == 0), stop=(k == KD - 1))
                last.then_inc(t_lg, 1)
                pe.wait_ge(t_mk, 2)
                for o, lhs in ((128, (tri,)), (160, (ones, tri)), (192, (ones, ones, tri)), (224, (ones, ones, ones))):
                    rows = 32 if o == 192 else P
                    for t, l in enumerate(lhs):
                        kk = TILES[t][1]
                        last = m.matmul(ps[0:rows, 2, o:o + 32], l[0:kk, 0:rows], msk[0:kk, t, :], start=(t == 0), stop=(t == len(lhs) - 1))
                last.then_inc(t_cm, 1)
                for t, (t0, rows) in enumerate(TILES):
                    last = m.transpose(ps[0:E_, 0, t0:t0 + rows], gm[0:rows, t, :], ident[0:rows, 0:rows])
                last.then_inc(t_gt, 1)
                pe.wait_ge(t_eb, 1)
                m.matmul(ps[0:1, 2, 256:320], ebc[0:64, 0:1], ident[0:64, 0:64], start=True, stop=True).then_inc(t_tb, 1)

        if stop <= 6:
            return
        m_f = S("expert_piece_used")
        m_p, m_g = S("block_tokens_selected"), S("block_gates_selected")
        m_x, m_xs, m_xt, m_xc = S("block_gathered"), S("block_copied"), S("block_transposed"), S("block_transposed_copied")
        m_u = S("gate_up_ready")
        m_gl, m_sg, m_a = S("gate_limited"), S("gate_sigmoid_ready"), S("activation_ready")
        m_at, m_ac = S("activation_transposed"), S("activation_copied")
        m_gt, m_gc = S("block_gates_transposed"), S("block_gates_copied")
        m_yc = S("block_output_copied")
        m_s, m_sa = S("scattered"), S("scattered_added")
        PER = 4
        B_X, B_XT, B_G, B_U, B_Y, B_S = 0, 1, 2, 3, 4, 5
        B_GT, B_AT = B_S, B_S + 1

        with nc.Block() as block:
            @block.sync
            def _(sp):
                e = sp.value_load(tab[0:1, 0:1], min_val=0, max_val=E_ - 1)
                with sp.If(e > 0):
                    for i in range(6):
                        sp.wait_ge(m_w[i], 16)
                        load_piece(sp, e, i, m_re)
                    sp.wait_ge(m_re, 16 * 6)

        with nc.Block() as block:
            def last_block(eng):
                return eng.value_load(tab[0:1, TAB_N:TAB_N + 1], min_val=0, max_val=NBLK - 1)

            def expert(eng, b):
                return eng.value_load(tab[0:1, bass.ds(b, 1)], min_val=0, max_val=E_ - 1)

            @block.sync
            def _(sp):
                end = last_block(sp)

                def first_two(b, c, odd):
                    e = expert(sp, b)
                    for i in range(2):
                        if c is not None:
                            sp.wait_ge(m_f, c * 6 + (i + 1))
                        load_piece(sp, e, i, (m_wo if odd else m_w)[i], odd)

                with sp.If(end > 0):
                    first_two(1, None, True)
                with sp.Fori(0, (NBLK - 1) // 2) as i2:
                    for odd in (0, 1):
                        c = i2 * 2 + odd
                        with sp.If(c < end):
                            e = expert(sp, c + 1)
                            for i in range(2, 6):
                                sp.wait_ge(m_f, c * 6 + (i + 1))
                                load_piece(sp, e, i, m_w[i])
                        with sp.If(c + 1 < end):
                            first_two(c + 2, c, odd == 1)

            @block.scalar
            def _(act):
                a = nc.scalar
                end = last_block(act)
                act.wait_ge(m_x, 1)
                a.copy(xs[:], ps[:, B_X, :]).then_inc(m_xs, 1)
                act.wait_ge(m_xt, 1)
                a.copy(xe[:].rearrange("p f h j -> p (f h j)"), ps[:, B_XT, :]).then_inc(m_xc, 1)

                def run(b, c):
                    act.wait_ge(m_gl, b + 1)
                    a.activation(sg[:], gl[:], ACT.Sigmoid, scale=SALPHA).then_inc(m_sg, 1)
                    act.wait_ge(m_x, b + 2)
                    a.copy(xs[:], ps[:, B_X, :]).then_inc(m_xs, 1)
                    if c is not None:
                        act.wait_ge(m_s, b * 6)
                    act.wait_ge(m_gt, b + 1)
                    a.copy(gT[:, 0:T], ps[:, B_GT, 0:T]).then_inc(m_gc, 1)
                    act.wait_ge(m_u, b + 1)
                    act.wait_ge(m_xt, b + 2)
                    a.copy(xe[:].rearrange("p f h j -> p (f h j)"), ps[:, B_XT, :]).then_inc(m_xc, 1)
                    act.wait_ge(m_at, b + 1)
                    a.copy(aT[:].rearrange("p f h j -> p (f h j)"), ps[:, B_AT, :]).then_inc(m_ac, 1)
                    act.wait_ge(m_f, b * 6 + 6)
                    a.copy(ysb[:], ps[:, B_Y, :]).then_inc(m_yc, 1)

                run(0, None)
                for j in range(6):
                    rows = TILES[j // 2][1]
                    act.wait_ge(t_y, j + 1)
                    a.copy(yacc[0:rows, j // 2, 512 * (j % 2):512 * (j % 2) + 512], ps[0:rows, B_S + j % 3, :]).then_inc(t_yc, 1)
                with act.Fori(0, NBLK - 1) as c:
                    with act.If(c < end):
                        run(c + 1, c)

            @block.vector
            def _(dve):
                v = nc.vector
                dstep.on(dve)
                end = last_block(dve)
                v.memset(gT[:, T:3 * P], 0.0).then_inc(t_bz, 1)
                dstep(v.memset(boff[:], 0.0))

                def tokens(e):
                    dstep(v.tensor_scalar(dsel[:].unsqueeze(2), dest[:, :, bass.ds(e, 1)], boff[:, 0:1], None, ALU.subtract))
                    v.tensor_tensor(psel[:], jcol[:].unsqueeze(1).broadcast_to([P, 3, BLK]), dsel[:].unsqueeze(2).broadcast_to([P, 3, BLK]),
                                    ALU.is_equal).then_inc(m_p, 1)

                def add(j, n):
                    rows = TILES[j // 2][1]
                    y = yacc[0:rows, j // 2, 512 * (j % 2):512 * (j % 2) + 512]
                    dve.wait_ge(m_s, n + (j + 1))
                    v.tensor_tensor(y, y, ps[0:rows, B_S + j % 3, :], ALU.add).then_inc(m_sa, 1)

                def run(b, c):
                    e = expert(dve, b)
                    if c is not None:
                        dve.wait_ge(m_gt, b)
                        dve.wait_ge(m_u, b)
                    dve.wait_ge(m_p, b + 1)
                    v.tensor_tensor(gsel[:], psel[:].unsqueeze(2).broadcast_to([P, 3, 2, BLK]),
                                    gm[:, :, bass.ds(e, 1)].unsqueeze(3).broadcast_to([P, 3, 2, BLK]), ALU.mult).then_inc(m_g, 1)
                    v.tensor_copy(esel[:], ident[:, bass.ds(e, 1)].broadcast_to([P, BLK])).then_inc(m_g, 1)
                    dstep(v.tensor_scalar(boff[:], boff[:], float(BLK), None, ALU.add))
                    dve.wait_ge(m_x, b + 1)
                    dve.wait_ge(m_g, b * 2 + 2)
                    tokens(expert(dve, b + 1))
                    if c is not None:
                        for j in range(6):
                            add(j, c * 6)
                        dve.wait_ge(m_sa, b * 6)
                        dve.wait_ge(m_a, b)
                        dve.wait_ge(m_at, b)
                    dve.wait_ge(m_u, b + 1)
                    v.tensor_scalar(gl[:], ps[:, B_G, :], LIMIT, None, ALU.min).then_inc(m_gl, 1)
                    dstep(v.tensor_scalar(up[:], ps[:, B_U, :], LIMIT, -LIMIT, ALU.min, ALU.max))
                    dve.wait_ge(m_gl, b + 1)
                    dstep(v.scalar_tensor_tensor(up[:], up[:], 1.0, gl[:], ALU.add, ALU.mult))
                    dve.wait_ge(m_sg, b + 1)
                    v.tensor_tensor(av_[:], up[:], sg[:], ALU.mult).then_inc(m_a, 1)

                tokens(expert(dve, 0))
                run(0, None)
                dve.wait_ge(t_yc, 6)
                with turns(dve, 0, NBLK - 1, (dstep, PER)) as c:
                    with dve.If(c < end):
                        run(c + 1, c)
                for j in range(6):
                    add(j, end * 6)

            @block.tensor
            def _(pe):
                m = nc.tensor
                end = last_block(pe)
                half = [slice(0, BLK), slice(BLK, 2 * BLK)]

                def gather():
                    for t, (_, rows) in enumerate(TILES):
                        for h in range(2):
                            last = m.matmul(ps[half[h], B_X, :], psel[0:rows, t, :], xtok[0:rows, t, CW * h:CW * h + CW],
                                            start=(t == 0), stop=(t == 2))
                    last.then_inc(m_x, 1)

                def turn(bank, src, signal):
                    for f in range(4):
                        last = m.transpose(ps[:, bank, f * P:(f + 1) * P], src[:, f * P:(f + 1) * P], ident[:])
                    last.then_inc(signal, 1)

                def scatter(n):
                    for j in range(6):
                        t, h = j // 2, j % 2
                        if j >= 3:
                            pe.wait_ge(m_sa, n + (j - 2))
                        m.matmul(ps[:, B_S + j % 3, :], gT[half[h], t * P:(t + 1) * P], ysb[half[h], :],
                                 start=True, stop=True).then_inc(m_s, 1)

                def run(b, c, odd=0, i2=-1):
                    pe.wait_ge(m_g, b * 2 + 2)
                    pe.wait_ge(m_xc, b + 1)
                    for i in range(4):
                        if i == 1 and c is not None:
                            pe.wait_ge(m_gc, b)
                            pe.wait_ge(m_yc, b)
                            scatter(c * 6)
                        if i >= 2:
                            pe.wait_ge(m_w[i], b * 16 + 16)
                        elif odd:
                            pe.wait_ge(m_wo[i], i2 * 16 + 16)
                        else:
                            pe.wait_ge(m_w[i], i2 * 16 + 32)
                        w = wodd[i] if odd and i < 2 else wq[i]
                        for k in range(2 * i, 2 * i + 2):
                            for bank, col in ((B_G, 0), (B_U, D)):
                                for h in range(2):
                                    last = m.matmul(ps[half[h], bank, :], xe[:, k % 4, k // 4, :],
                                                    w[:, k % 2, col + CW * h:col + CW * h + CW], start=(k == 0), stop=False)
                        last.then_inc(m_f, 1)
                    for bank, col in ((B_G, 0), (B_U, D)):
                        for h in range(2):
                            last = m.matmul(ps[half[h], bank, :], esel[:], bgr[:, col + CW * h:col + CW * h + CW], start=False, stop=True)
                    last.then_inc(m_u, 1)
                    pe.wait_ge(m_p, b + 2)
                    pe.wait_ge(m_xs, b + 1)
                    gather()
                    if c is not None:
                        pe.wait_ge(m_sa, b * 6)
                    for t, (t0, rows) in enumerate(TILES):
                        last = m.matmul(ps[:, B_GT, t0:t0 + rows], gsel[0:rows, t, :, :].rearrange("p h j -> p (h j)"),
                                        ident[0:rows, 0:rows], start=True, stop=True)
                    last.then_inc(m_gt, 1)
                    pe.wait_ge(m_xs, b + 2)
                    turn(B_XT, xs, m_xt)
                    pe.wait_ge(m_a, b + 1)
                    turn(B_AT, av_, m_at)
                    pe.wait_ge(m_ac, b + 1)
                    for i in range(2):
                        pe.wait_ge(m_w[4 + i], b * 16 + 16)
                        for k in range(4 * i, 4 * i + 4):
                            for h in range(2):
                                last = m.matmul(ps[half[h], B_Y, :], aT[:, k % 4, k // 4, :], wd_[i][:, k % 4, CW * h:CW * h + CW],
                                                start=(k == 0), stop=(k == KD - 1))
                        last.then_inc(m_f, 1)

                pe.wait_ge(t_bz, 2)
                pe.wait_ge(t_b, 32)
                pe.wait_ge(m_p, 1)
                gather()
                pe.wait_ge(m_xs, 1)
                turn(B_XT, xs, m_xt)
                run(0, None)
                pe.wait_ge(t_gc, 1)
                pe.wait_ge(m_gc, 1)
                pe.wait_ge(m_ac, 1)
                for j in range(6):
                    (t0, rows), n = TILES[j // 2], j % 2
                    if j >= 3:
                        pe.wait_ge(t_yc, j - 2)
                    m.matmul(ps[0:rows, B_S + j % 3, :], gmT[:, t0:t0 + rows], bdr[:, 512 * n:512 * n + 512], start=True, stop=True).then_inc(t_y, 1)
                pe.wait_ge(t_yc, 6)
                with pe.Fori(0, (NBLK - 1) // 2) as i2:
                    for odd in (1, 0):
                        c = i2 * 2 + (1 - odd)
                        with pe.If(c < end):
                            run(c + 1, c, odd, i2)
                pe.wait_ge(m_gc, end + 1)
                pe.wait_ge(m_yc, end + 1)
                scatter(end * 6)

        if stop <= 7:
            return
        dstep = Steps(S("last_dve_step"))
        with nc.Block() as block:
            @block.sync
            def _(sp):
                sp.dma_start(lnw[:], row(ln2_g[0])).then_inc(g_ln, 16)
                sp.dma_start(lnb[:], row(ln2_b[0])).then_inc(g_ln, 16)
                for t in range(2):
                    sp.wait_ge(ln_done, 4 + t)
                    sp.dma_start(y_prompt[0, P * t:P * t + P, :], xtok[:, t, :]).then_inc(s_out, 16)
                sp.wait_ge(ln_done, 6)
                sp.dma_start(y_sample.rearrange("b s d -> (b s) d"), xtok[0:32, 2, :]).then_inc(s_out, 16)
                sp.wait_ge(s_out, 48 + 16 * (NB + 1) + 48)

            @block.scalar
            def _(act):
                ln_scalar(act, 2)

            @block.vector
            def _(dve):
                v = nc.vector
                dstep.on(dve)
                v.memset(lvar[:], 1.0)
                dstep(v.memset(lst4[:], 0.0))
                for t, (_, rows) in enumerate(TILES):
                    x = xtok[0:rows, t, :]
                    dstep(v.scalar_tensor_tensor(x, x, ALPHA, yacc[0:rows, t, :], ALU.mult, ALU.add,
                                                 accum_out=lst4[0:rows, t, 0:1]))
                dve.wait_ge(g_ln, 64)
                ln_vector(dve, dstep, 2)


_INS = ["x_prompt", "x_sample", "state_hgrn", "state_ssm", "state_conv", "hg_lower_bounds", "w_in", "hg_norm_w",
        "hg_proj", "conv_w", "conv_b", "dt_bias", "a_log", "d_skip", "ssd_norm_w", "ssd_proj", "w_out", "ln1_g",
        "ln1_b", "router_w", "router_b", "w_gu", "b_gu", "w_down", "b_down", "ln2_g", "ln2_b"]
_OUTS = [(1, SEQ, D), (NB, NS, D), (1, 1, HH, P, P), (1, 1, SH, SP_, SN), (1, 1, CK - 1, XBC),
         (1, NB, HH, P, P), (1, NB, SH, SP_, SN), (1, NB, CK - 1, XBC)]


def kernel(**inputs):
    import numpy as _np
    import concourse.bacc as _bacc
    from concourse.bass_utils import run_bass_kernel_spmd as _run

    nc = _bacc.Bacc("TRN2", target_bir_lowering=False, num_devices=1)
    arrays, args = {}, []
    for name in _INS:
        a = _np.ascontiguousarray(inputs[name])
        arrays[f"in_{name}"] = a
        args.append(nc.dram_tensor(f"in_{name}", a.shape, mybir.dt.from_np(a.dtype), kind="ExternalInput").ap())
    for i, shape in enumerate(_OUTS):
        args.append(nc.dram_tensor(f"out_{i}", shape, F32, kind="ExternalOutput").ap())
    build(nc, *args)
    r = _run(nc, [arrays], core_ids=[0])
    return tuple(r.results[0][f"out_{i}"] for i in range(len(_OUTS)))
```
